# Optimizing a Trainium2 kernel written in Bass

```python
import math
import numpy as np
import jax
import jax.numpy as jnp
from jax import lax

D_MODEL = 1024
BATCH = 1
SEQ = 2048
DEPTH = 1
DEC_BATCH = 8
DEC_SEQ = 8
PAST_LEN = 1024
PAGE_SIZE = 128

MIX_WIDTH = D_MODEL
A_WIDTH = MIX_WIDTH // 2
A_HEAD_DIM = 64
A_HEADS = A_WIDTH // A_HEAD_DIM
DILATIONS = ((128, 1), (512, 4), (2048, 16))
WIN_MAX = 2048
BAND = 128
B_WIDTH = MIX_WIDTH - A_WIDTH
B_HEAD_DIM = 128
B_HEADS = B_WIDTH // B_HEAD_DIM
CONV_WIDTH = 4
CONV_CH = 3 * B_WIDTH
GDN_CHUNK = 64
IN_COLS = 3 * A_WIDTH + 4 * B_WIDTH + 2 * B_HEADS
N_MEM = 256
X_HEADS = 4
X_HEAD_DIM = D_MODEL // 8
X_WIDTH = X_HEADS * X_HEAD_DIM
N_GROUPS = 4
GROUP_EXPERTS = 8
N_EXPERTS = N_GROUPS * GROUP_EXPERTS
EXPERT_FF = D_MODEL // 2
TOP_K = 2
MOE_BLOCK = 128
EPS = 1e-6
F32 = jnp.float32

kernel_name = 'hymba_dilated_gdn_hmoe_step'

def rmsnorm(x, g):
    xf = x.astype(F32)
    y = xf * lax.rsqrt(jnp.mean(xf * xf, axis=-1, keepdims=True) + EPS)
    return (y * g.astype(F32)).astype(x.dtype)

def l2norm(x):
    return x * lax.rsqrt(jnp.sum(x * x, axis=-1, keepdims=True) + EPS)

def split_in(z):
    sizes = [A_WIDTH] * 3 + [B_WIDTH] * 4 + [B_HEADS] * 2
    return jnp.split(z, np.cumsum(sizes)[:-1].tolist(), axis=-1)

def attn_heads(qa, ka, va, g_qa, g_ka):
    shape = qa.shape[:-1] + (A_HEADS, A_HEAD_DIM)
    q = rmsnorm(qa.reshape(shape), g_qa) * (A_HEAD_DIM ** -0.5)
    k = rmsnorm(ka.reshape(shape), g_ka)
    return q, k, va.reshape(shape)

def dilated_prompt(q, k, v, window, dil):
    n, s, h, dh = q.shape
    sub_win = window // dil
    length = s // dil
    nb = -(-length // BAND)
    lp = nb * BAND

    def to_sub(t):
        t = t.reshape(n, length, dil, h, dh).transpose(0, 2, 1, 3, 4)
        t = jnp.pad(t, ((0, 0), (0, 0), (0, lp - length), (0, 0), (0, 0)))
        return t.reshape(n, dil, nb, BAND, h, dh)

    def with_prev(t):
        prev = jnp.pad(t[:, :, :-1], ((0, 0), (0, 0), (1, 0), (0, 0), (0, 0), (0, 0)))
        return jnp.concatenate([prev, t], axis=3)

    qb = to_sub(q)
    kc = with_prev(to_sub(k))
    vc = with_prev(to_sub(v))
    s_ = jnp.einsum('brnqhd,brnkhd->brnhqk', qb, kc, preferred_element_type=F32)
    qi = jnp.arange(BAND)[:, None]
    kj = jnp.arange(2 * BAND)[None, :]
    dist = qi + BAND - kj
    key_abs = jnp.arange(nb)[:, None, None] * BAND - BAND + kj[None]
    mask = (dist >= 0) & (dist <= sub_win) & (key_abs >= 0)
    s_ = jnp.where(mask[None, None, :, None], s_, -jnp.inf)
    m = jnp.max(s_, axis=-1, keepdims=True)
    p = jnp.exp(s_ - m)
    den = jnp.sum(p, axis=-1, keepdims=True)
    o = jnp.einsum('brnhqk,brnkhd->brnhqd', p, vc.astype(F32)) / den
    lse = (m + jnp.log(den))[..., 0]
    o = o.transpose(0, 1, 2, 4, 3, 5).reshape(n, dil, lp, h, dh)[:, :, :length]
    o = o.transpose(0, 2, 1, 3, 4).reshape(n, s, h, dh)
    lse = lse.transpose(0, 1, 2, 4, 3).reshape(n, dil, lp, h)[:, :, :length]
    lse = lse.transpose(0, 2, 1, 3).reshape(n, s, h)
    return o, lse

def dilated_step(q, kcat, vcat, window, dil, w_buf):
    t_new = q.shape[1]
    nk = window // dil + 1
    idx = w_buf + jnp.arange(t_new)[:, None] - dil * jnp.arange(nk)[None, :]
    valid = idx >= 0
    idx = jnp.maximum(idx, 0)
    kg = jnp.take(kcat, idx, axis=1)
    vg = jnp.take(vcat, idx, axis=1)
    s_ = jnp.einsum('bthd,btjhd->bthj', q, kg, preferred_element_type=F32)
    s_ = jnp.where(valid[None, :, None, :], s_, -jnp.inf)
    m = jnp.max(s_, axis=-1, keepdims=True)
    p = jnp.exp(s_ - m)
    den = jnp.sum(p, axis=-1, keepdims=True)
    o = jnp.einsum('bthj,btjhd->bthd', p, vg.astype(F32)) / den
    return o, (m + jnp.log(den))[..., 0]

def combine_dilations(results):
    outs = jnp.stack([r[0] for r in results])
    wts = jax.nn.softmax(jnp.stack([r[1] for r in results]), axis=0)
    return jnp.sum(wts[..., None] * outs, axis=0)

def causal_conv_silu(u, w, prev):
    full = jnp.concatenate([prev.astype(u.dtype), u], axis=1)
    n_new = u.shape[1]
    y = sum(full[:, i:i + n_new] * w[i] for i in range(CONV_WIDTH))
    return jax.nn.silu(y), full[:, n_new:]

def gdn_inputs(u, a, b_, a_log, dt_bias):
    n, length, _ = u.shape
    u = u.astype(F32).reshape(n, length, 3, B_HEADS, B_HEAD_DIM)
    q = l2norm(u[:, :, 0]) * (B_HEAD_DIM ** -0.5)
    k = l2norm(u[:, :, 1])
    v = u[:, :, 2]
    g = -jnp.exp(a_log.astype(F32)) * jax.nn.softplus(a.astype(F32) + dt_bias.astype(F32))
    beta = jax.nn.sigmoid(b_.astype(F32))
    return q, k, v, g, beta

def gdn_chunked(q, k, v, g, beta, s0):
    n, length, h, dk = q.shape
    c = GDN_CHUNK
    nc = length // c

    def chunks(t):
        t = t.reshape((n, nc, c, h) + t.shape[3:])
        return jnp.moveaxis(jnp.moveaxis(t, 1, 0), 2, 3)

    qc, kc, vc, gc, bc = (chunks(t) for t in (q, k, v, g, beta))
    gcum = jnp.cumsum(gc, axis=-1)
    diff = gcum[..., :, None] - gcum[..., None, :]
    ii = jnp.arange(c)
    strict = ii[:, None] > ii[None, :]
    incl = ii[:, None] >= ii[None, :]
    dec_strict = jnp.exp(jnp.where(strict, diff, -jnp.inf))
    dec_incl = jnp.exp(jnp.where(incl, diff, -jnp.inf))
    kk = jnp.einsum('xbhid,xbhjd->xbhij', kc, kc)
    tmat = jnp.eye(c, dtype=F32) + bc[..., :, None] * dec_strict * kk
    gamma = jnp.exp(gcum)
    w = lax.linalg.triangular_solve(tmat, (bc * gamma)[..., None] * kc, left_side=True, lower=True, unit_diagonal=True)
    uv = lax.linalg.triangular_solve(tmat, bc[..., None] * vc, left_side=True, lower=True, unit_diagonal=True)
    qk = jnp.einsum('xbhid,xbhjd->xbhij', qc, kc) * dec_incl
    tail = jnp.exp(gcum[..., -1:] - gcum)
    last = jnp.exp(gcum[..., -1])

    def step(s, xs):
        w_, uv_, q_, k_, qk_, gam_, tail_, last_ = xs
        u = uv_ - jnp.einsum('bhcd,bhde->bhce', w_, s)
        o = gam_[..., None] * jnp.einsum('bhcd,bhde->bhce', q_, s) + jnp.einsum('bhij,bhje->bhie', qk_, u)
        s = last_[..., None, None] * s + jnp.einsum('bhcd,bhce->bhde', k_ * tail_[..., None], u)
        return s, o

    s_fin, o = lax.scan(step, s0, (w, uv, qc, kc, qk, gamma, tail, last))
    o = jnp.swapaxes(jnp.moveaxis(o, 0, 1), 2, 3).reshape(n, length, h, -1)
    return o, s_fin

def gdn_recurrent(q, k, v, g, beta, s0):
    def step(s, xs):
        q_, k_, v_, g_, b_ = xs
        s = jnp.exp(g_)[..., None, None] * s
        u = b_[..., None] * (v_ - jnp.einsum('bhde,bhd->bhe', s, k_))
        s = s + jnp.einsum('bhd,bhe->bhde', k_, u)
        return s, jnp.einsum('bhde,bhd->bhe', s, q_)

    xs = tuple(jnp.moveaxis(t, 1, 0) for t in (q, k, v, g, beta))
    s_fin, o = lax.scan(step, s0, xs)
    return jnp.moveaxis(o, 0, 1), s_fin

def gdn_output(o, z, g_out):
    n, length = o.shape[:2]
    gate = jax.nn.silu(z.astype(F32)).reshape(n, length, B_HEADS, B_HEAD_DIM)
    return (rmsnorm(o, g_out) * gate).reshape(n, length, B_WIDTH).astype(z.dtype)

def mem_kv(mem, g_mem, w_xk, w_xv, g_xk):
    n, m, _ = mem.shape
    mn = rmsnorm(mem, g_mem)
    k = rmsnorm((mn @ w_xk).reshape(n, m, X_HEADS, X_HEAD_DIM), g_xk)
    v = (mn @ w_xv).reshape(n, m, X_HEADS, X_HEAD_DIM)
    return k, v

def mem_attend(hn, mem_k, mem_v, w_xq, g_xq, w_xo):
    n, length, _ = hn.shape
    q = rmsnorm((hn @ w_xq).reshape(n, length, X_HEADS, X_HEAD_DIM), g_xq)
    s = jnp.einsum('blhd,bmhd->bhlm', q, mem_k, preferred_element_type=F32) * (X_HEAD_DIM ** -0.5)
    p = jax.nn.softmax(s, axis=-1)
    o = jnp.einsum('bhlm,bmhd->blhd', p, mem_v.astype(F32))
    return o.reshape(n, length, X_WIDTH).astype(hn.dtype) @ w_xo

def route(hn, w_rg, b_rg, w_re, b_re):
    hf = hn.astype(F32)
    pg = jax.nn.softmax(hf @ w_rg.astype(F32) + b_rg.astype(F32), axis=-1)
    pg_top, g_idx = lax.top_k(pg, 1)
    le = (hf @ w_re.astype(F32) + b_re.astype(F32)).reshape(-1, N_GROUPS, GROUP_EXPERTS)
    le = jnp.take_along_axis(le, g_idx[:, :, None], axis=1)[:, 0]
    pe_top, e_idx = lax.top_k(jax.nn.softmax(le, axis=-1), TOP_K)
    wts = pg_top * pe_top / jnp.sum(pe_top, axis=-1, keepdims=True)
    return g_idx * GROUP_EXPERTS + e_idx, wts

def moe_ffn(xf, ids, wts, w_gate, w_up, w_down):
    n = xf.shape[0]
    nk = n * TOP_K
    flat_e = ids.reshape(-1)
    flat_t = jnp.repeat(jnp.arange(n, dtype=jnp.int32), TOP_K)
    flat_w = wts.reshape(-1)
    order = jnp.argsort(flat_e)
    se = flat_e[order]
    counts = jnp.bincount(flat_e, length=N_EXPERTS)
    start = jnp.cumsum(counts) - counts
    padded = (counts + MOE_BLOCK - 1) // MOE_BLOCK * MOE_BLOCK
    pend = jnp.cumsum(padded)
    dest = pend[se] - padded[se] + jnp.arange(nk) - start[se]
    n_blocks = -(-nk // MOE_BLOCK) + N_EXPERTS
    rows = n_blocks * MOE_BLOCK
    row_tok = jnp.zeros((rows,), jnp.int32).at[dest].set(flat_t[order])
    row_w = jnp.zeros((rows,), F32).at[dest].set(flat_w[order])
    blk_e = jnp.minimum(jnp.searchsorted(pend, jnp.arange(n_blocks) * MOE_BLOCK, side='right'), N_EXPERTS - 1)
    xb = xf[row_tok].reshape(n_blocks, MOE_BLOCK, -1)

    def expert_block(args):
        xblk, e = args
        return (jax.nn.silu(xblk @ w_gate[e]) * (xblk @ w_up[e])) @ w_down[e]

    yb = lax.map(expert_block, (xb, blk_e)).reshape(rows, -1).astype(F32) * row_w[:, None]
    return jnp.zeros(xf.shape, F32).at[row_tok].add(yb).astype(xf.dtype)

def channel_mixer(h, p):
    n, length, d = h.shape
    hn = rmsnorm(h, p['g_ffn']).reshape(n * length, d)
    ids, wts = route(hn, p['w_rg'], p['b_rg'], p['w_re'], p['b_re'])
    return moe_ffn(hn, ids, wts, p['w_gate'], p['w_up'], p['w_down']).reshape(n, length, d)

def layer_forward(h, win_k, win_v, conv_prev, s0, mem_k, mem_v, p):
    n, length, _ = h.shape
    qa, ka, va, qb, kb, vb, zb, ab, bb = split_in(rmsnorm(h, p['g_mix']) @ p['w_in'])
    q, k, v = attn_heads(qa, ka, va, p['g_qa'], p['g_ka'])
    if win_k is None:
        res = [dilated_prompt(q, k, v, w, d) for w, d in DILATIONS]
        keep = min(WIN_MAX, length)
        new_k, new_v = k[:, length - keep:], v[:, length - keep:]
    else:
        w_buf = win_k.shape[1]
        kcat = jnp.concatenate([win_k.astype(k.dtype), k], axis=1)
        vcat = jnp.concatenate([win_v.astype(v.dtype), v], axis=1)
        res = [dilated_step(q, kcat, vcat, w, d, w_buf) for w, d in DILATIONS]
        new_k, new_v = kcat[:, length:], vcat[:, length:]
    o_a = combine_dilations(res).reshape(n, length, A_WIDTH).astype(h.dtype)
    u, conv_new = causal_conv_silu(jnp.concatenate([qb, kb, vb], axis=-1), p['conv_w'], conv_prev)
    gq, gk, gv, gg, gbeta = gdn_inputs(u, ab, bb, p['a_log'], p['dt_bias'])
    gdn = gdn_chunked if win_k is None else gdn_recurrent
    o, s_fin = gdn(gq, gk, gv, gg, gbeta, s0)
    o_b = gdn_output(o, zb, p['g_gdn'])
    h = h + jnp.concatenate([o_a, o_b], axis=-1) @ p['w_out']
    h = h + mem_attend(rmsnorm(h, p['g_xattn']), mem_k, mem_v, p['w_xq'], p['g_xq'], p['w_xo'])
    h = h + channel_mixer(h, p)
    return h, new_k, new_v, conv_new, s_fin

def setup_inputs(seed: int = 0) -> dict:
    key = jax.random.key(seed)
    keys = iter(jax.random.split(key, 48))

    def nrm(shape, scale):
        return scale * jax.random.normal(next(keys), shape, F32)

    def gain(shape):
        return 1.0 + 0.02 * jax.random.normal(next(keys), shape, F32)

    L = DEPTH
    w_buf = min(WIN_MAX, PAST_LEN)
    a_log = jnp.log(jax.random.uniform(next(keys), (L, B_HEADS), F32, 1.0, 16.0))
    dt = jnp.exp(jax.random.uniform(next(keys), (L, B_HEADS), F32, math.log(1e-3), math.log(1e-1)))
    dt_bias = dt + jnp.log(-jnp.expm1(-dt))
    return {
        'x_prompt': nrm((BATCH, SEQ, D_MODEL), 1.0),
        'x_sample': nrm((DEC_BATCH, DEC_SEQ, D_MODEL), 1.0),
        'mem_prompt': nrm((BATCH, N_MEM, D_MODEL), 1.0),
        'cache_win_k': nrm((L, DEC_BATCH, w_buf, A_HEADS, A_HEAD_DIM), 1.0),
        'cache_win_v': nrm((L, DEC_BATCH, w_buf, A_HEADS, A_HEAD_DIM), 1.0),
        'state_conv': nrm((L, DEC_BATCH, CONV_WIDTH - 1, CONV_CH), 1.0),
        'state_delta': nrm((L, DEC_BATCH, B_HEADS, B_HEAD_DIM, B_HEAD_DIM), 0.1),
        'cache_mem_k': nrm((L, DEC_BATCH, N_MEM, X_HEADS, X_HEAD_DIM), 1.0),
        'cache_mem_v': nrm((L, DEC_BATCH, N_MEM, X_HEADS, X_HEAD_DIM), 1.0),
        'g_mix': gain((L, D_MODEL)),
        'w_in': nrm((L, D_MODEL, IN_COLS), D_MODEL ** -0.5),
        'g_qa': gain((L, A_HEAD_DIM)),
        'g_ka': gain((L, A_HEAD_DIM)),
        'conv_w': nrm((L, CONV_WIDTH, CONV_CH), 0.5),
        'a_log': a_log,
        'dt_bias': dt_bias,
        'g_gdn': gain((L, B_HEAD_DIM)),
        'w_out': nrm((L, MIX_WIDTH, D_MODEL), MIX_WIDTH ** -0.5),
        'g_xattn': gain((L, D_MODEL)),
        'g_mem': gain((L, D_MODEL)),
        'w_xq': nrm((L, D_MODEL, X_WIDTH), D_MODEL ** -0.5),
        'w_xk': nrm((L, D_MODEL, X_WIDTH), D_MODEL ** -0.5),
        'w_xv': nrm((L, D_MODEL, X_WIDTH), D_MODEL ** -0.5),
        'g_xq': gain((L, X_HEAD_DIM)),
        'g_xk': gain((L, X_HEAD_DIM)),
        'w_xo': nrm((L, X_WIDTH, D_MODEL), X_WIDTH ** -0.5),
        'g_ffn': gain((L, D_MODEL)),
        'w_rg': nrm((L, D_MODEL, N_GROUPS), D_MODEL ** -0.5),
        'b_rg': nrm((L, N_GROUPS), 0.01),
        'w_re': nrm((L, D_MODEL, N_EXPERTS), D_MODEL ** -0.5),
        'b_re': nrm((L, N_EXPERTS), 0.01),
        'w_gate': nrm((L, N_EXPERTS, D_MODEL, EXPERT_FF), D_MODEL ** -0.5),
        'w_up': nrm((L, N_EXPERTS, D_MODEL, EXPERT_FF), D_MODEL ** -0.5),
        'w_down': nrm((L, N_EXPERTS, EXPERT_FF, D_MODEL), EXPERT_FF ** -0.5),
    }

def reference(x_prompt, x_sample, mem_prompt, cache_win_k, cache_win_v, state_conv, state_delta,
              cache_mem_k, cache_mem_v, g_mix, w_in, g_qa, g_ka, conv_w, a_log, dt_bias, g_gdn, w_out,
              g_xattn, g_mem, w_xq, w_xk, w_xv, g_xq, g_xk, w_xo,
              g_ffn, w_rg, b_rg, w_re, b_re, w_gate, w_up, w_down):
    hp, hs = x_prompt, x_sample
    nb = x_prompt.shape[0]
    wkp, wvp, cvp, sdp, mkp, mvp, wks, wvs, cvs, sds = ([] for _ in range(10))
    for l in range(DEPTH):
        p = dict(g_mix=g_mix[l], w_in=w_in[l], g_qa=g_qa[l], g_ka=g_ka[l], conv_w=conv_w[l],
                 a_log=a_log[l], dt_bias=dt_bias[l], g_gdn=g_gdn[l], w_out=w_out[l],
                 g_xattn=g_xattn[l], w_xq=w_xq[l], g_xq=g_xq[l], w_xo=w_xo[l],
                 g_ffn=g_ffn[l], w_rg=w_rg[l], b_rg=b_rg[l], w_re=w_re[l], b_re=b_re[l],
                 w_gate=w_gate[l], w_up=w_up[l], w_down=w_down[l])
        mk, mv = mem_kv(mem_prompt, g_mem[l], w_xk[l], w_xv[l], g_xk[l])
        conv0 = jnp.zeros((nb, CONV_WIDTH - 1, CONV_CH), x_prompt.dtype)
        s0 = jnp.zeros((nb, B_HEADS, B_HEAD_DIM, B_HEAD_DIM), F32)
        hp, k_p, v_p, c_p, s_p = layer_forward(hp, None, None, conv0, s0, mk, mv, p)
        wkp.append(k_p)
        wvp.append(v_p)
        cvp.append(c_p)
        sdp.append(s_p)
        mkp.append(mk)
        mvp.append(mv)
        hs, k_s, v_s, c_s, s_s = layer_forward(hs, cache_win_k[l], cache_win_v[l], state_conv[l],
                                               state_delta[l].astype(F32), cache_mem_k[l], cache_mem_v[l], p)
        wks.append(k_s)
        wvs.append(v_s)
        cvs.append(c_s)
        sds.append(s_s)
    return (hp, hs,
            jnp.stack(wkp), jnp.stack(wvp), jnp.stack(cvp), jnp.stack(sdp).astype(state_delta.dtype),
            jnp.stack(mkp), jnp.stack(mvp),
            jnp.stack(wks), jnp.stack(wvs), jnp.stack(cvs), jnp.stack(sds).astype(state_delta.dtype))


_drawn_inputs = setup_inputs


def setup_inputs(seed=0):
    import zlib

    import numpy as np

    out = dict(_drawn_inputs(seed))
    spreads = {}
    factors = {'g_qa': 3.746,
     'g_ka': 2.931,
     'g_gdn': 2.939,
     'g_xattn': 5.432,
     'g_mem': 2.827,
     'g_xq': 5.289,
     'g_xk': 2.919,
     'b_rg': 43.56,
     'b_re': 12.64,
     'g_ffn': 4.497}
    for name, (base, spread) in spreads.items():
        noise = np.random.default_rng([zlib.crc32(name.encode()), seed]).standard_normal(out[name].shape)
        drawn = base * np.exp(spread * noise) if base else spread * noise
        out[name] = jnp.asarray(drawn.astype(out[name].dtype))
    for name, factor in factors.items():
        out[name] = (out[name] * factor).astype(out[name].dtype)
    return out
```

```python
from contextlib import ExitStack, contextmanager

import numpy as np
import concourse.bass as bass
from concourse import mybir

F32 = mybir.dt.float32
I32 = mybir.dt.int32
U32 = mybir.dt.uint32
BF16 = mybir.dt.bfloat16
ALU = mybir.AluOpType
ACT = mybir.ActivationFunctionType
AXX = mybir.AxisListType.X
bf16 = mybir.dt.np(BF16)

P = 128
D = 1024
KD = D // P
SEQ = 2048
DEC_B = 8
DEC_T = 8
NS = DEC_B * DEC_T
PT = SEQ // P
NT = PT + 1
ROWS = NT * P
AH, AD = 8, 64
AW = AH * AD
BH, BD = 4, 128
BW = BH * BD
CONV = 4
CCH = 3 * BW
IN_COLS = 3 * AW + 4 * BW + 2 * BH
W_BUF = 1024
XH, XD = 4, 128
XW = XH * XD
NMEM = 256
NG, GE = 4, 8
NE = NG * GE
FF = D // 2
EPS = 1e-6
NEG = -1e30
DILS = (1, 4, 16)
BLK = 128
NBLK = -(-2 * (SEQ + NS) // BLK) + NE
NBLK += NBLK % 2


class Stage:

    def __init__(self, nc, name):
        self.nc, self.name, self.stack, self.sems = nc, name, ExitStack(), []

    def __enter__(self):
        return self

    def __exit__(self, *e):
        self.stack.__exit__(*e)
        if e[0] is None:
            self.nc.clear_and_free_semaphores(self.sems)
            self.nc.all_engine_barrier()

    def sb(self, name, shape, dt=F32):
        return self.stack.enter_context(self.nc.sbuf_tensor(f"{self.name}_{name}", shape, dt))

    def ps(self, name, shape, dt=F32):
        return self.stack.enter_context(self.nc.psum_tensor(f"{self.name}_{name}", shape, dt))

    def sem(self, *names):
        out = [self.nc.alloc_semaphore(f"{self.name}_{n}") for n in names]
        self.sems += out
        return out[0] if len(out) == 1 else out


class Chain:

    def __init__(self, eng, sem, per, turn):
        self.eng, self.sem, self.base, self.per, self.n = eng, sem, turn * per, per, 0

    def mark(self, ins):
        self.n += 1
        return ins.then_inc(self.sem, 1)

    def wait(self):
        self.eng.wait_ge(self.sem, self.base + self.n)

    def then(self, ins):
        self.mark(ins)
        self.wait()

    def done(self):
        assert self.n == self.per, f"{self.n} steps a turn, not {self.per}"


def bc(ap, shape):
    return ap.unsqueeze(len(shape) - 1).to_broadcast(shape)


def project_in(nc, t):
    chunks = 8
    with Stage(nc, "inp") as s:
        w = s.sb("w", [P, KD, IN_COLS])
        ident = s.sb("ident", [P, P])
        gmix = s.sb("gmix", [P, KD])
        gq = s.sb("gq", [P, AD])
        gk = s.sb("gk", [P, AD])
        x = s.sb("x", [P, D])
        xn = s.sb("xn", [P, D])
        nT = s.sb("nT", [P, KD, P])
        st = s.sb("st", [P, 8])
        qs = s.sb("qs", [P, 2, AW])
        hs = s.sb("hs", [P, 2, 3, AH])
        out = s.sb("out", [P, IN_COLS])
        zero = s.sb("zero", [CONV - 1, CCH])
        zero_ok, zero_in, moved_on, carried = s.sem("zero_ok", "zero_in", "moved_on", "carried")
        pt = s.ps("pt", [P, 2, 512])
        po = s.ps("po", [P, 4, 512])
        (w_in, consts_in, x_in, ss_ok, mean_ok, root_ok, rstd_ok, xn_ok, xT_ok, nT_ok, proj, moved_a, moved_v,
         sq_ok, hroot_ok, hmean_ok, stored, dve_own) = s.sem(
            "w_in", "consts_in", "x_in", "ss_ok", "mean_ok", "root_ok", "rstd_ok", "xn_ok", "xT_ok",
            "nT_ok", "proj", "moved_a", "moved_v", "sq_ok", "hroot_ok", "hmean_ok", "stored", "dve_own")
        col = [0, 512, 1024, 1536, 2048, 2560, 3072, 3584, IN_COLS]
        A_MOVES, V_MOVES, STORES = (3, 5), (0, 1, 2, 4, 6, 7), 6

        def moved(eng, i, c, before=0):
            sem, order = (moved_a, A_MOVES) if c in A_MOVES else (moved_v, V_MOVES)
            eng.wait_ge(sem, i * len(order) + (1 - before) * len(order) + order.index(c) + 1)

        with nc.Block() as block:
            @block.sync
            def _(sp):
                sp.dma_start(ident[:], t["ident"]).then_inc(consts_in, 16)
                sp.dma_start(gmix[:], t["g_mix"]).then_inc(consts_in, 16)
                sp.dma_start(gq[:], t["g_qa"]).then_inc(consts_in, 16)
                sp.dma_start(gk[:], t["g_ka"]).then_inc(consts_in, 16)
                for k in range(KD):
                    sp.dma_start(w[:, k, :], t["w_in"][k * P:(k + 1) * P, :]).then_inc(w_in, 16)
                sp.wait_ge(zero_ok, 1)
                sp.dma_start(t["u"][0:CONV - 1], zero[:]).then_inc(zero_in, 16)
                sp.wait_ge(zero_in, 16)
                with sp.Fori(0, NT) as i:
                    moved(sp, i, 0)
                    sp.dma_start(t["q"][i], out[:, 0:512]).then_inc(stored, 16)
                    moved(sp, i, 1)
                    sp.dma_start(t["k"][i], out[:, 512:1024]).then_inc(stored, 16)
                    moved(sp, i, 2)
                    sp.dma_start(t["v"][i], out[:, 1024:1536]).then_inc(stored, 16)
                    moved(sp, i, 4)
                    moved(sp, i, 5)
                    sp.dma_start(t["u"][CONV - 1:].rearrange("(n p) c -> n p c", p=P)[i], out[:, 1536:3072]).then_inc(stored, 16)
                    moved(sp, i, 7)
                    sp.dma_start(t["z"][i], out[:, 3072:3584]).then_inc(stored, 16)
                    sp.dma_start(t["ab"][i], out[:, 3584:IN_COLS]).then_inc(stored, 16)
                sp.wait_ge(stored, (NT + 1) * 16 * STORES)
                kk, vv, us = (t[n].rearrange("n p c -> (n p) c")[SEQ:SEQ + NS].rearrange("(b r) c -> b r c", b=DEC_B)
                              if n != "u" else t[n][CONV - 1 + SEQ:CONV - 1 + SEQ + NS].rearrange("(b r) c -> b r c", b=DEC_B)
                              for n in ("k", "v", "u"))
                for dst, src in ((t["us"][:, 0:CONV - 1], t["conv0"]), (t["us"][:, CONV - 1:], us),
                                 (t["conv_p"], t["u"][SEQ:SEQ + CONV - 1]), (t["conv_s"], us[:, DEC_T - CONV + 1:]),
                                 (t["win_k"][:, W_BUF - DEC_T:], kk), (t["win_v"][:, W_BUF - DEC_T:], vv)):
                    sp.dma_start(dst, src).then_inc(carried, 16)
                sp.wait_ge(carried, 16 * 6)

            @block.gpsimd
            def _(pool):
                pool.memset(zero[:], 0.0).then_inc(zero_ok, 1)
                with pool.Fori(0, NT) as i:
                    pool.wait_ge(xn_ok, i + 1)
                    pool.dma_start(x[:], t["x"][i]).then_inc(x_in, 16)

            @block.scalar
            def _(act):
                act.sem_inc(xn_ok, 1)
                act.sem_inc(moved_a, len(A_MOVES))
                act.sem_inc(stored, 16 * STORES)
                act.wait_ge(w_in, KD * 16)
                for b in range(DEC_B):
                    for new, old in (("win_k", "cache_k"), ("win_v", "cache_v")):
                        act.dma_start(t[new][b, 0:W_BUF - DEC_T], t[old][b, DEC_T:]).then_inc(moved_on, 16)
                with act.Fori(0, NT) as i:
                    act.wait_ge(x_in, i * 16 + 16)
                    act.wait_ge(xT_ok, i + 1)
                    act.activation(xn[:], x[:], ACT.Square, accum_out=st[:, 0:1]).then_inc(ss_ok, 1)
                    act.wait_ge(mean_ok, i + 1)
                    act.activation(st[:, 2:3], st[:, 1:2], ACT.Sqrt).then_inc(root_ok, 1)
                    act.wait_ge(rstd_ok, i + 1)
                    act.activation(xn[:], x[:], ACT.Copy, scale=st[:, 3:4]).then_inc(xn_ok, 1)
                    for c in range(2):
                        act.wait_ge(proj, i * chunks + c + 1)
                        moved(act, i, c, before=1)
                        act.activation(qs[:, c, :], po[:, c, :], ACT.Square).then_inc(sq_ok, 1)
                        act.wait_ge(hmean_ok, i * 2 + c + 1)
                        act.activation(hs[:, c, 1, :], hs[:, c, 0, :], ACT.Sqrt).then_inc(hroot_ok, 1)
                    for c in A_MOVES:
                        act.wait_ge(proj, i * chunks + c + 1)
                        if c == A_MOVES[0]:
                            act.wait_ge(stored, i * 16 * STORES + 16 * STORES)
                        act.activation(out[:, col[c]:col[c + 1]], po[:, c % 4, :], ACT.Copy).then_inc(moved_a, 1)
                act.wait_ge(moved_on, 2 * DEC_B * 16)

            @block.vector
            def _(dve):
                dve.sem_inc(moved_v, len(V_MOVES))
                dve.wait_ge(consts_in, 64)
                with dve.Fori(0, NT) as i:
                    own = Chain(dve, dve_own, 6, i)
                    dve.wait_ge(ss_ok, i + 1)
                    dve.tensor_scalar(st[:, 1:2], st[:, 0:1], 1.0 / D, EPS, ALU.mult, ALU.add).then_inc(mean_ok, 1)
                    dve.wait_ge(root_ok, i + 1)
                    dve.reciprocal(st[:, 3:4], st[:, 2:3]).then_inc(rstd_ok, 1)
                    dve.wait_ge(xT_ok, i + 2)
                    for h in range(2):
                        dve.tensor_tensor(nT[:, 4 * h:4 * h + 4, :], pt[:, h, :].rearrange("p (k n) -> p k n", k=4),
                                          bc(gmix[:, 4 * h:4 * h + 4], [P, 4, P]), ALU.mult).then_inc(nT_ok, 1)
                    for c in range(2):
                        g = (gq, gk)[c]
                        a, b = ((1.0, AD * EPS), (1.0 / AD, EPS))[c]
                        dve.wait_ge(sq_ok, i * 2 + c + 1)
                        sq = qs[:, c, :].rearrange("p (h d) -> p h d", h=AH)
                        own.then(dve.tensor_reduce(hs[:, c, 2, :], sq, AXX, ALU.add))
                        dve.tensor_scalar(hs[:, c, 0, :], hs[:, c, 2, :], a, b, ALU.mult, ALU.add).then_inc(hmean_ok, 1)
                        dve.wait_ge(hroot_ok, i * 2 + c + 1)
                        own.then(dve.reciprocal(hs[:, c, 2, :], hs[:, c, 1, :]))
                        if c == 0:
                            dve.wait_ge(stored, i * 16 * STORES + 16 * STORES)
                        own.then(dve.tensor_tensor(sq, po[:, c, :].rearrange("p (h d) -> p h d", h=AH),
                                                   bc(hs[:, c, 2, :], [P, AH, AD]), ALU.mult))
                        dve.tensor_tensor(out[:, col[c]:col[c + 1]].rearrange("p (h d) -> p h d", h=AH), sq,
                                          g[:].unsqueeze(1).to_broadcast([P, AH, AD]), ALU.mult).then_inc(moved_v, 1)
                    own.done()
                    for c in V_MOVES[2:]:
                        dve.wait_ge(proj, i * chunks + c + 1)
                        n = col[c + 1] - col[c]
                        dve.tensor_copy(out[:, col[c]:col[c + 1]], po[:, c % 4, 0:n]).then_inc(moved_v, 1)

            @block.tensor
            def _(pe):
                pe.sem_inc(xT_ok, 1)
                pe.wait_ge(consts_in, 64)
                pe.wait_ge(w_in, KD * 16)
                with pe.Fori(0, NT) as i:
                    pe.wait_ge(xn_ok, i + 2)
                    for k in range(KD):
                        last = pe.transpose(pt[:, k // 4, (k % 4) * P:(k % 4 + 1) * P], xn[:, k * P:(k + 1) * P], ident[:])
                    last.then_inc(xT_ok, 1)
                    pe.wait_ge(nT_ok, i * 2 + 2)
                    for c in range(chunks):
                        n = col[c + 1] - col[c]
                        moved(pe, i, (c + 4) % 8, before=1 if c < 4 else 0)
                        for k in range(KD):
                            last = pe.matmul(po[:, c % 4, 0:n], nT[:, k, :], w[:, k, col[c]:col[c + 1]],
                                             start=(k == 0), stop=(k == KD - 1))
                        last.then_inc(proj, 1)


def need(eng, sem, value):
    if not isinstance(value, int) or value > 0:
        eng.wait_ge(sem, value)


def attend_prompt(nc, t):
    VA = AD + 1
    with Stage(nc, "att") as s:
        ident = s.sb("ident", [P, P])
        identb = s.sb("identb", [P, P], BF16)
        mask = s.sb("mask", [P, 2 * 2 * P], BF16)
        raw = s.sb("raw", [P, 2, 2, AW])
        qT = s.sb("qT", [P, 4, P])
        kT = s.sb("kT", [P, 4, 4, P])
        va = s.sb("va", [P, 4, AH, VA])
        prob = s.sb("prob", [P, 2, AH, 2 * P])
        pT = s.sb("pT", [P, 4, 4, P])
        res = s.sb("res", [P, 2, AH * VA + AH])
        score = s.ps("score", [P, AH, 2 * P])
        turn = s.ps("turn", [P, 2, 512])
        outp = s.ps("outp", [P, 2, 512])
        raw_in = s.sem("raw_in0", "raw_in1")
        stored = s.sem("stored0", "stored1")
        v_in = s.sem("v_in0", "v_in1", "v_in2", "v_in3")
        (consts_in, ones_ok, qk_turned, qk_moved, score_ok, max_ok, exp_ok, p_turned,
         p_moved, pv_ok, o_moved) = s.sem(
            "consts_in", "ones_ok", "qk_turned", "qk_moved", "score_ok", "max_ok",
            "exp_ok", "p_turned", "p_moved", "pv_ok", "o_moved")
        flat = {n: t[n].rearrange("n p c -> (n p) c")[0:SEQ] for n in "qkv"}

        def place(h):
            return h // 4 * 4 + h % 2 * 2 + h % 4 // 2

        def rows(ap, d, i, u):
            if d == 1:
                return ap.rearrange("(n g j) c -> n g j c", g=4, j=P)[i, u]
            if d == 4:
                return ap.rearrange("(n j r) c -> r n j c", r=4, j=P)[i, u]
            return ap.rearrange("(j s g) c -> s g j c", s=4, g=4)[i, u]

        def groups(eng, group):
            group(0, 1, 0, (False, True, True, True))
            with eng.Fori(1, 4) as i:
                group(i, 1, i, (True,) * 4)
            with eng.Fori(0, 4) as i:
                group(i + 4, 4, i, (False, True, True, True))
            with eng.Fori(0, 4) as i:
                group(i + 8, 16, i, (False,) * 4)

        def both(ahead, behind):
            def group(g, d, i, prev):
                for u in range(5):
                    if u < 4:
                        ahead(g * 4 + u, g, u, d, i, prev[u])
                    if u > 0 and behind:
                        behind(g * 4 + u - 1, g, u - 1, d, i, prev[u - 1])
            return group

        def uses(g, u):
            return g * 2 + u // 2

        with nc.Block() as block:
            @block.sync
            def _(sp):
                sp.dma_start(ident[:], t["ident"]).then_inc(consts_in, 16)
                sp.dma_start(identb[:], t["identb"]).then_inc(consts_in, 16)
                sp.dma_start(mask[:], t["att_mask"]).then_inc(consts_in, 16)

                def load(b, g, u, d, i, prev):
                    need(sp, qk_turned, 2 * b - 2)
                    for n, name in enumerate("qk"):
                        sp.dma_start(raw[:, u % 2, n, :], rows(flat[name], d, i, u)).then_inc(raw_in[u % 2], 16)
                    need(sp, pv_ok, 2 * b - 4)
                    sp.dma_start(va[:, u, :, 0:AD], rows(flat["v"], d, i, u).rearrange("p (h d) -> p h d", h=AH)).then_inc(v_in[u], 16)

                groups(sp, both(load, None))

            @block.gpsimd
            def _(pool):
                pool.memset(va[:, :, :, AD:VA], 1.0).then_inc(ones_ok, 1)

            @block.scalar
            def _(act):
                def ahead(b, g, u, d, i, prev):
                    for n, dst in ((0, qT[:]), (1, kT[:, :, u, :])):
                        act.wait_ge(qk_turned, 2 * b + n + 1)
                        act.activation(dst, turn[:, n, :].rearrange("p (c n) -> p c n", c=4),
                                       ACT.Copy).then_inc(qk_moved, 1)
                    lo = 0 if prev else P
                    for h in range(AH):
                        if h % 4 == 0:
                            act.wait_ge(max_ok, 2 * b + h // 4 + 1)
                        e = act.activation(prob[:, u % 2, h, lo:], score[:, place(h), lo:], ACT.Exp,
                                           bias=res[:, u % 2, AH * VA + h:AH * VA + h + 1])
                        if h % 4 == 3:
                            e.then_inc(exp_ok, 1)

                def behind(b, g, u, d, i, prev):
                    for h in range(2):
                        act.wait_ge(pv_ok, 2 * b + h + 1)
                        act.activation(res[:, u % 2, h * 4 * VA:(h + 1) * 4 * VA], outp[:, h, 0:4 * VA],
                                       ACT.Copy).then_inc(o_moved, 1)
                    act.wait_ge(o_moved, 2 * b + 2)
                    dst = t["att"][DILS.index(d)].rearrange("n p c -> (n p) c")[0:SEQ]
                    act.dma_start(rows(dst, d, i, u), res[:, u % 2, :]).then_inc(stored[u % 2], 16)

                groups(act, both(ahead, behind))
                for k in range(2):
                    act.wait_ge(stored[k], len(DILS) * PT // 2 * 16)

            @block.vector
            def _(dve):
                def ahead(b, g, u, d, i, prev):
                    lo = 0 if prev else P
                    for h in range(2):
                        dve.wait_ge(score_ok, 2 * b + h + 1)
                        if h == 0:
                            need(dve, stored[u % 2], uses(g, u) * 16)
                        m = res[:, u % 2, AH * VA + 4 * h:AH * VA + 4 * h + 4].rearrange("p (c a) -> p a c", a=2)
                        dve.tensor_reduce(m, score[:, 4 * h:4 * h + 4, lo:].rearrange("p (a c) k -> p a c k", a=2),
                                          AXX, ALU.max, negate=True).then_inc(max_ok, 1)

                def behind(b, g, u, d, i, prev):
                    n = 4 if prev else 2
                    for j in range(4):
                        dve.wait_ge(p_turned, 4 * b + j + 1)
                        dve.tensor_copy(pT[:, j, 0:n, :], turn[:, j % 2, 0:n * P].rearrange("p (c n) -> p c n", c=n)).then_inc(p_moved, 1)

                groups(dve, both(ahead, behind))

            @block.tensor
            def _(pe):
                pe.wait_ge(consts_in, 48)
                pe.wait_ge(ones_ok, 1)

                def ahead(b, g, u, d, i, prev):
                    pe.wait_ge(raw_in[u % 2], uses(g, u) * 32 + 32)
                    need(pe, p_moved, 4 * (b - 1) if u else 4 * b)
                    for n in range(2):
                        for c in range(4):
                            last = pe.transpose(turn[:, n, c * P:(c + 1) * P], raw[:, u % 2, n, c * P:(c + 1) * P], ident[:])
                        last.then_inc(qk_turned, 1)
                    need(pe, exp_ok, 2 * b)
                    for h in range(2):
                        for n in range(2):
                            pe.matmul(score[:, 4 * h + 2 * n:4 * h + 2 * n + 2, :], identb[:], mask[:], start=True, stop=True)
                    pe.wait_ge(qk_moved, 2 * b + 2)
                    for h in range(AH):
                        r = slice(AD * (h % 2), AD * (h % 2) + AD)
                        parts = [(P, u)]
                        if prev:
                            parts = [(0, u - 1, 2)] if u else [(0, 3), (P, 0)]
                        for part in parts:
                            w = 2 if len(part) == 3 else 1
                            last = pe.matmul(score[:, place(h), part[0]:part[0] + w * P], qT[r, h // 2, :],
                                             kT[r, h // 2, part[1]:part[1] + w, :], start=False,
                                             stop=True, skip_group_check=True)
                        if h % 4 == 3:
                            last.then_inc(score_ok, 1)

                def behind(b, g, u, d, i, prev):
                    halves = 2 if prev else 1

                    def turn_p(j):
                        if j % 2 == 0:
                            pe.wait_ge(exp_ok, 2 * b + j // 2 + 1)
                        if j >= 2:
                            pe.wait_ge(p_moved, 4 * b + j - 1)
                        for h in range(2):
                            for k in range(halves):
                                c = (2 - halves + k) * P
                                last = pe.transpose(turn[:, j % 2, (h * halves + k) * P:(h * halves + k + 1) * P],
                                                    prob[:, u % 2, 2 * j + h, c:c + P], ident[:])
                        last.then_inc(p_turned, 1)

                    def product(j):
                        pe.wait_ge(p_moved, 4 * b + j + 1)
                        if j == 0:
                            pe.wait_ge(v_in[u], g * 16 + 16)
                            need(pe, o_moved, 2 * b)
                        for h in range(2):
                            for k in range(halves):
                                slot = (u - halves + 1 + k) % 4
                                last = pe.matmul(outp[:, j // 2, (2 * (j % 2) + h) * VA:(2 * (j % 2) + h + 1) * VA],
                                                 pT[:, j, h * halves + k, :], va[:, slot, 2 * j + h, :],
                                                 start=(j % 2 == 0 and h == 0 and k == 0), stop=(k == halves - 1),
                                                 skip_group_check=True)
                        if j % 2 == 1:
                            last.then_inc(pv_ok, 1)

                    turn_p(0)
                    turn_p(1)
                    product(0)
                    turn_p(2)
                    product(1)
                    turn_p(3)
                    product(2)
                    product(3)

                groups(pe, both(ahead, behind))


G_LNB, G_CUM, G_GAM, G_BETA, G_BGAM, G_TAIL, G_LAST0, G_LAST1, G_KINDS = range(9)


def gates(nc, s, t, cst, tiles, first, chunks, sample):
    G = s.sb("G", [P, tiles, G_KINDS, BH])
    with Stage(nc, s.name + "g") as r:
        ab = r.sb("ab", [P, tiles, 2, BH])
        par = r.sb("par", [P, 2, BH])
        xx = r.sb("xx", [P, tiles, 2, BH])
        ax = r.sb("ax", [P, tiles, 2, BH])
        m = r.sb("m", [P, 2 + chunks, P])
        g = r.sb("g", [P, tiles, BH])
        na = r.sb("na", [P, BH])
        acc = r.ps("acc", [P, 4, 512])
        loaded, dv, sc, mm = r.sem("loaded", "dv", "sc", "mm")
        n = tiles * BH
        with nc.Block() as block:
            @block.sync
            def _(sp):
                sp.dma_start(ab[:].rearrange("p n a h -> p n (a h)"),
                             t["ab"][first:first + tiles].rearrange("n p c -> p n c")).then_inc(loaded, 16)
                sp.dma_start(par[:], t["gate_par"]).then_inc(loaded, 16)
                sp.dma_start(m[:], t[cst + "_sums"]).then_inc(loaded, 16)

            @block.vector
            def _(dve):
                own = Chain(dve, dv, 0, 0)
                dve.wait_ge(loaded, 48)
                own.mark(dve.tensor_tensor(xx[:, :, 0, :], ab[:, :, 0, :],
                                           par[:, 1, :].unsqueeze(1).to_broadcast([P, tiles, BH]), ALU.add))
                own.then(dve.tensor_scalar(xx[:, :, 1, :], ab[:, :, 1, :], -1.0, None, ALU.mult))
                own.then(dve.tensor_scalar(ax[:], xx[:], -1.0, None, ALU.mult))
                own.then(dve.tensor_tensor(ax[:], ax[:], xx[:], ALU.min))
                dve.wait_ge(sc, 1)
                own.then(dve.tensor_scalar(ax[:], ax[:], 1.0, None, ALU.add))
                dve.wait_ge(sc, 2)
                own.then(dve.tensor_scalar(xx[:], xx[:], 0.0, None, ALU.max))
                own.then(dve.tensor_tensor(xx[:], xx[:], ax[:], ALU.add))
                dve.wait_ge(sc, 3)
                own.then(dve.tensor_tensor(g[:], xx[:, :, 0, :], na[:].unsqueeze(1).to_broadcast([P, tiles, BH]), ALU.mult))
                own.then(dve.tensor_scalar(g[:], g[:], -1.0, None, ALU.mult))
                own.then(dve.tensor_scalar(G[:, :, G_LNB, :], xx[:, :, 1, :], -1.0, None, ALU.mult))
                dve.wait_ge(mm, 1)
                v = lambda k: acc[:, k, 0:n].rearrange("p (n h) -> p n h", h=BH)
                own.then(dve.tensor_copy(G[:, :, G_CUM, :], v(0)))
                own.then(dve.tensor_tensor(G[:, :, G_TAIL, :], v(1), G[:, :, G_CUM, :], ALU.subtract))
                own.then(dve.tensor_tensor(G[:, :, G_BGAM, :], G[:, :, G_LNB, :], G[:, :, G_CUM, :], ALU.add))
                for c in range(chunks):
                    own.then(dve.tensor_copy(G[:, :, G_LAST0 + c, :], v(2 + c)))

            @block.scalar
            def _(act):
                act.wait_ge(dv, 4)
                act.activation(ax[:], ax[:], ACT.Exp).then_inc(sc, 1)
                act.wait_ge(dv, 5)
                act.activation(ax[:], ax[:], ACT.Ln).then_inc(sc, 1)
                act.activation(na[:], par[:, 0, :], ACT.Exp).then_inc(sc, 1)
                act.wait_ge(dv, 13 + chunks)
                act.activation(G[:, :, G_GAM, :], G[:, :, G_CUM, :], ACT.Exp).then_inc(sc, 1)
                act.activation(G[:, :, G_BETA, :], G[:, :, G_LNB, :], ACT.Exp).then_inc(sc, 1)
                act.activation(G[:, :, G_BGAM, :], G[:, :, G_BGAM, :], ACT.Exp).then_inc(sc, 1)
                for k in [G_TAIL] + [G_LAST0 + c for c in range(chunks)]:
                    act.activation(G[:, :, k, :], G[:, :, k, :], ACT.Exp).then_inc(sc, 1)

            @block.tensor
            def _(pe):
                pe.wait_ge(loaded, 48)
                pe.wait_ge(dv, 9)
                for k in range(2 + chunks):
                    last = pe.matmul(acc[:, k, 0:n], m[:, k, :], g[:].rearrange("p n h -> p (n h)"), start=True, stop=True)
                last.then_inc(mm, 1)
    return G


def delta_net(nc, t, sample=False):
    cst = "gs" if sample else "gp"
    tiles = 1 if sample else PT
    first = PT if sample else 0
    levels = 3 if sample else 6
    C = P // 2
    R = slice(0, C) if sample else slice(0, P)
    n_consts = 9 if sample else 7
    with Stage(nc, cst) as s:
        G = gates(nc, s, t, cst, tiles, first, 0 if sample else 2, sample)
        ident = s.sb("ident", [P, P])
        identb = s.sb("identb", [P, P], BF16)
        ones = s.sb("ones", [P, 2, P])
        maskb = s.sb("maskb", [P, 2, BH * P], BF16)
        lvl = s.sb("lvl", [P, levels, P])
        wc = s.sb("wc", [P, CONV, CCH])
        gout = s.sb("gout", [P, BD])
        U = s.sb("U", [P, CONV, CCH])
        cv = s.sb("cv", [P, CCH])
        uu = s.sb("uu", [P, 3, BH, BD])
        z = s.sb("z", [P, BH, BD])
        sq = s.sb("sq", [P, 2 * BH, BD])
        nrm = s.sb("nrm", [P, 4, 2, BH])
        cur = s.sb("cur", [P, G_KINDS, BH])
        fac = s.sb("fac", [P, 4, BH])
        kh = s.sb("kh", [P, BH, BD])
        qh = s.sb("qh", [P, BH, BD])
        qg = s.sb("qg", [P, BH, BD])
        kb = s.sb("kb", [P, BH, BD])
        kt = s.sb("kt", [P, BH, BD])
        vb = s.sb("vb", [P, BH, BD])
        dg = s.sb("dg", [P, BH, P])
        kqT = s.sb("kqT", [P, BH, 2, P])
        qgT = s.sb("qgT", [P, BH, P])
        dec = s.sb("dec", [P, 2, BH, P])
        A = s.sb("A", [P, BH, P])
        KQ = s.sb("KQ", [P, BH, P])
        As = s.sb("As", [P, levels, BH, P])
        MN = s.sb("MN", [P, BH, 2, P])
        Y = s.sb("Y", [P, BH, P])
        WT = s.sb("WT", [P, BH, P])
        uv = s.sb("uv", [P, BH, BD])
        u = s.sb("u", [P, BH, BD])
        ob = s.sb("ob", [P, BH, BD])
        fo = s.sb("fo", [P, 4, BH])
        if sample:
            S = s.sb("S", [P, DEC_B, BH, BD])
            cm = s.sb("cm", [P, DEC_B, C])
            rm = s.sb("rm", [P, 2, DEC_B])
            WTm = s.sb("WTm", [P, BH, DEC_B, C])
            qTm = s.sb("qTm", [P, BH, DEC_B, C])
            um = s.sb("um", [P, 2, DEC_B, BD])
            gl = s.sb("gl", [P, BH, DEC_B])
            last = s.sb("last", [P, BH, DEC_B])
        else:
            S = s.sb("S", [P, BH, BD])
            Sl = s.sb("Sl", [P, BH, BD])
        pk = s.ps("pk", [P, 4, 512])
        pd = s.ps("pd", [P, 2, BH // 2, 2, P])
        pw = s.ps("pw", [P, 512])
        po = s.ps("po", [P, 512])
        E = dict(zip(*(lambda n: (n, s.sem(*n)))(
            "consts_in conv_ok u_in z_in u_silu z_silu qk_sq n2_ok n_ok cur_ok fac_ok kh_ok qh_ok qg_ok dg_ok kb_ok "
            "kt_ok vb_ok zg_ok turned_k turned_q turned_qg kT_ok qT_ok qgT_ok sums_ok dec_ok kkq_ok A_ok KQ_ok "
            "As_dve As_pool A0T_ok MN_ok Y_mm Y_ok step_mm half_ok WT_mm WT_ok uv_mm uv_ok ws_mm u_ok ds_mm Sl_ok "
            "S_ok o_mm o_sq o_n2 o_root ob_ok tile_done stored own_dve own_pool "
            "gl_ok WTm_ok qTm_ok um_ok last_mm last_ok S_in pad_ok".split())))
        halves = ((0, 2), (2, 4))
        h3 = lambda ap: ap.rearrange("p (h n) -> p h n", h=BH)

        with nc.Block() as block:
            @block.sync
            def _(sp):
                for dst, name in ((ident, "ident"), (identb, "identb"), (ones, "ones"), (maskb, cst + "_mask"),
                                  (lvl, cst + "_lvl"), (gout, "g_gdn")):
                    sp.dma_start(dst[:], t[name]).then_inc(E["consts_in"], 16)
                sp.dma_start(wc[:], t["conv_w"].partition_broadcast(P)).then_inc(E["consts_in"], 16)
                if sample:
                    sp.dma_start(cm[:], t["gs_cols"]).then_inc(E["consts_in"], 16)
                    sp.dma_start(rm[:], t["gs_rows"]).then_inc(E["consts_in"], 16)
                    for b in range(DEC_B):
                        sp.dma_start(S[:, b], t["delta0"][b].rearrange("h k v -> k h v")).then_inc(E["S_in"], 16)
                with sp.Fori(0, tiles) as i:
                    sp.wait_ge(E["conv_ok"], i + 1)
                    for k in range(CONV):
                        if sample:
                            for b in range(DEC_B):
                                sp.dma_start(U[b * DEC_T:(b + 1) * DEC_T, k, :], t["us"][b, k:k + DEC_T, :]).then_inc(E["u_in"], 16)
                        else:
                            sp.dma_start(U[:, k, :], t["u"][k:k + SEQ].rearrange("(n p) c -> n p c", p=P)[i]).then_inc(E["u_in"], 16)
                    sp.wait_ge(E["tile_done"], i + 1)
                    sp.dma_start(z[:].rearrange("p h d -> p (h d)"), t["z"][i + first]).then_inc(E["z_in"], 16)

            u_loads = 16 * CONV * (DEC_B if sample else 1)

            @block.gpsimd
            def _(pool):
                pool.sem_inc(E["tile_done"], 1)
                pool.wait_ge(E["consts_in"], n_consts * 16)
                if sample:
                    pool.memset(U[:], 0.0).then_inc(E["conv_ok"], 1)
                else:
                    pool.sem_inc(E["conv_ok"], 1)
                with pool.Fori(0, tiles) as i:
                    own = Chain(pool, E["own_pool"], 6, i)
                    pool.wait_ge(E["u_in"], i * u_loads + u_loads)
                    for k in range(CONV):
                        own.mark(pool.tensor_tensor(U[:, k, :], U[:, k, :], wc[:, k, :], ALU.mult))
                    own.wait()
                    own.mark(pool.tensor_tensor(U[:, 0, :], U[:, 0, :], U[:, 1, :], ALU.add))
                    own.then(pool.tensor_tensor(U[:, 2, :], U[:, 2, :], U[:, 3, :], ALU.add))
                    if not sample:
                        pool.wait_ge(E["tile_done"], i + 1)
                    pool.tensor_tensor(cv[:], U[:, 0, :], U[:, 2, :], ALU.add).then_inc(E["conv_ok"], 1)
                    pool.wait_ge(E["z_silu"], i + 1)
                    pool.tensor_tensor(z[:], z[:], gout[:].unsqueeze(1).to_broadcast([P, BH, BD]), ALU.mult).then_inc(E["zg_ok"], 1)
                    pool.wait_ge(E["fac_ok"], i + 1)
                    pool.tensor_tensor(vb[:], uu[:, 2], bc(cur[:, G_BETA, :], [P, BH, BD]), ALU.mult).then_inc(E["vb_ok"], 1)
                    pool.tensor_tensor(kb[:], uu[:, 1], bc(fac[:, 1, :], [P, BH, BD]), ALU.mult).then_inc(E["kb_ok"], 1)
                    pool.tensor_tensor(kt[:], uu[:, 1], bc(fac[:, 2, :], [P, BH, BD]), ALU.mult).then_inc(E["kt_ok"], 1)
                    pool.wait_ge(E["A_ok"], i + 1)
                    for q in range(levels // 2, levels):
                        pool.tensor_tensor(As[:, q], A[:], lvl[:, q].unsqueeze(1).to_broadcast([P, BH, P]), ALU.mult).then_inc(E["As_pool"], 1)
                    own.done()

            @block.scalar
            def _(act):
                with act.Fori(0, tiles) as i:
                    act.wait_ge(E["conv_ok"], i + 2)
                    act.wait_ge(E["tile_done"], i + 1)
                    act.activation(uu[:].rearrange("p a h d -> p (a h d)"), cv[:], ACT.Silu).then_inc(E["u_silu"], 1)
                    act.wait_ge(E["z_in"], i * 16 + 16)
                    act.activation(z[:], z[:], ACT.Silu).then_inc(E["z_silu"], 1)
                    act.wait_ge(E["u_silu"], i + 1)
                    act.activation(sq[:], uu[:, 0:2].rearrange("p a h d -> p (a h) d"), ACT.Square).then_inc(E["qk_sq"], 1)
                    act.wait_ge(E["n2_ok"], i + 1)
                    act.wait_ge(E["cur_ok"], i * 4 + 3)
                    act.activation(nrm[:, 2], nrm[:, 1], ACT.Sqrt).then_inc(E["n_ok"], 1)
                    for ev, out, dst, k in (("turned_k", "kT_ok", kqT[:, :, 0, :], 0), ("turned_q", "qT_ok", kqT[:, :, 1, :], 1),
                                            ("turned_qg", "qgT_ok", qgT[:], 2)):
                        act.wait_ge(E[ev], i + 1)
                        act.activation(dst, h3(pk[:, k, :]), ACT.Copy).then_inc(E[out], 1)
                    act.wait_ge(E["sums_ok"], i + 1)
                    act.wait_ge(E["cur_ok"], i * 4 + 2)
                    for k in range(2):
                        src = (pw, po)[k]
                        for h in range(BH):
                            act.activation(dec[:, k, h, :], src[:, h * P:(h + 1) * P], ACT.Exp,
                                           bias=(fac[:, 3, h:h + 1], nrm[:, 3, 0, h:h + 1])[k]).then_inc(E["dec_ok"], 1)
                    for q in range(1, levels):
                        for a, (lo, hi) in enumerate(halves):
                            act.wait_ge(E["Y_mm"], i * 2 * (levels - 1) + 2 * (q - 1) + a + 1)
                            act.activation(Y[:, lo:hi, :], pk[:, 1 + a, 0:2 * P].rearrange("p (h n) -> p h n", h=2),
                                           ACT.Copy).then_inc(E["Y_ok"], 1)
                    act.wait_ge(E["uv_mm"], i + 1)
                    act.activation(uv[:], pd[:, 1].rearrange("p a b n -> p (a b) n"), ACT.Copy).then_inc(E["uv_ok"], 1)
                    act.activation(WT[:], pd[:, 0].rearrange("p a b n -> p (a b) n"), ACT.Copy).then_inc(E["WT_ok"], 1)
                    if sample:
                        act.wait_ge(E["last_mm"], 1)
                        act.activation(last[:], pk[:, 3, 0:BH * DEC_B].rearrange("p (h b) -> p h b", b=DEC_B), ACT.Exp).then_inc(E["last_ok"], 1)
                    act.wait_ge(E["o_mm"], i + 1)
                    act.activation(sq[R, 0:BH], h3(po[R, :]), ACT.Square).then_inc(E["o_sq"], 1)
                    act.wait_ge(E["o_n2"], i + 1)
                    act.activation(fo[R, 2], fo[R, 1], ACT.Sqrt).then_inc(E["o_root"], 1)
                    act.wait_ge(E["tile_done"], i + 2)
                    act.dma_start(t["ob"][i + first], ob[:].rearrange("p h d -> p (h d)")).then_inc(E["stored"], 16)
                    act.wait_ge(E["stored"], i * 16 + 16)
                if sample:
                    for b in range(DEC_B):
                        act.dma_start(t["delta_s"][b].rearrange("h k v -> k h v"), S[:, b]).then_inc(E["stored"], 16)
                    act.wait_ge(E["stored"], 16 + 16 * DEC_B)
                else:
                    act.dma_start(t["delta_p"].rearrange("h k v -> k h v"), S[:]).then_inc(E["stored"], 16)
                    act.wait_ge(E["stored"], tiles * 16 + 16)

            @block.vector
            def _(dve):
                if sample:
                    dve.memset(ob[:], 0.0).then_inc(E["pad_ok"], 1)
                    dve.wait_ge(E["pad_ok"], 1)
                else:
                    dve.memset(S[:], 0.0).then_inc(E["S_ok"], 1)
                dve.wait_ge(E["consts_in"], n_consts * 16)
                with dve.Fori(0, tiles) as i:
                    own = Chain(dve, E["own_dve"], 5, i)
                    dve.wait_ge(E["tile_done"], i + 1)
                    kinds = G_LAST0 if sample else G_KINDS
                    own.then(dve.tensor_copy(cur[:, 0:kinds, :], G[:, 0 if sample else i, 0:kinds, :]))
                    dve.tensor_tensor(dg[:], ident[:].unsqueeze(1).to_broadcast([P, BH, P]), bc(cur[:, G_CUM, :], [P, BH, P]),
                                      ALU.mult).then_inc(E["dg_ok"], 1)
                    dve.tensor_scalar(nrm[:, 3, 0, :], cur[:, G_CUM, :], -1.0, None, ALU.mult).then_inc(E["cur_ok"], 1)
                    dve.tensor_tensor(fac[:, 3, :], cur[:, G_CUM, :], cur[:, G_LNB, :], ALU.add).then_inc(E["cur_ok"], 1)
                    dve.wait_ge(E["qk_sq"], i + 1)
                    own.then(dve.tensor_reduce(nrm[:, 0].rearrange("p a h -> p (a h)"), sq[:], AXX, ALU.add))
                    dve.tensor_scalar(nrm[:, 1, 0], nrm[:, 0, 0], float(BD), BD * EPS, ALU.mult, ALU.add).then_inc(E["cur_ok"], 1)
                    dve.tensor_scalar(nrm[:, 1, 1], nrm[:, 0, 1], EPS, None, ALU.add).then_inc(E["n2_ok"], 1)
                    dve.wait_ge(E["n_ok"], i + 1)
                    own.then(dve.reciprocal(nrm[:, 0], nrm[:, 2]))
                    dve.tensor_tensor(fac[:, 0, :], nrm[:, 0, 0], cur[:, G_GAM, :], ALU.mult).then_inc(E["cur_ok"], 1)
                    dve.tensor_tensor(fac[:, 1:3, :], cur[:, G_BGAM:G_TAIL + 1, :],
                                      nrm[:, 0, 1].unsqueeze(1).to_broadcast([P, 2, BH]), ALU.mult).then_inc(E["fac_ok"], 1)
                    dve.tensor_tensor(kh[:], uu[:, 1], bc(nrm[:, 0, 1], [P, BH, BD]), ALU.mult).then_inc(E["kh_ok"], 1)
                    dve.tensor_tensor(qh[:], uu[:, 0], bc(nrm[:, 0, 0], [P, BH, BD]), ALU.mult).then_inc(E["qh_ok"], 1)
                    dve.wait_ge(E["cur_ok"], i * 4 + 4)
                    dve.tensor_tensor(qg[:], uu[:, 0], bc(fac[:, 0, :], [P, BH, BD]), ALU.mult).then_inc(E["qg_ok"], 1)
                    dve.wait_ge(E["kkq_ok"], i + 1)
                    dve.wait_ge(E["dec_ok"], i * 2 * BH + BH)
                    kkq = pd[:].rearrange("p a b k n -> p (a b) k n")
                    dve.tensor_tensor(A[:], kkq[:, :, 0, :], dec[:, 0], ALU.mult).then_inc(E["A_ok"], 1)
                    dve.wait_ge(E["dec_ok"], i * 2 * BH + 2 * BH)
                    dve.tensor_tensor(KQ[:], kkq[:, :, 1, :], dec[:, 1], ALU.mult).then_inc(E["KQ_ok"], 1)
                    dve.wait_ge(E["A_ok"], i + 1)
                    for q in range(levels // 2):
                        dve.tensor_tensor(As[:, q], A[:], lvl[:, q].unsqueeze(1).to_broadcast([P, BH, P]), ALU.mult).then_inc(E["As_dve"], 1)
                    dve.wait_ge(E["As_dve"], i * (levels // 2) + levels // 2)
                    ib = ident[:].unsqueeze(1).to_broadcast([P, BH, P])
                    dve.tensor_tensor(MN[:, :, 1, :], ib, As[:, 0], ALU.subtract).then_inc(E["MN_ok"], 1)
                    dve.wait_ge(E["A0T_ok"], i + 1)
                    dve.tensor_tensor(MN[:, :, 0, :], ib, h3(pk[:, 0, :]), ALU.subtract).then_inc(E["MN_ok"], 1)
                    for q in range(1, levels):
                        for a, (lo, hi) in enumerate(halves):
                            if q == 1 and a == 0:
                                dve.wait_ge(E["MN_ok"], i * 2 + 2)
                            dve.wait_ge(E["step_mm"], i * 2 * (levels - 1) + 2 * (q - 1) + a + 1)
                            dve.tensor_tensor(MN[:, lo:hi], MN[:, lo:hi], pd[:, a], ALU.subtract).then_inc(E["half_ok"], 1)
                    if not sample:
                        dve.wait_ge(E["uv_ok"], i + 1)
                        for c in range(2):
                            r = slice(C * c, C * c + C)
                            dve.wait_ge(E["S_ok"], i * 2 + c + 1)
                            dve.tensor_tensor(Sl[:], S[:], bc(cur[:, G_LAST0 + c, :], [P, BH, BD]), ALU.mult).then_inc(E["Sl_ok"], 1)
                            dve.wait_ge(E["ws_mm"], i * 2 + c + 1)
                            dve.tensor_tensor(u[r], uv[r], h3(pw[r, :]), ALU.subtract).then_inc(E["u_ok"], 1)
                            dve.wait_ge(E["ds_mm"], i * 2 + c + 1)
                            dve.wait_ge(E["Sl_ok"], i * 2 + c + 1)
                            dve.tensor_tensor(S[:], Sl[:], h3(pk[:, 3, :]), ALU.add).then_inc(E["S_ok"], 1)
                    else:
                        spread = lambda ap: ap[:, :, 0:C].unsqueeze(2).to_broadcast([P, BH, DEC_B, C])
                        cmb = cm[:].unsqueeze(1).to_broadcast([P, BH, DEC_B, C])
                        dve.tensor_tensor(gl[:], bc(cur[:, G_CUM, :], [P, BH, DEC_B]),
                                          rm[:, 1].unsqueeze(1).to_broadcast([P, BH, DEC_B]), ALU.mult).then_inc(E["gl_ok"], 1)
                        dve.wait_ge(E["WT_ok"], 1)
                        dve.tensor_tensor(WTm[:], spread(WT), cmb, ALU.mult).then_inc(E["WTm_ok"], 1)
                        dve.tensor_tensor(qTm[:], spread(qgT), cmb, ALU.mult).then_inc(E["qTm_ok"], 1)
                        dve.wait_ge(E["uv_ok"], 1)
                        dve.wait_ge(E["ws_mm"], 1)
                        dve.tensor_tensor(u[R], uv[R], h3(pw[R, :]), ALU.subtract).then_inc(E["u_ok"], 1)
                        dve.wait_ge(E["o_mm"], 1)
                        dve.wait_ge(E["last_ok"], 1)
                        for b in range(DEC_B):
                            dve.tensor_tensor(S[:, b], S[:, b], bc(last[:, :, b], [P, BH, BD]), ALU.mult).then_inc(E["Sl_ok"], 1)
                        for h in range(BH):
                            if h >= 2:
                                dve.wait_ge(E["ds_mm"], h - 1)
                            dve.tensor_tensor(um[R, h % 2], u[R, h].unsqueeze(1).to_broadcast([C, DEC_B, BD]),
                                              bc(rm[R, 0], [C, DEC_B, BD]), ALU.mult).then_inc(E["um_ok"], 1)
                            dve.wait_ge(E["ds_mm"], h + 1)
                            if h == 0:
                                dve.wait_ge(E["Sl_ok"], DEC_B)
                            for a in range(2):
                                dve.tensor_tensor(S[:, 4 * a:4 * a + 4, h, :], S[:, 4 * a:4 * a + 4, h, :],
                                                  h3(pk[:, 1 + a, :]), ALU.add).then_inc(E["S_ok"], 1)
                    dve.wait_ge(E["o_sq"], i + 1)
                    own.then(dve.tensor_reduce(fo[R, 0], sq[R, 0:BH], AXX, ALU.add))
                    dve.tensor_scalar(fo[R, 1], fo[R, 0], 1.0 / BD, EPS, ALU.mult, ALU.add).then_inc(E["o_n2"], 1)
                    dve.wait_ge(E["o_root"], i + 1)
                    dve.wait_ge(E["zg_ok"], i + 1)
                    own.then(dve.reciprocal(fo[R, 3], fo[R, 2]))
                    dve.tensor_tensor(ob[R], h3(po[R, :]), bc(fo[R, 3], [R.stop, BH, BD]), ALU.mult).then_inc(E["ob_ok"], 1)
                    dve.wait_ge(E["ob_ok"], i + 1)
                    dve.tensor_tensor(ob[R], ob[R], z[R], ALU.mult).then_inc(E["tile_done"], 1)
                    own.done()

            @block.tensor
            def _(pe):
                pe.wait_ge(E["consts_in"], n_consts * 16)
                with pe.Fori(0, tiles) as i:
                    pe.wait_ge(E["dg_ok"], i + 1)
                    for k, dst in ((0, pw), (1, po)):
                        pe.matmul(dst[:, :], ones[:, k, :], dg[:].rearrange("p h n -> p (h n)"), start=True, stop=False)
                        last = pe.matmul(dst[:, :], identb[:], maskb[:, k, :], start=False, stop=True)
                    last.then_inc(E["sums_ok"], 1)
                    for ev, out, src, k in (("kh_ok", "turned_k", kh, 0), ("qh_ok", "turned_q", qh, 1), ("qg_ok", "turned_qg", qg, 2)):
                        pe.wait_ge(E[ev], i + 1)
                        for h in range(BH):
                            last = pe.transpose(pk[:, k, h * P:(h + 1) * P], src[:, h, :], ident[:])
                        last.then_inc(E[out], 1)
                    pe.wait_ge(E["kT_ok"], i + 1)
                    pe.wait_ge(E["qT_ok"], i + 1)
                    for h in range(BH):
                        last = pe.matmul(pd[:, h // 2, h % 2], kqT[:, h, 0, :], kqT[:, h], start=True, stop=True)
                    last.then_inc(E["kkq_ok"], 1)
                    pe.wait_ge(E["As_dve"], i * (levels // 2) + 1)
                    for h in range(BH):
                        last = pe.transpose(pk[:, 0, h * P:(h + 1) * P], As[:, 0, h, :], ident[:])
                    last.then_inc(E["A0T_ok"], 1)
                    pe.wait_ge(E["KQ_ok"], i + 1)
                    pe.wait_ge(E["qgT_ok"], i + 1)
                    for q in range(1, levels):
                        if q < levels // 2:
                            pe.wait_ge(E["As_dve"], i * (levels // 2) + q + 1)
                        else:
                            pe.wait_ge(E["As_pool"], i * (levels - levels // 2) + q - levels // 2 + 1)
                        for a, (lo, hi) in enumerate(halves):
                            if q == 1:
                                pe.wait_ge(E["MN_ok"], i * 2 + 2)
                            else:
                                pe.wait_ge(E["half_ok"], i * 2 * (levels - 1) + 2 * (q - 2) + a + 1)
                            for h in range(lo, hi):
                                last = pe.matmul(pk[:, 1 + a, (h - lo) * P:(h - lo + 1) * P], As[:, q, h, :], MN[:, h, 0, :], start=True, stop=True)
                            last.then_inc(E["Y_mm"], 1)
                        for a, (lo, hi) in enumerate(halves):
                            pe.wait_ge(E["Y_ok"], i * 2 * (levels - 1) + 2 * (q - 1) + a + 1)
                            for h in range(lo, hi):
                                pe.matmul(pd[:, a, h - lo, 0, :], MN[:, h, 1, :], Y[:, h, :], start=True, stop=True)
                                last = pe.matmul(pd[:, a, h - lo, 1, :], Y[:, h, :], MN[:, h, 1, :], start=True, stop=True)
                            last.then_inc(E["step_mm"], 1)
                    pe.wait_ge(E["half_ok"], i * 2 * (levels - 1) + 2 * (levels - 1))
                    pe.wait_ge(E["vb_ok"], i + 1)
                    for h in range(BH):
                        last = pe.matmul(pd[:, 1, h // 2, h % 2], MN[:, h, 0, :], vb[:, h, :], start=True, stop=True)
                    pe.wait_ge(E["kb_ok"], i + 1)
                    for h in range(BH):
                        last = pe.matmul(pd[:, 0, h // 2, h % 2], kb[:, h, :], MN[:, h, 0, :], start=True, stop=True)
                    last.then_inc(E["uv_mm"], 1)
                    pe.wait_ge(E["WT_ok"], i + 1)
                    pe.wait_ge(E["kt_ok"], i + 1)
                    if not sample:
                        for c in range(2):
                            r = slice(C * c, C * c + C)
                            pe.wait_ge(E["S_ok"], i * 2 + c + 1)
                            for h in range(BH):
                                last = pe.matmul(pw[r, h * BD:(h + 1) * BD], WT[:, h, r], S[:, h, :], start=True, stop=True)
                            last.then_inc(E["ws_mm"], 1)
                            for h in range(BH):
                                pe.matmul(po[r, h * BD:(h + 1) * BD], qgT[:, h, r], S[:, h, :], start=(h == 0), stop=False, skip_group_check=True)
                            pe.wait_ge(E["u_ok"], i * 2 + c + 1)
                            for h in range(BH):
                                last = pe.matmul(pk[:, 3, h * BD:(h + 1) * BD], kt[r, h, :], u[r, h, :], start=True, stop=True)
                            last.then_inc(E["ds_mm"], 1)
                        for h in range(BH):
                            last = pe.matmul(po[:, h * BD:(h + 1) * BD], KQ[:, h, :], u[:, h, :], start=False, stop=True, skip_group_check=True)
                        last.then_inc(E["o_mm"], 1)
                    else:
                        pe.wait_ge(E["S_in"], 16 * DEC_B)
                        pe.wait_ge(E["WTm_ok"], 1)
                        for h in range(BH):
                            for b in range(DEC_B):
                                last = pe.matmul(pw[R, h * BD:(h + 1) * BD], WTm[:, h, b, :], S[:, b, h, :],
                                                 start=(b == 0), stop=(b == DEC_B - 1))
                        last.then_inc(E["ws_mm"], 1)
                        pe.wait_ge(E["qTm_ok"], 1)
                        for h in range(BH):
                            for b in range(DEC_B):
                                pe.matmul(po[R, h * BD:(h + 1) * BD], qTm[:, h, b, :], S[:, b, h, :],
                                          start=(h == 0 and b == 0), stop=False, skip_group_check=True)
                        pe.wait_ge(E["u_ok"], 1)
                        for h in range(BH):
                            last = pe.matmul(po[R, h * BD:(h + 1) * BD], KQ[R, h, R], u[R, h, :], start=False, stop=True, skip_group_check=True)
                        last.then_inc(E["o_mm"], 1)
                        pe.wait_ge(E["gl_ok"], 1)
                        pe.matmul(pk[:, 3, 0:BH * DEC_B], ones[:, 1, :], gl[:].rearrange("p h b -> p (h b)"),
                                  start=True, stop=True).then_inc(E["last_mm"], 1)
                        for h in range(BH):
                            pe.wait_ge(E["um_ok"], h + 1)
                            if h:
                                pe.wait_ge(E["S_ok"], 2 * h)
                            for a in range(2):
                                mm = pe.matmul(pk[:, 1 + a, :], kt[R, h, :], um[R, h % 2, 4 * a:4 * a + 4, :], start=True, stop=True)
                            mm.then_inc(E["ds_mm"], 1)


def attend_sample(nc, t, mem):
    H = XH if mem else AH
    R = H * DEC_T
    full = NMEM // P if mem else 6
    new = 0 if mem else DEC_T
    NK = full * P + new
    tiles = [(j, P) for j in range(full)] + ([(full, new)] if new else [])
    T = len(tiles)
    CH = AW // P
    splits = [(0, min(NK, 512))] + ([(512, NK)] if NK > 512 else [])
    qname, oname = ("qx", "ox") if mem else ("q", "oa")
    with Stage(nc, "sm" if mem else "sw") as s:
        ident = s.sb("ident", [P, P])
        q = s.sb("q", [P, AW])
        qT = s.sb("qT", [P, CH, NS])
        qz = s.sb("qz", [P, CH, R])
        hm = s.sb("hm", [P, CH, H])
        kk = s.sb("kk", [P, T, AW])
        vv = s.sb("vv", [P, T, AW])
        kT = s.sb("kT", [P, CH, NK])
        mult = s.sb("mult", [R, NK])
        sc = s.sb("sc", [R, NK])
        pr = s.sb("pr", [R, NK])
        st = s.sb("st", [R, 4])
        pT = s.sb("pT", [P, T, R])
        om = s.sb("om", [R, AW])
        own_cols = s.sb("own_cols", [R, AW])
        sel = s.sb("sel", [R, DEC_T])
        oT = s.sb("oT", [P, CH, NS])
        o = s.sb("o", [P, AW])
        tr = s.ps("tr", [P, 2, 512])
        ps = s.ps("ps", [P, 2, 512])
        pp = s.ps("pp", [P, 512])
        pv = s.ps("pv", [P, 512])
        px = s.ps("px", [P, 512])
        names = ("consts_in q_in pad_ok qT_mm qT_ok k_in v_in qz_ok kT_mm kT_ok score_ok sc_ok max_ok exp_ok pT_mm "
                 "seen pT_ok pv_ok rden_ok on_ok om_ok sel_mm oT_ok back_mm o_ok stored").split()
        E = dict(zip(names, s.sem(*names)))
        k_loads = (2 if mem else 4) * 16

        def loads(eng, b, dst, cache, newrows, sem):
            if mem:
                for j in range(full):
                    eng.dma_start(dst[:, j, :], cache[b, j * P:(j + 1) * P, :]).then_inc(sem, 16)
            else:
                far = cache[b, 0:W_BUF // 2].rearrange("(j n r) c -> j n r c", j=2, r=16)
                for j in range(2):
                    eng.dma_start(dst[:, j, :], far[j, :, 0:DEC_T, :]).then_inc(sem, 16)
                eng.dma_start(dst[:, 2:6, :], cache[b, W_BUF // 2:].rearrange("(j p) c -> p j c", p=P)).then_inc(sem, 16)
                eng.dma_start(dst[0:new, full, :], newrows[b]).then_inc(sem, 16)

        with nc.Block() as block:
            @block.sync
            def _(sp):
                ck, cv = (t["mem_k"], t["mem_v"]) if mem else (t["cache_k"], t["cache_v"])
                nk = t["k"][PT, 0:NS].rearrange("(b r) c -> b r c", b=DEC_B)
                nv = t["v"][PT, 0:NS].rearrange("(b r) c -> b r c", b=DEC_B)
                sp.dma_start(q[:], t[qname][PT]).then_inc(E["q_in"], 16)
                sp.dma_start(ident[:], t["ident"]).then_inc(E["consts_in"], 16)
                pre = "sm_" if mem else "sw_"
                for dst, name in ((hm, "hm"), (own_cols, "own"), (sel, "sel")):
                    sp.dma_start(dst[:], t[pre + name]).then_inc(E["consts_in"], 16)
                sp.dma_start(mult[:], t[pre + "mult"]).then_inc(E["consts_in"], 16)
                with sp.Fori(0, DEC_B) as b:
                    sp.wait_ge(E["kT_mm"], b * T + 1)
                    loads(sp, b, kk, ck, nk, E["k_in"])
                    sp.wait_ge(E["pv_ok"], b + 1)
                    loads(sp, b, vv, cv, nv, E["v_in"])
                sp.wait_ge(E["o_ok"], 1)
                sp.dma_start(t[oname][PT], o[:]).then_inc(E["stored"], 16)
                sp.wait_ge(E["stored"], 16)

            @block.scalar
            def _(act):
                act.wait_ge(E["qT_mm"], 1)
                act.activation(qT[:], px[:, 0:CH * NS].rearrange("p (c n) -> p c n", c=CH), ACT.Copy).then_inc(E["qT_ok"], 1)
                with act.Fori(0, DEC_B) as b:
                    for j, n in tiles:
                        act.wait_ge(E["kT_mm"], b * T + j + 2)
                        if j == 0:
                            act.wait_ge(E["score_ok"], b + 1)
                        act.activation(kT[:, :, j * P:j * P + n], tr[:, j % 2, 0:CH * n].rearrange("p (c n) -> p c n", c=CH),
                                       ACT.Copy).then_inc(E["kT_ok"], 1)
                    act.wait_ge(E["max_ok"], b + 1)
                    act.wait_ge(E["pT_mm"], b + 1)
                    act.activation(pr[:], sc[:], ACT.Exp, bias=st[:, 0:1], accum_out=st[:, 1:2]).then_inc(E["exp_ok"], 1)
                    act.wait_ge(E["pT_mm"], b + 2)
                    act.wait_ge(E["pv_ok"], b + 1)
                    act.activation(pT[:], pp[:, 0:T * R].rearrange("p (j r) -> p j r", j=T), ACT.Copy).then_inc(E["pT_ok"], 1) \
                        if not new else None
                    if new:
                        act.activation(pT[:, 0:full], pp[:, 0:full * R].rearrange("p (j r) -> p j r", j=full), ACT.Copy).then_inc(E["pT_ok"], 1)
                        act.activation(pT[0:new, full], pp[0:new, full * R:T * R], ACT.Copy).then_inc(E["pT_ok"], 1)
                    act.wait_ge(E["rden_ok"], b + 1)
                    act.wait_ge(E["pv_ok"], b + 2)
                    act.wait_ge(E["om_ok"], b + 1)
                    act.activation(om[:], pv[0:R, :], ACT.Copy, scale=st[:, 2:3]).then_inc(E["on_ok"], 1)

            @block.vector
            def _(dve):
                dve.sem_inc(E["om_ok"], 1)
                dve.memset(o[:], 0.0).then_inc(E["pad_ok"], 1)
                dve.wait_ge(E["consts_in"], 80)
                dve.wait_ge(E["qT_ok"], 1)
                with dve.Fori(0, DEC_B) as b:
                    dve.wait_ge(E["score_ok"], b + 1)
                    dve.tensor_tensor(qz[:].rearrange("p c (h n) -> p c h n", h=H),
                                      qT[:, :, bass.ds(b * DEC_T, DEC_T)].unsqueeze(2).to_broadcast([P, CH, H, DEC_T]),
                                      hm[:].unsqueeze(3).to_broadcast([P, CH, H, DEC_T]), ALU.mult).then_inc(E["qz_ok"], 1)
                    dve.wait_ge(E["score_ok"], b + 2)
                    for k, (lo, hi) in enumerate(splits):
                        dve.tensor_tensor(sc[:, lo:hi], ps[0:R, k, 0:hi - lo], mult[:, lo:hi], ALU.add).then_inc(E["sc_ok"], 1)
                    dve.wait_ge(E["sc_ok"], (b + 1) * len(splits))
                    dve.tensor_reduce(st[:, 0:1], sc[:], AXX, ALU.max, negate=True).then_inc(E["max_ok"], 1)
                    dve.wait_ge(E["exp_ok"], b + 1)
                    dve.reciprocal(st[:, 2:3], st[:, 1:2]).then_inc(E["rden_ok"], 1)
                    dve.wait_ge(E["on_ok"], b + 1)
                    dve.tensor_tensor(om[:], om[:], own_cols[:], ALU.mult).then_inc(E["om_ok"], 1)
                    dve.wait_ge(E["sel_mm"], b + 1)
                    dve.tensor_copy(oT[:, :, bass.ds(b * DEC_T, DEC_T)],
                                    px[:, 0:CH * DEC_T].rearrange("p (c n) -> p c n", c=CH)).then_inc(E["oT_ok"], 1)
                dve.wait_ge(E["back_mm"], 1)
                dve.wait_ge(E["pad_ok"], 1)
                dve.tensor_copy(o[0:NS, :], pv[0:NS, :]).then_inc(E["o_ok"], 1)

            @block.tensor
            def _(pe):
                pe.sem_inc(E["kT_mm"], 1)
                pe.sem_inc(E["pv_ok"], 1)
                pe.sem_inc(E["score_ok"], 1)
                pe.sem_inc(E["pT_mm"], 1)
                pe.wait_ge(E["consts_in"], 80)
                pe.wait_ge(E["q_in"], 16)
                for c in range(CH):
                    last = pe.transpose(px[:, c * NS:(c + 1) * NS], q[0:NS, c * P:(c + 1) * P], ident[0:NS, 0:NS])
                last.then_inc(E["qT_mm"], 1)
                with pe.Fori(0, DEC_B) as b:
                    pe.wait_ge(E["k_in"], b * k_loads + k_loads)
                    for j, n in tiles:
                        if j >= 2:
                            pe.wait_ge(E["kT_ok"], b * T + j - 1)
                            pe.sem_inc(E["seen"], 1)
                        for c in range(CH):
                            last = pe.transpose(tr[:, j % 2, c * n:(c + 1) * n], kk[0:n, j, c * P:(c + 1) * P], ident[0:n, 0:n])
                        last.then_inc(E["kT_mm"], 1)
                    pe.wait_ge(E["kT_ok"], b * T + T)
                    pe.wait_ge(E["qz_ok"], b + 1)
                    for k, (lo, hi) in enumerate(splits):
                        for c in range(CH):
                            last = pe.matmul(ps[0:R, k, 0:hi - lo], qz[:, c, :], kT[:, c, lo:hi], start=(c == 0), stop=(c == CH - 1))
                    last.then_inc(E["score_ok"], 1)
                    pe.wait_ge(E["exp_ok"], b + 1)
                    pe.sem_inc(E["seen"], 1)
                    for j, n in tiles:
                        last = pe.transpose(pp[0:n, j * R:(j + 1) * R], pr[:, j * P:j * P + n], ident[0:R, 0:R])
                    last.then_inc(E["pT_mm"], 1)
                    pe.wait_ge(E["v_in"], b * k_loads + k_loads)
                    pe.wait_ge(E["pT_ok"], b * (2 if new else 1) + (2 if new else 1))
                    pe.wait_ge(E["om_ok"], b + 1)
                    for j, n in tiles:
                        last = pe.matmul(pv[0:R, :], pT[0:n, j, :], vv[0:n, j, :], start=(j == 0), stop=(j == T - 1))
                    last.then_inc(E["pv_ok"], 1)
                    pe.wait_ge(E["om_ok"], b + 2)
                    for c in range(CH):
                        last = pe.matmul(px[:, c * DEC_T:(c + 1) * DEC_T], om[:, c * P:(c + 1) * P], sel[:], start=True, stop=True)
                    last.then_inc(E["sel_mm"], 1)
                pe.wait_ge(E["oT_ok"], DEC_B)
                for c in range(CH):
                    last = pe.transpose(pv[0:NS, c * P:(c + 1) * P], oT[:, c, :], ident[:])
                last.then_inc(E["back_mm"], 1)


def attend_window_sample(nc, t):
    attend_sample(nc, t, mem=False)


def attend_memory_sample(nc, t):
    attend_sample(nc, t, mem=True)


def memory_kv(nc, t):
    M = NMEM // P
    with Stage(nc, "mkv") as s:
        ident = s.sb("ident", [P, P])
        w = s.sb("w", [P, 2, KD, XW])
        gm = s.sb("gm", [P, KD])
        gk = s.sb("gk", [P, XD])
        x = s.sb("x", [P, M, D])
        xn = s.sb("xn", [P, D])
        nT = s.sb("nT", [P, KD, P])
        st = s.sb("st", [P, M, 4])
        sq = s.sb("sq", [P, XH, XD])
        kst = s.sb("kst", [P, 3, XH])
        kv = s.sb("kv", [P, M, 2, XH, XD])
        tr = s.ps("tr", [P, 2, 512])
        po = s.ps("po", [P, 2, 512])
        names = ("loaded w_in ss_ok mean_ok root_ok rstd_ok xn_ok xT_ok nT_ok kv_mm sq_ok sum_ok n2_ok kroot_ok krec_ok kn_ok k_ok v_ok stored").split()
        E = dict(zip(names, s.sem(*names)))
        v3 = lambda ap: ap.rearrange("p (h d) -> p h d", h=XH)
        with nc.Block() as block:
            @block.sync
            def _(sp):
                sp.dma_start(x[:], t["mem"].rearrange("n p d -> p n d")).then_inc(E["loaded"], 16)
                sp.dma_start(ident[:], t["ident"]).then_inc(E["loaded"], 16)
                sp.dma_start(gm[:], t["g_mem"]).then_inc(E["loaded"], 16)
                sp.dma_start(gk[:], t["g_xk"]).then_inc(E["loaded"], 16)
                for n, name in enumerate(("w_xk", "w_xv")):
                    sp.dma_start(w[:, n], t[name].rearrange("(k p) c -> p k c", p=P)).then_inc(E["w_in"], 16)
                for i in range(M):
                    sp.wait_ge(E["k_ok"], i + 1)
                    sp.dma_start(t["mem_kp"][i], kv[:, i, 0].rearrange("p h d -> p (h d)")).then_inc(E["stored"], 16)
                    sp.wait_ge(E["v_ok"], i + 1)
                    sp.dma_start(t["mem_vp"][i], kv[:, i, 1].rearrange("p h d -> p (h d)")).then_inc(E["stored"], 16)
                sp.wait_ge(E["stored"], 32 * M)

            @block.scalar
            def _(act):
                act.wait_ge(E["loaded"], 64)
                for i in range(M):
                    need(act, E["xT_ok"], i)
                    act.activation(xn[:], x[:, i], ACT.Square, accum_out=st[:, i, 0:1]).then_inc(E["ss_ok"], 1)
                    act.wait_ge(E["mean_ok"], i + 1)
                    act.activation(st[:, i, 2:3], st[:, i, 1:2], ACT.Sqrt).then_inc(E["root_ok"], 1)
                    act.wait_ge(E["rstd_ok"], i + 1)
                    act.activation(xn[:], x[:, i], ACT.Copy, scale=st[:, i, 3:4]).then_inc(E["xn_ok"], 1)
                    act.wait_ge(E["kv_mm"], 2 * i + 1)
                    need(act, E["kn_ok"], i)
                    act.activation(sq[:], v3(po[:, 0, :]), ACT.Square).then_inc(E["sq_ok"], 1)
                    act.wait_ge(E["n2_ok"], i + 1)
                    act.activation(kst[:, 2], kst[:, 1], ACT.Sqrt).then_inc(E["kroot_ok"], 1)
                    act.wait_ge(E["kv_mm"], 2 * i + 2)
                    act.activation(kv[:, i, 1], v3(po[:, 1, :]), ACT.Copy).then_inc(E["v_ok"], 1)

            @block.vector
            def _(dve):
                dve.wait_ge(E["loaded"], 64)
                for i in range(M):
                    dve.wait_ge(E["ss_ok"], i + 1)
                    dve.tensor_scalar(st[:, i, 1:2], st[:, i, 0:1], 1.0 / D, EPS, ALU.mult, ALU.add).then_inc(E["mean_ok"], 1)
                    dve.wait_ge(E["root_ok"], i + 1)
                    dve.reciprocal(st[:, i, 3:4], st[:, i, 2:3]).then_inc(E["rstd_ok"], 1)
                    dve.wait_ge(E["xT_ok"], i + 1)
                    need(dve, E["kv_mm"], 2 * i)
                    for h in range(2):
                        dve.tensor_tensor(nT[:, 4 * h:4 * h + 4, :], tr[:, h, :].rearrange("p (k n) -> p k n", k=4),
                                          bc(gm[:, 4 * h:4 * h + 4], [P, 4, P]), ALU.mult).then_inc(E["nT_ok"], 1)
                    dve.wait_ge(E["sq_ok"], i + 1)
                    dve.tensor_reduce(kst[:, 0], sq[:], AXX, ALU.add).then_inc(E["sum_ok"], 1)
                    dve.wait_ge(E["sum_ok"], i + 1)
                    dve.tensor_scalar(kst[:, 1], kst[:, 0], 1.0 / XD, EPS, ALU.mult, ALU.add).then_inc(E["n2_ok"], 1)
                    dve.wait_ge(E["kroot_ok"], i + 1)
                    dve.reciprocal(kst[:, 0], kst[:, 2]).then_inc(E["krec_ok"], 1)
                    dve.wait_ge(E["krec_ok"], i + 1)
                    dve.tensor_tensor(sq[:], v3(po[:, 0, :]), bc(kst[:, 0], [P, XH, XD]), ALU.mult).then_inc(E["kn_ok"], 1)
                    dve.wait_ge(E["kn_ok"], i + 1)
                    dve.tensor_tensor(kv[:, i, 0], sq[:], gk[:].unsqueeze(1).to_broadcast([P, XH, XD]), ALU.mult).then_inc(E["k_ok"], 1)

            @block.tensor
            def _(pe):
                pe.wait_ge(E["loaded"], 64)
                for i in range(M):
                    pe.wait_ge(E["xn_ok"], i + 1)
                    need(pe, E["nT_ok"], 2 * i)
                    for k in range(KD):
                        last = pe.transpose(tr[:, k // 4, (k % 4) * P:(k % 4 + 1) * P], xn[:, k * P:(k + 1) * P], ident[:])
                    last.then_inc(E["xT_ok"], 1)
                    pe.wait_ge(E["nT_ok"], 2 * i + 2)
                    pe.wait_ge(E["w_in"], 32)
                    need(pe, E["kn_ok"], i)
                    need(pe, E["v_ok"], i)
                    for n in range(2):
                        for k in range(KD):
                            last = pe.matmul(po[:, n, :], nT[:, k, :], w[:, n, k, :], start=(k == 0), stop=(k == KD - 1))
                        last.then_inc(E["kv_mm"], 1)


def project_out(nc, t):
    VA = AD + 1
    with Stage(nc, "pout") as s:
        ident = s.sb("ident", [P, P])
        w = s.sb("w", [P, KD, D])
        wq = s.sb("wq", [P, KD, XW])
        gx = s.sb("gx", [P, KD])
        gq = s.sb("gq", [P, XD])
        att = s.sb("att", [P, len(DILS), AH * (AD + 2)])
        wa = s.sb("wa", [P, len(DILS), AH, VA])
        wt = s.sb("wt", [P, 4, AH])
        cat = s.sb("cat", [P, D])
        catT = s.sb("catT", [P, KD, P])
        x = s.sb("x", [P, D])
        h1 = s.sb("h1", [P, D])
        hn = s.sb("hn", [P, D])
        hT = s.sb("hT", [P, KD, P])
        st = s.sb("st", [P, 4])
        sq = s.sb("sq", [P, XH, XD])
        qst = s.sb("qst", [P, 3, XH])
        qx = s.sb("qx", [P, XH, XD])
        trc = s.ps("trc", [P, 2, 512])
        po = s.ps("po", [P, 2, 512])
        trh = s.ps("trh", [P, 2, 512])
        pq = s.ps("pq", [P, 512])
        names = ("consts_in w_in wq_in att_in oa_in ob_in x_in dw_ok wt_ok cat_ok catT_mm catT_ok out_mm h1_ok ss_ok mean_ok "
                 "root_ok rstd_ok hn_ok hT_mm hT_ok q_mm sq_ok n2_ok qroot_ok qx_ok h1_out qx_out own own2 own2b").split()
        E = dict(zip(names, s.sem(*names)))
        ND = len(DILS)
        v3 = lambda ap: ap.rearrange("p (h d) -> p h d", h=XH)

        def order(eng, first, second):
            first(0, False)
            with eng.Fori(1, PT) as i:
                first(i, False)
                second(i - 1)
            first(PT, True)
            second(PT - 1)
            second(PT)

        with nc.Block() as block:
            @block.sync
            def _(sp):
                for dst, name in ((ident, "ident"), (gx, "g_xattn"), (gq, "g_xq")):
                    sp.dma_start(dst[:], t[name]).then_inc(E["consts_in"], 16)

                def first(i, sample):
                    need(sp, E["cat_ok"], i)
                    if not sample:
                        sp.dma_start(att[:], t["att"][:, i].rearrange("a p c -> p a c")).then_inc(E["att_in"], 16)
                    need(sp, E["catT_mm"], i)
                    sp.dma_start(cat[:, AW:], t["ob"][i]).then_inc(E["ob_in"], 16)
                    if sample:
                        sp.dma_start(cat[:, 0:AW], t["oa"][i]).then_inc(E["oa_in"], 16)
                    need(sp, E["h1_ok"], 2 * i)
                    sp.dma_start(x[:], t["x"][i]).then_inc(E["x_in"], 16)
                    if isinstance(i, int) and i == 0:
                        sp.dma_start(w[:], t["w_out"].rearrange("(k p) c -> p k c", p=P)).then_inc(E["w_in"], 16)
                        sp.dma_start(wq[:], t["w_xq"].rearrange("(k p) c -> p k c", p=P)).then_inc(E["wq_in"], 16)

                order(sp, first, lambda i: None)

            @block.gpsimd
            def _(pool):
                def first(i, sample):
                    pool.wait_ge(E["h1_ok"], 2 * i + 2)
                    pool.dma_start(t["h1"][i], h1[:]).then_inc(E["h1_out"], 16)

                def second(i):
                    pool.wait_ge(E["qx_ok"], i + 1)
                    pool.dma_start(t["qx"][i], qx[:].rearrange("p h d -> p (h d)")).then_inc(E["qx_out"], 16)

                order(pool, first, second)
                pool.wait_ge(E["h1_out"], NT * 16)
                pool.wait_ge(E["qx_out"], NT * 16)

            @block.scalar
            def _(act):
                def first(i, sample):
                    if not sample:
                        act.wait_ge(E["dw_ok"], i + 1)
                        act.activation(wt[:, 1:], wt[:, 1:], ACT.Exp).then_inc(E["wt_ok"], 1)
                    for h in range(2):
                        act.wait_ge(E["catT_mm"], i + 1)
                        need(act, E["out_mm"], i)
                        act.activation(catT[:, 4 * h:4 * h + 4, :], trc[:, h, :].rearrange("p (k n) -> p k n", k=4),
                                       ACT.Copy).then_inc(E["catT_ok"], 1)
                    act.wait_ge(E["h1_ok"], 2 * i + 2)
                    need(act, E["hT_mm"], i)
                    act.activation(hn[:], h1[:], ACT.Square, accum_out=st[:, 0:1]).then_inc(E["ss_ok"], 1)
                    act.wait_ge(E["mean_ok"], i + 1)
                    act.activation(st[:, 2:3], st[:, 1:2], ACT.Sqrt).then_inc(E["root_ok"], 1)
                    act.wait_ge(E["rstd_ok"], i + 1)
                    act.activation(hn[:], h1[:], ACT.Copy, scale=st[:, 3:4]).then_inc(E["hn_ok"], 1)

                def second(i):
                    act.wait_ge(E["q_mm"], i + 1)
                    need(act, E["qx_ok"], i)
                    act.activation(sq[:], v3(pq[:, :]), ACT.Square).then_inc(E["sq_ok"], 1)
                    act.wait_ge(E["n2_ok"], i + 1)
                    act.activation(qst[:, 2], qst[:, 1], ACT.Sqrt).then_inc(E["qroot_ok"], 1)

                order(act, first, second)

            @block.vector
            def _(dve):
                dve.wait_ge(E["consts_in"], 48)

                def first(i, sample):
                    if sample:
                        dve.wait_ge(E["oa_in"], 16)
                        dve.sem_inc(E["cat_ok"], 1)
                    else:
                        own = Chain(dve, E["own"], 5, i)
                        nm = att[:, :, AH * VA:]
                        dve.wait_ge(E["att_in"], i * 16 + 16)
                        own.then(dve.tensor_tensor(wt[:, 0], nm[:, 0], nm[:, 1], ALU.min))
                        own.then(dve.tensor_tensor(wt[:, 0], wt[:, 0], nm[:, 2], ALU.min))
                        dve.tensor_tensor(wt[:, 1:], wt[:, 0].unsqueeze(1).to_broadcast([P, ND, AH]), nm, ALU.subtract).then_inc(E["dw_ok"], 1)
                        dve.wait_ge(E["wt_ok"], i + 1)
                        for a in range(ND):
                            dd = dve.tensor_tensor(wa[:, a], att[:, a, 0:AH * VA].rearrange("p (h d) -> p h d", h=AH),
                                                   bc(wt[:, 1 + a], [P, AH, VA]), ALU.mult)
                        own.then(dd)
                        own.then(dve.tensor_tensor(wa[:, 0], wa[:, 0], wa[:, 1], ALU.add))
                        own.then(dve.tensor_tensor(wa[:, 0], wa[:, 0], wa[:, 2], ALU.add))
                        own.done()
                        need(dve, E["catT_mm"], i)
                        dve.reciprocal(wt[:, 0], wa[:, 0, :, AD]).then_inc(E["own2"], 1)
                        dve.wait_ge(E["own2"], i + 1)
                        dve.tensor_tensor(cat[:, 0:AW].rearrange("p (h d) -> p h d", h=AH), wa[:, 0, :, 0:AD],
                                          bc(wt[:, 0], [P, AH, AD]), ALU.mult).then_inc(E["cat_ok"], 1)
                    dve.wait_ge(E["out_mm"], i + 1)
                    dve.wait_ge(E["x_in"], i * 16 + 16)
                    need(dve, E["hn_ok"], i)
                    need(dve, E["h1_out"], i * 16)
                    for h in range(2):
                        dve.tensor_tensor(h1[:, 512 * h:512 * h + 512], po[:, h, :], x[:, 512 * h:512 * h + 512], ALU.add).then_inc(E["h1_ok"], 1)
                    dve.wait_ge(E["ss_ok"], i + 1)
                    dve.tensor_scalar(st[:, 1:2], st[:, 0:1], 1.0 / D, EPS, ALU.mult, ALU.add).then_inc(E["mean_ok"], 1)
                    dve.wait_ge(E["root_ok"], i + 1)
                    dve.reciprocal(st[:, 3:4], st[:, 2:3]).then_inc(E["rstd_ok"], 1)

                def second(i):
                    for h in range(2):
                        dve.wait_ge(E["hT_mm"], i + 1)
                        dve.tensor_tensor(hT[:, 4 * h:4 * h + 4, :], trh[:, h, :].rearrange("p (k n) -> p k n", k=4),
                                          bc(gx[:, 4 * h:4 * h + 4], [P, 4, P]), ALU.mult).then_inc(E["hT_ok"], 1)
                    own = 3 * i if isinstance(i, int) else i * 3
                    dve.wait_ge(E["sq_ok"], i + 1)
                    dve.tensor_reduce(qst[:, 0], sq[:], AXX, ALU.add).then_inc(E["own2b"], 1)
                    dve.wait_ge(E["own2b"], own + 1)
                    dve.tensor_scalar(qst[:, 1], qst[:, 0], 1.0, XD * EPS, ALU.mult, ALU.add).then_inc(E["n2_ok"], 1)
                    dve.wait_ge(E["qroot_ok"], i + 1)
                    dve.reciprocal(qst[:, 0], qst[:, 2]).then_inc(E["own2b"], 1)
                    dve.wait_ge(E["own2b"], own + 2)
                    dve.tensor_tensor(sq[:], v3(pq[:, :]), bc(qst[:, 0], [P, XH, XD]), ALU.mult).then_inc(E["own2b"], 1)
                    dve.wait_ge(E["own2b"], own + 3)
                    need(dve, E["qx_out"], i * 16)
                    dve.tensor_tensor(qx[:], sq[:], gq[:].unsqueeze(1).to_broadcast([P, XH, XD]), ALU.mult).then_inc(E["qx_ok"], 1)

                order(dve, first, second)

            @block.tensor
            def _(pe):
                pe.wait_ge(E["consts_in"], 48)

                def first(i, sample):
                    pe.wait_ge(E["ob_in"], i * 16 + 16)
                    pe.wait_ge(E["cat_ok"], i + 1)
                    need(pe, E["catT_ok"], 2 * i)
                    for k in range(KD):
                        last = pe.transpose(trc[:, k // 4, (k % 4) * P:(k % 4 + 1) * P], cat[:, k * P:(k + 1) * P], ident[:])
                    last.then_inc(E["catT_mm"], 1)
                    pe.wait_ge(E["catT_ok"], 2 * i + 2)
                    if isinstance(i, int) and i == 0:
                        pe.wait_ge(E["w_in"], 16)
                        pe.wait_ge(E["wq_in"], 16)
                    need(pe, E["h1_ok"], 2 * i)
                    for n in range(2):
                        for k in range(KD):
                            last = pe.matmul(po[:, n, :], catT[:, k, :], w[:, k, 512 * n:512 * n + 512], start=(k == 0), stop=(k == KD - 1))
                    last.then_inc(E["out_mm"], 1)

                def second(i):
                    pe.wait_ge(E["hn_ok"], i + 1)
                    need(pe, E["hT_ok"], 2 * i)
                    for k in range(KD):
                        last = pe.transpose(trh[:, k // 4, (k % 4) * P:(k % 4 + 1) * P], hn[:, k * P:(k + 1) * P], ident[:])
                    last.then_inc(E["hT_mm"], 1)
                    pe.wait_ge(E["hT_ok"], 2 * i + 2)
                    need(pe, E["qx_ok"], i)
                    for k in range(KD):
                        last = pe.matmul(pq[:, :], hT[:, k, :], wq[:, k, :], start=(k == 0), stop=(k == KD - 1))
                    last.then_inc(E["q_mm"], 1)

                order(pe, first, second)


def attend_memory(nc, t):
    NL = NG + NE
    with Stage(nc, "mx") as s:
        ident = s.sb("ident", [P, P])
        wo = s.sb("wo", [P, XH, D])
        wr = s.sb("wr", [P, KD, NL])
        br = s.sb("br", [P, NL])
        gf = s.sb("gf", [P, D])
        km = s.sb("km", [P, 2, XW])
        vm = s.sb("vm", [P, 2, XW])
        kT = s.sb("kT", [P, XH, NMEM])
        q = s.sb("q", [P, XW])
        qT = s.sb("qT", [P, XH, P])
        ft = s.sb("ft", [P, 3, XH])
        pr = s.sb("pr", [P, XH, NMEM])
        pT = s.sb("pT", [P, 2, 4, P])
        ox = s.sb("ox", [P, XW])
        oxT = s.sb("oxT", [P, XH, P])
        h1 = s.sb("h1", [P, D])
        h2 = s.sb("h2", [P, D])
        h0 = s.sb("h0", [P, D])
        hn = s.sb("hn", [P, D])
        hT = s.sb("hT", [P, KD, P])
        st = s.sb("st", [P, 4])
        lg = s.sb("lg", [P, NL])
        A = s.ps("A", [P, 2, 512])
        S = s.ps("S", [P, XH, NMEM])
        V = s.ps("V", [P, 512])
        X = s.ps("X", [P, 2, 512])
        T = s.ps("T", [P, 512])
        names = ("consts_in w_in km_mm kT_ok q_in q_mm qT_ok score_ok max_ok exp_ok p_mm pT_ok pv_ok rden_ok ox_ok ox_in "
                 "ox_mm oxT_ok xo_mm h1_in h2_ok ss_ok mean_ok root_ok rstd_ok h0_ok hn_ok h_mm hT_ok lg_mm lg_ok h2_out hn_out lg_out").split()
        E = dict(zip(names, s.sem(*names)))
        v3 = lambda ap: ap.rearrange("p (h d) -> p h d", h=XH)

        def order(eng, first, second):
            first(0)
            with eng.Fori(1, PT) as i:
                first(i)
                second(i - 1)
            second(PT - 1)
            second(PT)

        with nc.Block() as block:
            @block.sync
            def _(sp):
                for dst, src in ((ident[:], t["ident"]), (km[:], t["mem_kp"].rearrange("n p c -> p n c")),
                                 (vm[:], t["mem_vp"].rearrange("n p c -> p n c")), (br[:], t["b_r"]), (gf[:], t["g_ffn"])):
                    sp.dma_start(dst, src).then_inc(E["consts_in"], 16)

                def first(i):
                    need(sp, E["q_mm"], i)
                    sp.dma_start(q[:], t["qx"][i]).then_inc(E["q_in"], 16)
                    if isinstance(i, int) and i == 0:
                        sp.dma_start(wo[:], t["w_xo"].rearrange("(k p) c -> p k c", p=P)).then_inc(E["w_in"], 16)
                        sp.dma_start(wr[:], t["w_r"].rearrange("(k p) c -> p k c", p=P)).then_inc(E["w_in"], 16)

                def second(i):
                    need(sp, E["h2_ok"], 2 * i)
                    sp.dma_start(h1[:], t["h1"][i]).then_inc(E["h1_in"], 16)

                def stores(i):
                    sp.wait_ge(E["h2_ok"], 2 * i + 2)
                    sp.dma_start(t["h2"][i], h2[:]).then_inc(E["h2_out"], 16)
                    sp.wait_ge(E["hn_ok"], i + 1)
                    sp.dma_start(t["hn"][i], hn[:]).then_inc(E["hn_out"], 16)
                    sp.wait_ge(E["lg_ok"], i + 1)
                    sp.dma_start(t["lg"][i], lg[:]).then_inc(E["lg_out"], 16)

                first(0)
                first(1)
                second(0)
                with sp.Fori(2, PT) as i:
                    first(i)
                    second(i - 1)
                    stores(i - 2)
                second(PT - 1)
                stores(PT - 2)
                sp.wait_ge(E["ox_mm"], PT)
                sp.dma_start(ox[:], t["ox"][PT]).then_inc(E["ox_in"], 16)
                second(PT)
                stores(PT - 1)
                stores(PT)
                for e in ("h2_out", "hn_out", "lg_out"):
                    sp.wait_ge(E[e], NT * 16)

            @block.gpsimd
            def _(pool):
                pool.wait_ge(E["consts_in"], 80)

                def second(i):
                    pool.wait_ge(E["h0_ok"], i + 1)
                    need(pool, E["h_mm"], 2 * i)
                    need(pool, E["hn_out"], i * 16)
                    pool.tensor_tensor(hn[:], h0[:], gf[:], ALU.mult).then_inc(E["hn_ok"], 1)

                order(pool, lambda i: None, second)

            @block.scalar
            def _(act):
                for n in range(2):
                    act.wait_ge(E["km_mm"], n + 1)
                    act.activation(kT[:, :, n * P:(n + 1) * P], v3(A[:, n, :]), ACT.Copy).then_inc(E["kT_ok"], 1)

                def first(i):
                    act.wait_ge(E["q_mm"], i + 1)
                    act.activation(qT[:], v3(A[:, 0, :]), ACT.Copy).then_inc(E["qT_ok"], 1)
                    act.wait_ge(E["max_ok"], i + 1)
                    need(act, E["p_mm"], 2 * i)
                    for h in range(XH):
                        e = act.activation(pr[:, h, :], S[:, h, :], ACT.Exp, bias=ft[:, 0, h:h + 1], accum_out=ft[:, 1, h:h + 1])
                        e.then_inc(E["exp_ok"], 1)

                def second(i):
                    act.wait_ge(E["ox_mm"], i + 1)
                    act.activation(oxT[:], v3(T[:, :]), ACT.Copy).then_inc(E["oxT_ok"], 1)
                    act.wait_ge(E["h2_ok"], 2 * i + 2)
                    need(act, E["hn_ok"], i)
                    act.activation(h0[:], h2[:], ACT.Square, accum_out=st[:, 0:1]).then_inc(E["ss_ok"], 1)
                    act.wait_ge(E["mean_ok"], i + 1)
                    act.activation(st[:, 2:3], st[:, 1:2], ACT.Sqrt).then_inc(E["root_ok"], 1)
                    act.wait_ge(E["rstd_ok"], i + 1)
                    act.activation(h0[:], h2[:], ACT.Copy, scale=st[:, 3:4]).then_inc(E["h0_ok"], 1)
                    for n in range(2):
                        act.wait_ge(E["h_mm"], 2 * i + n + 1)
                        act.activation(hT[:, 4 * n:4 * n + 4, :], v3((T[:, :], X[:, 1, :])[n]), ACT.Copy).then_inc(E["hT_ok"], 1)

                order(act, first, second)

            @block.vector
            def _(dve):
                dve.wait_ge(E["consts_in"], 80)

                def first(i):
                    dve.wait_ge(E["score_ok"], i + 1)
                    need(dve, E["ox_ok"], i)
                    dve.tensor_reduce(ft[:, 0], S[:], AXX, ALU.max, negate=True).then_inc(E["max_ok"], 1)
                    for n in range(2):
                        dve.wait_ge(E["p_mm"], 2 * i + n + 1)
                        dve.tensor_copy(pT[:, n], v3(A[:, n, :])).then_inc(E["pT_ok"], 1)
                    dve.wait_ge(E["exp_ok"], i * XH + XH)
                    dve.reciprocal(ft[:, 2], ft[:, 1]).then_inc(E["rden_ok"], 1)
                    dve.wait_ge(E["rden_ok"], i + 1)
                    dve.wait_ge(E["pv_ok"], i + 1)
                    need(dve, E["ox_mm"], i)
                    dve.tensor_tensor(v3(ox[:]), v3(V[:, :]), bc(ft[:, 2], [P, XH, XD]), ALU.mult).then_inc(E["ox_ok"], 1)

                def second(i):
                    dve.wait_ge(E["xo_mm"], i + 1)
                    dve.wait_ge(E["h1_in"], i * 16 + 16)
                    need(dve, E["h0_ok"], i)
                    need(dve, E["h2_out"], i * 16)
                    for n in range(2):
                        dve.tensor_tensor(h2[:, 512 * n:512 * n + 512], X[:, n, :], h1[:, 512 * n:512 * n + 512], ALU.add).then_inc(E["h2_ok"], 1)
                    dve.wait_ge(E["ss_ok"], i + 1)
                    dve.tensor_scalar(st[:, 1:2], st[:, 0:1], 1.0 / D, EPS, ALU.mult, ALU.add).then_inc(E["mean_ok"], 1)
                    dve.wait_ge(E["root_ok"], i + 1)
                    dve.reciprocal(st[:, 3:4], st[:, 2:3]).then_inc(E["rstd_ok"], 1)
                    dve.wait_ge(E["lg_mm"], i + 1)
                    need(dve, E["lg_out"], i * 16)
                    dve.tensor_tensor(lg[:], X[:, 0, 0:NL], br[:], ALU.add).then_inc(E["lg_ok"], 1)

                order(dve, first, second)

            @block.tensor
            def _(pe):
                pe.wait_ge(E["consts_in"], 80)
                for n in range(2):
                    for h in range(XH):
                        last = pe.transpose(A[:, n, h * P:(h + 1) * P], km[:, n, h * P:(h + 1) * P], ident[:])
                    last.then_inc(E["km_mm"], 1)
                pe.wait_ge(E["kT_ok"], 2)

                def first(i):
                    pe.wait_ge(E["q_in"], i * 16 + 16)
                    need(pe, E["pT_ok"], 2 * i)
                    for h in range(XH):
                        last = pe.transpose(A[:, 0, h * P:(h + 1) * P], q[:, h * P:(h + 1) * P], ident[:])
                    last.then_inc(E["q_mm"], 1)
                    pe.wait_ge(E["qT_ok"], i + 1)
                    need(pe, E["exp_ok"], i * XH)
                    for h in range(XH):
                        last = pe.matmul(S[:, h, :], qT[:, h, :], kT[:, h, :], start=True, stop=True)
                    last.then_inc(E["score_ok"], 1)

                def first_b(i):
                    for n in range(2):
                        pe.wait_ge(E["exp_ok"], i * XH + 2 * n + 2)
                        for m in range(4):
                            h, k = 2 * n + m // 2, m % 2
                            last = pe.transpose(A[:, n, m * P:(m + 1) * P], pr[:, h, k * P:(k + 1) * P], ident[:])
                        last.then_inc(E["p_mm"], 1)
                    need(pe, E["ox_ok"], i)
                    for n in range(2):
                        pe.wait_ge(E["pT_ok"], 2 * i + n + 1)
                        for m in range(4):
                            h, k = 2 * n + m // 2, m % 2
                            last = pe.matmul(V[:, h * P:(h + 1) * P], pT[:, n, m, :], vm[:, k, h * P:(h + 1) * P],
                                             start=(h == 0 and k == 0), stop=(k == 1), skip_group_check=True)
                    last.then_inc(E["pv_ok"], 1)

                def second(i):
                    if isinstance(i, int) and i == PT:
                        pe.wait_ge(E["ox_in"], 16)
                    else:
                        pe.wait_ge(E["ox_ok"], i + 1)
                    need(pe, E["hT_ok"], 2 * i)
                    for h in range(XH):
                        last = pe.transpose(T[:, h * P:(h + 1) * P], ox[:, h * P:(h + 1) * P], ident[:])
                    last.then_inc(E["ox_mm"], 1)
                    pe.wait_ge(E["oxT_ok"], i + 1)
                    need(pe, E["lg_ok"], i)
                    for n in range(2):
                        for h in range(XH):
                            last = pe.matmul(X[:, n, :], oxT[:, h, :], wo[:, h, 512 * n:512 * n + 512], start=(h == 0), stop=(h == XH - 1))
                    last.then_inc(E["xo_mm"], 1)

                def second_b(i):
                    pe.wait_ge(E["hn_ok"], i + 1)
                    for n in range(2):
                        for k in range(4):
                            last = pe.transpose((T[:, :], X[:, 1, :])[n][:, k * P:(k + 1) * P], hn[:, (4 * n + k) * P:(4 * n + k + 1) * P], ident[:])
                        last.then_inc(E["h_mm"], 1)
                    pe.wait_ge(E["hT_ok"], 2 * i + 2)
                    for k in range(KD):
                        last = pe.matmul(X[:, 0, 0:NL], hT[:, k, :], wr[:, k, :], start=(k == 0), stop=(k == KD - 1))
                    last.then_inc(E["lg_mm"], 1)

                first(0)
                pe.wait_ge(E["w_in"], 32)
                first_b(0)
                with pe.Fori(1, PT) as i:
                    first(i)
                    second(i - 1)
                    first_b(i)
                    second_b(i - 1)
                for i in (PT - 1, PT):
                    second(i)
                    second_b(i)


def route(nc, t):
    KB = ROWS // BLK
    with Stage(nc, "rt") as s:
        lg = s.sb("lg", [P, NT, NG + NE])
        io = s.sb("io", [P, NE])
        kb = s.sb("kb", [P, KB])
        ib = s.sb("ib", [P, NBLK])
        tri = s.sb("tri", [P, 2, P])
        tok = s.sb("tok", [P, NT], I32)
        valid = s.sb("valid", [P, NT])
        zero = s.sb("zero", [P, NBLK], I32)
        g4 = s.sb("g4", [P, 3, NT, NG])
        m = s.sb("m", [P, 8, NT])
        le = s.sb("le", [P, NT, NE])
        ca = s.sb("ca", [P, NT, NE])
        oh = s.sb("oh", [P, 2, NT, NE])
        C = s.sb("C", [P, NT, NE])
        tot = s.sb("tot", [P, NT + 1, NE])
        cmpk = s.sb("cmpk", [P, NE, KB])
        pe_ = s.sb("ends", [P, 2, 16 + NE])
        nb = s.sb("nb", [P, NE])
        cmpb = s.sb("cmpb", [P, NBLK, NE])
        be = s.sb("be", [P, NBLK])
        bei = s.sb("bei", [P, NBLK], I32)
        dst = s.sb("dst", [P, 2, NT])
        dsti = s.sb("dsti", [P, 2, NT], I32)
        wts = s.sb("wts", [P, 2, NT])
        pr = s.ps("rank", [P, 2, 512])
        pt = s.ps("total", [P, 2, 512])
        names = "loaded zero_ok zeroed own exp_ok sums_ok placed scattered saved".split()
        E = dict(zip(names, s.sem(*names)))
        CH = 16
        parts = [(0, CH), (CH, NT)]
        with nc.Block() as block:
            @block.sync
            def _(sp):
                sp.dma_start(lg[:], t["lg"].rearrange("n p c -> p n c")).then_inc(E["loaded"], 16)
                for dstt, name in ((io, "r_iota"), (kb, "r_blocks"), (ib, "r_places"), (tri, "r_tri"), (tok, "r_tok"), (valid, "r_valid")):
                    sp.dma_start(dstt[:], t[name]).then_inc(E["loaded"], 16)
                sp.wait_ge(E["zero_ok"], 1)
                sp.dma_start(t["i_rows"].rearrange("(p n) o -> p (n o)", p=P), zero[:]).then_inc(E["zeroed"], 16)
                sp.wait_ge(E["placed"], 1)
                for dd, src in ((t["i_dst"], dsti), (t["wts"], wts), (t["i_exp"], bei)):
                    sp.dma_start(dd, src[:]).then_inc(E["saved"], 16)
                sp.wait_ge(E["saved"], 48)

            @block.gpsimd
            def _(pool):
                pool.memset(zero[:], 0).then_inc(E["zero_ok"], 1)
                pool.wait_ge(E["zeroed"], 16)
                pool.wait_ge(E["placed"], 1)
                for i in range(NT):
                    n = P if i < PT else NS
                    for a in range(2):
                        pool.indirect_dma_start(t["i_rows"], bass.IndirectOffsetOnAxis(ap=dsti[0:n, a, i:i + 1].bitcast(U32), axis=0),
                                                tok[0:n, i:i + 1], None).then_inc(E["scattered"], 16)
                pool.wait_ge(E["scattered"], 16 * 2 * NT)

            @block.scalar
            def _(act):
                act.wait_ge(E["own"], 4)
                act.activation(g4[:, 1], g4[:, 0], ACT.Exp).then_inc(E["exp_ok"], 1)
                act.wait_ge(E["own"], 22)
                act.activation(m[:, 6], m[:, 5], ACT.Exp).then_inc(E["exp_ok"], 1)

            @block.tensor
            def _(pe):
                pe.wait_ge(E["loaded"], 7 * 16)
                pe.wait_ge(E["own"], 21)
                for k, (lo, hi) in enumerate(parts):
                    rhs = C[:, lo:hi, :].rearrange("p n e -> p (n e)")
                    pe.matmul(pr[:, k, 0:(hi - lo) * NE], tri[:, 0, :], rhs, start=True, stop=True)
                    last = pe.matmul(pt[:, k, 0:(hi - lo) * NE], tri[:, 1, :], rhs, start=True, stop=True)
                last.then_inc(E["sums_ok"], 1)

            @block.vector
            def _(dve):
                own = Chain(dve, E["own"], 0, 0)
                V = dve.tensor_tensor
                TS = dve.tensor_scalar
                bn = lambda ap, n: bc(ap, [P, NT, n])
                row = lambda ap, n: ap.unsqueeze(1).to_broadcast([P, NT, n])
                dve.wait_ge(E["loaded"], 7 * 16)
                own.then(dve.tensor_reduce(m[:, 0], lg[:, :, 0:NG], AXX, ALU.max))
                own.then(V(g4[:, 0], lg[:, :, 0:NG], bn(m[:, 0], NG), ALU.subtract))
                own.then(TS(g4[:, 2], g4[:, 0], 0.0, 1000.0, ALU.is_lt, ALU.mult))
                own.then(V(g4[:, 2], g4[:, 2], row(io[:, 0:NG], NG), ALU.add))
                own.then(dve.tensor_reduce(m[:, 1], g4[:, 2], AXX, ALU.min))
                own.then(V(g4[:, 2], row(io[:, 0:NG], NG), bn(m[:, 1], NG), ALU.not_equal))
                own.then(TS(g4[:, 2], g4[:, 2], NEG, None, ALU.mult))
                own.then(V(le[:].rearrange("p n (g e) -> p n g e", g=NG), lg[:, :, NG:].rearrange("p n (g e) -> p n g e", g=NG),
                           g4[:, 2].unsqueeze(3).to_broadcast([P, NT, NG, GE]), ALU.add))
                for a in range(2):
                    own.then(dve.tensor_reduce(m[:, 2 + a], le[:], AXX, ALU.max))
                    own.then(V(ca[:], le[:], bn(m[:, 2 + a], NE), ALU.is_lt))
                    own.then(dve.scalar_tensor_tensor(out=ca[:], in0=ca[:], scalar=1000.0, in1=row(io[:], NE), op0=ALU.mult, op1=ALU.add))
                    own.then(dve.tensor_reduce(m[:, 4], ca[:], AXX, ALU.min))
                    own.then(V(oh[:, a], row(io[:], NE), bn(m[:, 4], NE), ALU.is_equal))
                    if a == 0:
                        own.then(dve.scalar_tensor_tensor(out=le[:], in0=oh[:, 0], scalar=3 * NEG, in1=le[:], op0=ALU.mult, op1=ALU.add))
                own.then(V(C[:], oh[:, 0], oh[:, 1], ALU.add))
                own.then(V(C[:], C[:], bn(valid[:], NE), ALU.mult))
                own.then(V(m[:, 5], m[:, 3], m[:, 2], ALU.subtract))
                dve.wait_ge(E["exp_ok"], 2)
                own.then(dve.tensor_reduce(m[:, 0], g4[:, 1], AXX, ALU.add))
                own.then(TS(m[:, 7], m[:, 6], 1.0, None, ALU.add))
                own.then(V(m[:, 0], m[:, 0], m[:, 7], ALU.mult))
                own.then(dve.reciprocal(wts[:, 0], m[:, 0]))
                own.then(V(wts[:, 1], wts[:, 0], m[:, 6], ALU.mult))
                dve.wait_ge(E["sums_ok"], 1)
                own.then(dve.memset(tot[:, 0], 0.0))
                for i in range(NT):
                    k, j = divmod(i, CH)
                    own.then(V(tot[:, i + 1], tot[:, i], pt[:, k, j * NE:(j + 1) * NE], ALU.add))
                own.then(V(cmpk[:], bc(tot[:, NT], [P, NE, KB]), kb[:].unsqueeze(1).to_broadcast([P, NE, KB]), ALU.is_gt))
                own.then(dve.tensor_reduce(nb[:], cmpk[:], AXX, ALU.add))
                own.then(dve.memset(pe_[:], 0.0))
                own.then(dve.tensor_copy(pe_[:, 0, 16:], nb[:]))
                for k in range(5):
                    a, b, d = k % 2, 1 - k % 2, 1 << k
                    own.then(V(pe_[:, b, 16:], pe_[:, a, 16:], pe_[:, a, 16 - d:16 + NE - d], ALU.add))
                ends = pe_[:, 1, 16:]
                own.then(V(cmpb[:], ends.unsqueeze(1).to_broadcast([P, NBLK, NE]), bc(ib[:], [P, NBLK, NE]), ALU.is_le))
                own.then(dve.tensor_reduce(be[:], cmpb[:], AXX, ALU.add))
                own.then(TS(bei[:], be[:], float(NE - 1), None, ALU.min))
                own.then(V(nb[:], ends, nb[:], ALU.subtract))
                own.then(TS(nb[:], nb[:], float(BLK), None, ALU.mult))
                for k, (lo, hi) in enumerate(parts):
                    own.then(V(C[:, lo:hi], pr[:, k, 0:(hi - lo) * NE].rearrange("p (n e) -> p n e", e=NE), tot[:, lo:hi], ALU.add))
                own.then(V(C[:], C[:], row(nb[:], NE), ALU.add))
                for a in range(2):
                    own.then(V(oh[:, a], oh[:, a], C[:], ALU.mult))
                    own.then(dve.tensor_reduce(dst[:, a], oh[:, a], AXX, ALU.add))
                dve.tensor_copy(dsti[:], dst[:]).then_inc(E["placed"], 1)


def experts(nc, t):
    KF = FF // P
    with Stage(nc, "ex") as s:
        ident = s.sb("ident", [P, P])
        ei = s.sb("ei", [1, NBLK], I32)
        idx = s.sb("idx", [P, 2, 1], I32)
        xb = s.sb("xb", [P, 2, D])
        xT = s.sb("xT", [P, KD, P])
        wg = s.sb("wg", [P, 2, KD, FF])
        wu = s.sb("wu", [P, 2, KD, FF])
        wd = s.sb("wd", [P, 2, KF, D])
        sg = s.sb("sg", [P, FF])
        hh = s.sb("hh", [P, FF])
        hT = s.sb("hT", [P, KF, P])
        y = s.sb("y", [P, 2, D])
        tr = s.ps("tr", [P, 2, 512])
        gu = s.ps("gu", [P, 2, 512])
        th = s.ps("th", [P, 512])
        py = s.ps("py", [P, 2, 512])
        names = ("consts_in seen idx_in0 idx_in1 x_in0 x_in1 g_in0 g_in1 u_in0 u_in1 d_in0 d_in1 x_mm xT_ok gate_mm up_mm sg_ok hh_ok h_mm hT_ok y_mm y_ok "
                 "y_out0 y_out1").split()
        E = dict(zip(names, s.sem(*names)))
        v4 = lambda ap: ap.rearrange("p (k n) -> p k n", k=4)

        def blocks(eng, body):
            with eng.Fori(0, NBLK // 2) as i:
                for u in range(2):
                    body(i, u, 2 * i + u)

        with nc.Block() as block:
            @block.sync
            def _(sp):
                sp.dma_start(ident[:], t["ident"]).then_inc(E["consts_in"], 16)
                sp.dma_start(ei[:], t["i_exp"][0:1]).then_inc(E["consts_in"], 16)
                sp.wait_ge(E["consts_in"], 32)

                def load(i, u, b):
                    e = sp.value_load(ei[0:1, bass.ds(b, 1)], min_val=0, max_val=NE - 1)
                    sp.wait_ge(E["gate_mm"], b + 1)
                    sp.dma_start(wg[:, u], t["w_gate"][e].rearrange("(k p) c -> p k c", p=P)).then_inc(E[f"g_in{u}"], 16)
                    sp.wait_ge(E["up_mm"], b + 1)
                    sp.dma_start(wu[:, u], t["w_up"][e].rearrange("(k p) c -> p k c", p=P)).then_inc(E[f"u_in{u}"], 16)
                    sp.wait_ge(E["y_mm"], b + 1)
                    sp.dma_start(wd[:, u], t["w_down"][e].rearrange("(k p) c -> p k c", p=P)).then_inc(E[f"d_in{u}"], 16)

                blocks(sp, load)

            @block.gpsimd
            def _(pool):
                def gather(i, u, b):
                    pool.wait_ge(E["x_mm"], b + 1)
                    pool.dma_start(idx[:, u, :], t["i_rows"].rearrange("(n p) o -> n p o", p=P)[b]).then_inc(E[f"idx_in{u}"], 16)
                    pool.wait_ge(E[f"idx_in{u}"], i * 16 + 16)
                    pool.sem_inc(E["seen"], 1)
                    pool.indirect_dma_start(xb[:, u, :], None, t["hn"].rearrange("n p d -> (n p) d"),
                                            bass.IndirectOffsetOnAxis(ap=idx[:, u, :].bitcast(U32), axis=0)).then_inc(E[f"x_in{u}"], 16)

                blocks(pool, gather)

            @block.scalar
            def _(act):
                def work(i, u, b):
                    act.wait_ge(E["x_mm"], b + 3)
                    for n in range(2):
                        act.activation(xT[:, 4 * n:4 * n + 4, :], v4(tr[:, n, :]), ACT.Copy).then_inc(E["xT_ok"], 1)
                    act.wait_ge(E["gate_mm"], b + 3)
                    act.wait_ge(E["hh_ok"], b + 1)
                    act.activation(sg[:], gu[:, 0, :], ACT.Silu).then_inc(E["sg_ok"], 1)
                    act.wait_ge(E["h_mm"], b + 1)
                    act.activation(hT[:], v4(th[:, :]), ACT.Copy).then_inc(E["hT_ok"], 1)
                    act.wait_ge(E["y_ok"], 2 * b + 4)
                    act.dma_start(t["yb"][b], y[:, u, :]).then_inc(E[f"y_out{u}"], 16)

                blocks(act, work)
                for u in range(2):
                    act.wait_ge(E[f"y_out{u}"], NBLK // 2 * 16 + 16)

            @block.vector
            def _(dve):
                dve.sem_inc(E["hh_ok"], 1)
                dve.sem_inc(E["y_ok"], 2)
                dve.sem_inc(E["y_out0"], 16)
                dve.sem_inc(E["y_out1"], 16)

                def work(i, u, b):
                    dve.wait_ge(E["sg_ok"], b + 1)
                    dve.wait_ge(E["up_mm"], b + 3)
                    dve.tensor_tensor(hh[:], sg[:], gu[:, 1, :], ALU.mult).then_inc(E["hh_ok"], 1)
                    dve.wait_ge(E["y_mm"], b + 3)
                    dve.wait_ge(E[f"y_out{u}"], i * 16 + 16)
                    for n in range(2):
                        dve.tensor_copy(y[:, u, 512 * n:512 * n + 512], py[:, n, :]).then_inc(E["y_ok"], 1)

                blocks(dve, work)

            @block.tensor
            def _(pe):
                for e in ("x_mm", "gate_mm", "up_mm", "y_mm"):
                    pe.sem_inc(E[e], 2)
                pe.wait_ge(E["consts_in"], 32)

                def turn(i, u, b):
                    pe.wait_ge(E[f"x_in{u}"], i * 16 + 16)
                    for k in range(KD):
                        last = pe.transpose(tr[:, k // 4, (k % 4) * P:(k % 4 + 1) * P], xb[:, u, k * P:(k + 1) * P], ident[:])
                    last.then_inc(E["x_mm"], 1)

                def work(i, u, b):
                    turn(i, u, b)
                    pe.wait_ge(E["xT_ok"], 2 * b + 2)
                    pe.wait_ge(E[f"g_in{u}"], i * 16 + 16)
                    for k in range(KD):
                        last = pe.matmul(gu[:, 0, :], xT[:, k, :], wg[:, u, k, :], start=(k == 0), stop=(k == KD - 1))
                    last.then_inc(E["gate_mm"], 1)
                    pe.wait_ge(E[f"u_in{u}"], i * 16 + 16)
                    for k in range(KD):
                        last = pe.matmul(gu[:, 1, :], xT[:, k, :], wu[:, u, k, :], start=(k == 0), stop=(k == KD - 1))
                    last.then_inc(E["up_mm"], 1)
                    pe.wait_ge(E["hh_ok"], b + 2)
                    for k in range(KF):
                        last = pe.transpose(th[:, k * P:(k + 1) * P], hh[:, k * P:(k + 1) * P], ident[:])
                    last.then_inc(E["h_mm"], 1)
                    pe.wait_ge(E["hT_ok"], b + 1)
                    pe.wait_ge(E[f"d_in{u}"], i * 16 + 16)
                    pe.wait_ge(E["y_ok"], 2 * b + 2)
                    for n in range(2):
                        for k in range(KF):
                            last = pe.matmul(py[:, n, :], hT[:, k, :], wd[:, u, k, 512 * n:512 * n + 512], start=(k == 0), stop=(k == KF - 1))
                    last.then_inc(E["y_mm"], 1)

                blocks(pe, work)


def combine(nc, t):
    with Stage(nc, "cb") as s:
        di = s.sb("di", [P, 2, NT], I32)
        w = s.sb("w", [P, 2, NT])
        h = s.sb("h", [P, 2, D])
        a1 = s.sb("a1", [P, 2, D])
        a2 = s.sb("a2", [P, 2, D])
        s1 = s.sb("s1", [P, 2, D])
        s2 = s.sb("s2", [P, 2, D])
        consts_in, first_ok, both_ok = s.sem("consts_in", "first_ok", "both_ok")
        h_in, a_in, b_in, out_ok = (s.sem(n + "0", n + "1") for n in ("h_in", "a_in", "b_in", "out_ok"))
        rows_of = lambda i: P if i < PT else NS
        yb = t["yb"].rearrange("n p d -> (n p) d")
        with nc.Block() as block:
            def store(sp, i):
                n = rows_of(i)
                sp.wait_ge(both_ok, i + 1)
                sp.dma_start(t["y"][i, 0:n], s2[0:n, i % 2, :]).then_inc(out_ok[i % 2], 16)

            @block.sync
            def _(sp):
                sp.dma_start(di[:], t["i_dst"]).then_inc(consts_in, 16)
                sp.dma_start(w[:], t["wts"]).then_inc(consts_in, 16)
                for i in range(NT):
                    n, u = rows_of(i), i % 2
                    need(sp, first_ok, i - 1)
                    sp.dma_start(h[0:n, u, :], t["h2"][i, 0:n]).then_inc(h_in[u], 16)
                    if i:
                        store(sp, i - 1)
                store(sp, NT - 1)
                for u in range(2):
                    sp.wait_ge(out_ok[u], 16 * ((NT + 1 - u) // 2))

            @block.gpsimd
            def _(pool):
                pool.wait_ge(consts_in, 32)
                for i in range(NT):
                    n, u = rows_of(i), i % 2
                    need(pool, both_ok, i - 1)
                    for a, dst, sem in ((0, a1, a_in), (1, a2, b_in)):
                        pool.indirect_dma_start(dst[0:n, u, :], None, yb,
                                                bass.IndirectOffsetOnAxis(ap=di[0:n, a, i:i + 1].bitcast(U32), axis=0)).then_inc(sem[u], 16)

            @block.vector
            def _(dve):
                dve.wait_ge(consts_in, 32)
                for i in range(NT):
                    n, u = rows_of(i), i % 2
                    dve.wait_ge(h_in[u], 16 * (i // 2) + 16)
                    dve.wait_ge(a_in[u], 16 * (i // 2) + 16)
                    dve.scalar_tensor_tensor(out=s1[0:n, u, :], in0=a1[0:n, u, :], scalar=w[0:n, 0, i:i + 1], in1=h[0:n, u, :],
                                             op0=ALU.mult, op1=ALU.add).then_inc(first_ok, 1)
                    dve.wait_ge(first_ok, i + 1)
                    dve.wait_ge(b_in[u], 16 * (i // 2) + 16)
                    need(dve, out_ok[u], 16 * (i // 2))
                    dve.scalar_tensor_tensor(out=s2[0:n, u, :], in0=a2[0:n, u, :], scalar=w[0:n, 1, i:i + 1], in1=s1[0:n, u, :],
                                             op0=ALU.mult, op1=ALU.add).then_inc(both_ok, 1)


def build(nc, t, stages=None):
    for f in (stages or STAGES):
        f(nc, t)


def delta_net_sample(nc, t):
    delta_net(nc, t, sample=True)


STAGES = [project_in, attend_prompt, delta_net, delta_net_sample, attend_window_sample, memory_kv, project_out, attend_memory_sample, attend_memory, route, experts, combine]


def delta_consts(name, chunk, rows, levels):
    i, j = np.arange(P)[:, None], np.arange(P)[None, :]
    same = i // chunk == j // chunk
    sums = [same & (i <= j), same] + [(i // chunk == c) & (j >= 0) for c in range(2 if chunk == P // 2 else 0)]
    lvl = [((i >> q + 1) == (j >> q + 1)) & ((i >> q & 1) == 1) & ((j >> q & 1) == 0) for q in range(levels)]
    low = np.where(same & (j <= i), 0, NEG)
    return {
        name + "_sums": np.ascontiguousarray(np.stack(sums, 1).astype(np.float32)),
        name + "_lvl": np.ascontiguousarray(np.stack(lvl, 1).astype(np.float32)),
        name + "_mask": np.ascontiguousarray(np.stack([np.tile(low, (1, BH)), np.tile(low.T, (1, BH))], 1).astype(bf16)),
    }


def window_counts():
    far = [r for r in range(W_BUF // 2) if r % 16 < DEC_T]
    pos = np.array(far + list(range(W_BUF // 2, W_BUF + DEC_T)))
    back = W_BUF + np.arange(DEC_T)[:, None] - pos[None]
    return sum(((back >= 0) & (back % d == 0) & (back <= BLK * d)).astype(int) for d in DILS)


def sample_consts(name, heads, counts):
    f32 = np.float32
    feat = np.arange(AW)
    row = np.arange(heads * DEC_T)
    own = feat[None] // (AW // heads) == row[:, None] // DEC_T
    logs = np.where(counts > 0, np.log(np.maximum(counts, 1)), NEG)
    return {
        name + "hm": np.ascontiguousarray((feat[:, None] // (AW // heads) == np.arange(heads)[None]).astype(f32)
                                          .reshape(AW // P, P, heads).transpose(1, 0, 2)),
        name + "own": own.astype(f32),
        name + "sel": (row[:, None] % DEC_T == np.arange(DEC_T)[None]).astype(f32),
        name + "mult": np.tile(logs, (heads, 1)).astype(f32),
    }


def layout(a):
    f = lambda n: np.ascontiguousarray(np.asarray(a[n]))
    cols = lambda n: np.ascontiguousarray(f(n).reshape(KD, P).T)
    rep = lambda v: np.ascontiguousarray(np.broadcast_to(v, (P,) + v.shape))
    i, j = np.arange(P)[:, None], np.arange(P)[None, :]
    x = np.zeros((ROWS, D), np.float32)
    x[:SEQ] = f("x_prompt").reshape(SEQ, D)
    x[SEQ:SEQ + NS] = f("x_sample").reshape(NS, D)
    return {
        "x": x.reshape(NT, P, D),
        "ident": np.eye(P, dtype=np.float32),
        "identb": np.eye(P).astype(bf16),
        "att_mask": np.tile(np.concatenate([np.where(j >= i, 0, NEG), np.where(j <= i, 0, NEG)], 1), (1, 2)).astype(bf16),
        **delta_consts("gp", P // 2, P, 6), **delta_consts("gs", DEC_T, NS, 3),
        "ones": rep(np.ones((2, P), np.float32) * np.array([[-1.0], [1.0]], np.float32)),
        "gate_par": rep(np.stack([f("a_log").reshape(BH), f("dt_bias").reshape(BH)])),
        "conv_w": f("conv_w").reshape(CONV, CCH),
        **sample_consts("sw_", AH, window_counts()), **sample_consts("sm_", XH, np.ones((DEC_T, NMEM))),
        "mem_k": f("cache_mem_k").reshape(DEC_B, NMEM, XW),
        "mem_v": f("cache_mem_v").reshape(DEC_B, NMEM, XW),
        "mem": f("mem_prompt").reshape(NMEM // P, P, D),
        "g_mem": cols("g_mem"), "g_xattn": cols("g_xattn"),
        "g_xk": rep(f("g_xk").reshape(XD)), "g_xq": rep(f("g_xq").reshape(XD)),
        "w_xk": f("w_xk").reshape(D, XW), "w_xv": f("w_xv").reshape(D, XW),
        "w_xq": f("w_xq").reshape(D, XW), "w_out": f("w_out").reshape(D, D),
        "w_xo": f("w_xo").reshape(XW, D), "g_ffn": rep(f("g_ffn").reshape(D)),
        "w_r": np.ascontiguousarray(np.concatenate([f("w_rg")[0], f("w_re")[0]], 1)),
        "b_r": rep(np.concatenate([f("b_rg")[0], f("b_re")[0]])),
        "w_gate": f("w_gate")[0], "w_up": f("w_up")[0], "w_down": f("w_down")[0],
        "r_iota": rep(np.arange(NE, dtype=np.float32)),
        "r_blocks": rep(np.arange(ROWS // BLK, dtype=np.float32) * BLK),
        "r_places": rep(np.arange(NBLK, dtype=np.float32)),
        "r_tri": np.ascontiguousarray(np.stack([i < j, i < P + j], 1).astype(np.float32)),
        "r_tok": (i + P * np.arange(NT)[None]).astype(np.int32),
        "r_valid": (i + P * np.arange(NT)[None] < SEQ + NS).astype(np.float32),
        "conv0": f("state_conv").reshape(DEC_B, CONV - 1, CCH),
        "delta0": f("state_delta").reshape(DEC_B, BH, BD, BD),
        "cache_k": f("cache_win_k").reshape(DEC_B, W_BUF, AW),
        "cache_v": f("cache_win_v").reshape(DEC_B, W_BUF, AW),
        "gs_cols": rep((np.arange(NS)[None] // DEC_T == np.arange(DEC_B)[:, None]).astype(np.float32)),
        "gs_rows": np.ascontiguousarray(np.stack([i // DEC_T == np.arange(DEC_B)[None], i == DEC_T * np.arange(DEC_B)[None] + DEC_T - 1], 1).astype(np.float32)),
        "g_gdn": rep(f("g_gdn").reshape(BD)),
        "g_mix": cols("g_mix"),
        "g_qa": rep(f("g_qa").reshape(AD)),
        "g_ka": rep(f("g_ka").reshape(AD)),
        "w_in": f("w_in").reshape(D, IN_COLS),
    }


SCRATCH = {
    "i_rows": (NBLK * BLK, 1), "i_dst": (P, 2, NT), "wts": (P, 2, NT), "i_exp": (P, NBLK), "yb": (NBLK, P, D),
    "lg": (NT, P, NG + NE),
    "oa": (NT, P, AW), "ox": (NT, P, XW), "qx": (NT, P, XW), "h1": (NT, P, D), "h2": (NT, P, D), "hn": (NT, P, D),
    "att": (len(DILS), NT, P, AH * (AD + 2)),
    "q": (NT, P, AW), "u": (CONV - 1 + ROWS, CCH), "ob": (NT, P, BW), "us": (DEC_B, CONV - 1 + DEC_T, CCH), "z": (NT, P, BW), "ab": (NT, P, 2 * BH),
}
OUTPUTS = {
    "k": (NT, P, AW), "v": (NT, P, AW), "delta_p": (BH, BD, BD), "delta_s": (DEC_B, BH, BD, BD),
    "y": (NT, P, D), "mem_kp": (NMEM // P, P, XW), "mem_vp": (NMEM // P, P, XW),
    "win_k": (DEC_B, W_BUF, AW), "win_v": (DEC_B, W_BUF, AW), "conv_p": (CONV - 1, CCH), "conv_s": (DEC_B, CONV - 1, CCH),
}


def declare(nc, arrays, debug=False):
    t = {}
    for n, v in arrays.items():
        t[n] = nc.dram_tensor(f"in_{n}", v.shape, mybir.dt.from_np(v.dtype), kind="ExternalInput").ap()
    for n, sh in OUTPUTS.items():
        t[n] = nc.dram_tensor(f"out_{n}", sh, F32, kind="ExternalOutput").ap()
    for n, sh in SCRATCH.items():
        dt = I32 if n.startswith("i_") else F32
        if debug:
            t[n] = nc.dram_tensor(f"out_{n}", sh, dt, kind="ExternalOutput").ap()
        else:
            t[n] = nc.dram_tensor(f"tmp_{n}", sh, dt, kind="Internal").ap()
    return t


def kernel(**inputs):
    import concourse.bacc as bacc
    from concourse.bass_utils import run_bass_kernel_spmd

    arrays = layout(inputs)
    nc = bacc.Bacc("TRN2", target_bir_lowering=False, num_devices=1)
    t = declare(nc, arrays)
    build(nc, t)
    r = run_bass_kernel_spmd(nc, [{f"in_{n}": a for n, a in arrays.items()}], core_ids=[0]).results[0]
    out = {n: r[f"out_{n}"] for n in OUTPUTS}
    flat = {n: out[n].reshape((ROWS, -1)) for n in ("k", "v", "y")}
    return (flat["y"][:SEQ].reshape(1, SEQ, D), flat["y"][SEQ:SEQ + NS].reshape(DEC_B, DEC_T, D),
            flat["k"][:SEQ].reshape(1, 1, SEQ, AH, AD), flat["v"][:SEQ].reshape(1, 1, SEQ, AH, AD),
            out["conv_p"].reshape(1, 1, CONV - 1, CCH), out["delta_p"].reshape(1, 1, BH, BD, BD),
            out["mem_kp"].reshape(1, 1, NMEM, XH, XD), out["mem_vp"].reshape(1, 1, NMEM, XH, XD),
            out["win_k"].reshape(1, DEC_B, W_BUF, AH, AD), out["win_v"].reshape(1, DEC_B, W_BUF, AH, AD),
            out["conv_s"].reshape(1, DEC_B, CONV - 1, CCH), out["delta_s"].reshape(1, DEC_B, BH, BD, BD))
```

```python
from contextlib import ExitStack, contextmanager

import numpy as np
import concourse.bass as bass
from concourse import mybir

F32 = mybir.dt.float32
F32R = mybir.dt.float32r
I32 = mybir.dt.int32
U32 = mybir.dt.uint32
BF16 = mybir.dt.bfloat16
ALU = mybir.AluOpType
ACT = mybir.ActivationFunctionType
AXX = mybir.AxisListType.X
bf16 = mybir.dt.np(BF16)

P = 128
D = 1024
KD = D // P
SEQ = 2048
DEC_B = 8
DEC_T = 8
NS = DEC_B * DEC_T
PT = SEQ // P
NT = PT + 1
ROWS = NT * P
AH, AD = 8, 64
AW = AH * AD
BH, BD = 4, 128
BW = BH * BD
CONV = 4
CCH = 3 * BW
IN_COLS = 3 * AW + 4 * BW + 2 * BH
W_BUF = 1024
XH, XD = 4, 128
XW = XH * XD
NMEM = 256
NG, GE = 4, 8
NE = NG * GE
FF = D // 2
EPS = 1e-6
NEG = -1e30
DILS = (1, 4, 16)
BLK = 128
NBLK = -(-2 * (SEQ + NS) // BLK) + NE
NBLK += NBLK % 2
NBX = NBLK + 4


class Stage:

    def __init__(self, nc, name):
        self.nc, self.name, self.stack, self.sems = nc, name, ExitStack(), []

    def __enter__(self):
        return self

    def __exit__(self, *e):
        self.stack.__exit__(*e)
        if e[0] is None:
            self.nc.clear_and_free_semaphores(self.sems)
            self.nc.all_engine_barrier()

    def sb(self, name, shape, dt=F32):
        return self.stack.enter_context(self.nc.sbuf_tensor(f"{self.name}_{name}", shape, dt))

    def ps(self, name, shape, dt=F32):
        return self.stack.enter_context(self.nc.psum_tensor(f"{self.name}_{name}", shape, dt))

    def sem(self, *names):
        out = [self.nc.alloc_semaphore(f"{self.name}_{n}") for n in names]
        self.sems += out
        return out[0] if len(out) == 1 else out


class Chain:

    def __init__(self, eng, sem, per, turn):
        self.eng, self.sem, self.base, self.per, self.n = eng, sem, turn * per, per, 0

    def mark(self, ins):
        self.n += 1
        return ins.then_inc(self.sem, 1)

    def wait(self):
        self.eng.wait_ge(self.sem, self.base + self.n)

    def then(self, ins):
        self.mark(ins)
        self.wait()

    def done(self):
        assert self.n == self.per, f"{self.n} steps a turn, not {self.per}"


def need(eng, sem, value):
    if not isinstance(value, int) or value > 0:
        eng.wait_ge(sem, value)


def each(*parts):
    for step, tile in parts:
        if not isinstance(tile, int) or 0 <= tile < NT:
            step(tile)


def bc(ap, shape):
    return ap.unsqueeze(len(shape) - 1).to_broadcast(shape)


def split(eng, hi, lo, x, hi_ok, value):
    eng.tensor_copy(hi, x).then_inc(hi_ok, 1)
    eng.wait_ge(hi_ok, value)
    return eng.tensor_tensor(lo, x, hi.bitcast(F32), ALU.subtract)


def matmul3(pe, out, ah, al, bh, bl, start, stop):
    pe.matmul(out, ah, bh, start=start, stop=False)
    pe.matmul(out, ah, bl, start=False, stop=False)
    return pe.matmul(out, al, bh, start=False, stop=stop)


def project_in(nc, t):
    rows_u = t["u"][CONV - 1:].rearrange("(n p) c -> n p c", p=P)
    project_columns(nc, t, "ina", [(0, AW, t["q"]), (AW, 2 * AW, t["k"]), (2 * AW, 3 * AW, t["v"]), (3 * AW, 3 * AW + BW, rows_u[:, :, 0:BW])])


def project_in_rest(nc, t):
    rows_u = t["u"][CONV - 1:].rearrange("(n p) c -> n p c", p=P)
    u1, u2 = 3 * AW + BW, 3 * AW + 2 * BW
    z = 3 * AW + CCH
    project_columns(nc, t, "inb", [(u1, u2, rows_u[:, :, BW:2 * BW]), (z + BW, IN_COLS, t["ab"]), (u2, z, rows_u[:, :, 2 * BW:]), (z, z + BW, t["z"])])


def project_columns(nc, t, name, chunks):
    first_part = name == "ina"
    lo, hi = chunks[0][0], max(b for _, b, _ in chunks)
    C = len(chunks)
    with Stage(nc, name) as s:
        w = s.sb("w", [P, 2, KD, hi - lo], F32R)
        raw = s.sb("raw", [P, 2, hi - lo])
        ident = s.sb("ident", [P, P])
        gmix = s.sb("gmix", [P, KD])
        gqk = s.sb("gqk", [P, 2, AD])
        x = s.sb("x", [P, D])
        xn = s.sb("xn", [P, D])
        nT = s.sb("nT", [P, 2, KD * P], F32R)
        st = s.sb("st", [P, 4])
        qs = s.sb("qs", [P, 2, AW])
        hs = s.sb("hs", [P, 2, 3, AH])
        out = s.sb("out", [P, hi - lo])
        zero = s.sb("zero", [CONV - 1, CCH])
        pt = s.ps("pt", [P, 2 * 512])
        po = s.ps("po", [P, C, 512])
        names = ("consts_in w_in0 w_in1 w_hi w_ok x_in ss_ok mean_ok root_ok rstd_ok xn_ok x_turned nT_hi nT_ok proj halfway sq_ok hmean_ok hroot_ok own "
                 "moved0 moved1 moved2 moved3 stored0 stored1 stored2 stored3 zero_ok zero_in moved_on carried").split()
        E = dict(zip(names, s.sem(*names)))
        moved, stored = ([E[n + str(c)] for c in range(C)] for n in ("moved", "stored"))
        cols = [slice(a - lo, b - lo) for a, b, _ in chunks]
        samples = lambda ap: ap.rearrange("(b r) c -> b r c", b=DEC_B)
        vh = lambda ap: ap.rearrange("p (h d) -> p h d", h=AH)

        def order(eng, turn):
            for i in (-1, 0):
                turn(i)
            with eng.Fori(1, NT - 1) as i:
                turn(i)
            turn(NT - 1)

        with nc.Block() as block:
            @block.sync
            def _(sp):
                def stores(i):
                    for c, (_, _, dst) in enumerate(chunks):
                        sp.wait_ge(moved[c], i + 1)
                        sp.dma_start(dst[i], out[:, cols[c]]).then_inc(stored[c], 16)

                def carry(dst, src):
                    sp.dma_start(dst, src).then_inc(E["carried"], 16)

                for dst, src in ((ident[:], t["ident"]), (gmix[:], t["g_mix"]), (gqk[:, 0], t["g_qa"]), (gqk[:, 1], t["g_ka"])):
                    sp.dma_start(dst, src).then_inc(E["consts_in"], 16)
                for k in range(KD):
                    need(sp, E["w_ok"], k - 1)
                    sp.dma_start(raw[:, k % 2], t["w_in"][k * P:(k + 1) * P, lo:hi]).then_inc(E[f"w_in{k % 2}"], 16)
                if first_part:
                    sp.wait_ge(E["zero_ok"], 1)
                    sp.dma_start(t["u"][0:CONV - 1], zero[:]).then_inc(E["zero_in"], 16)
                    sp.wait_ge(E["zero_in"], 16)
                else:
                    for dst, src in ((t["win_k"], t["k"]), (t["win_v"], t["v"])):
                        carry(dst[:, W_BUF - DEC_T:], samples(src.rearrange("n p c -> (n p) c")[SEQ:SEQ + NS]))
                    carry(t["us"][:, 0:CONV - 1], t["conv0"])
                order(sp, lambda i: each((stores, i)))
                for c in range(C):
                    sp.wait_ge(stored[c], NT * 16)
                if not first_part:
                    us = samples(t["u"][CONV - 1 + SEQ:CONV - 1 + SEQ + NS])
                    carry(t["us"][:, CONV - 1:], us)
                    carry(t["conv_p"], t["u"][SEQ:SEQ + CONV - 1])
                    carry(t["conv_s"], us[:, DEC_T - CONV + 1:])
                    sp.wait_ge(E["carried"], 16 * 6)

            @block.gpsimd
            def _(pool):
                def load(i):
                    need(pool, E["xn_ok"], i)
                    pool.dma_start(x[:], t["x"][i]).then_inc(E["x_in"], 16)

                if first_part:
                    pool.memset(zero[:], 0.0).then_inc(E["zero_ok"], 1)
                order(pool, lambda i: each((load, i + 1)))

            @block.scalar
            def _(act):
                def norm(i):
                    act.wait_ge(E["x_in"], i * 16 + 16)
                    need(act, E["x_turned"], i)
                    act.activation(xn[:], x[:], ACT.Square, accum_out=st[:, 0:1]).then_inc(E["ss_ok"], 1)
                    act.wait_ge(E["mean_ok"], i + 1)
                    act.activation(st[:, 2:3], st[:, 1:2], ACT.Sqrt).then_inc(E["root_ok"], 1)
                    act.wait_ge(E["rstd_ok"], i + 1)
                    act.activation(xn[:], x[:], ACT.Copy, scale=st[:, 3:4]).then_inc(E["xn_ok"], 1)

                def move(i):
                    for c in range(C):
                        act.wait_ge(E["proj"], i * C + c + 1)
                        need(act, moved[c], i)
                        if first_part and c < 2:
                            act.activation(qs[:, c, :], po[:, c, :], ACT.Square).then_inc(E["sq_ok"], 1)
                            act.wait_ge(E["hmean_ok"], i * 2 + c + 1)
                            act.activation(hs[:, c, 1, :], hs[:, c, 0, :], ACT.Sqrt).then_inc(E["hroot_ok"], 1)
                        else:
                            need(act, stored[c], i * 16)
                            act.activation(out[:, cols[c]], po[:, c, 0:cols[c].stop - cols[c].start], ACT.Copy).then_inc(moved[c], 1)

                act.wait_ge(E["consts_in"], 64)
                norm(0)
                for k in range(KD):
                    act.wait_ge(E[f"w_in{k % 2}"], 16 * (k // 2) + 16)
                    act.activation(w[:, 0, k], raw[:, k % 2], ACT.Copy, scale=gmix[:, k:k + 1]).then_inc(E["w_hi"], 1)
                new, old = (t["win_k"], t["cache_k"]) if first_part else (t["win_v"], t["cache_v"])
                piece = (W_BUF - DEC_T) // (NT - 2) // DEC_T * DEC_T

                def window(i):
                    if isinstance(i, int) and i < NT - 1:
                        return
                    n = W_BUF - DEC_T - piece * (NT - 2) if isinstance(i, int) else piece
                    at = (i - 1) * piece
                    act.dma_start(new[:, bass.ds(at, n)], old[:, bass.ds(at + DEC_T, n)]).then_inc(E["moved_on"], 16)

                order(act, lambda i: None if isinstance(i, int) and i < 0 else each((norm, i + 1), (window, i), (move, i)))
                act.wait_ge(E["moved_on"], (NT - 1) * 16)

            @block.vector
            def _(dve):
                def norm(i):
                    dve.wait_ge(E["ss_ok"], i + 1)
                    dve.tensor_scalar(st[:, 1:2], st[:, 0:1], 1.0 / D, EPS, ALU.mult, ALU.add).then_inc(E["mean_ok"], 1)
                    dve.wait_ge(E["root_ok"], i + 1)
                    dve.reciprocal(st[:, 3:4], st[:, 2:3]).then_inc(E["rstd_ok"], 1)

                def heads(i):
                    if not first_part:
                        return
                    own = Chain(dve, E["own"], 6, i)
                    for c in range(2):
                        a, b = ((1.0, AD * EPS), (1.0 / AD, EPS))[c]
                        dve.wait_ge(E["sq_ok"], i * 2 + c + 1)
                        own.then(dve.tensor_reduce(hs[:, c, 2, :], vh(qs[:, c, :]), AXX, ALU.add))
                        dve.tensor_scalar(hs[:, c, 0, :], hs[:, c, 2, :], a, b, ALU.mult, ALU.add).then_inc(E["hmean_ok"], 1)
                        dve.wait_ge(E["hroot_ok"], i * 2 + c + 1)
                        own.then(dve.reciprocal(hs[:, c, 2, :], hs[:, c, 1, :]))
                        own.then(dve.tensor_tensor(vh(qs[:, c, :]), vh(po[:, c, :]), bc(hs[:, c, 2, :], [P, AH, AD]), ALU.mult))
                        need(dve, stored[c], i * 16)
                        dve.tensor_tensor(vh(out[:, cols[c]]), vh(qs[:, c, :]),
                                          gqk[:, c].unsqueeze(1).to_broadcast([P, AH, AD]), ALU.mult).then_inc(moved[c], 1)
                    own.done()

                def turned(i):
                    dve.wait_ge(E["x_turned"], i + 1)
                    for h in range(2):
                        need(dve, (E["halfway"], E["proj"])[h], i * (1, C)[h])
                        kk = slice(512 * h, 512 * h + 512)
                        split(dve, nT[:, 0, kk], nT[:, 1, kk], pt[:, kk], E["nT_hi"], 2 * i + h + 1).then_inc(E["nT_ok"], 1)

                dve.wait_ge(E["consts_in"], 64)
                norm(0)
                turned(0)
                for k in range(KD):
                    dve.wait_ge(E["w_hi"], k + 1)
                    dve.scalar_tensor_tensor(out=w[:, 1, k], in0=raw[:, k % 2], scalar=gmix[:, k:k + 1], in1=w[:, 0, k].bitcast(F32),
                                             op0=ALU.mult, op1=ALU.subtract).then_inc(E["w_ok"], 1)
                order(dve, lambda i: None if isinstance(i, int) and i < 0 else each((norm, i + 1), (heads, i), (turned, i + 1)))

            @block.tensor
            def _(pe):
                def turn(i):
                    pe.wait_ge(E["xn_ok"], i + 1)
                    need(pe, E["nT_ok"], 2 * i)
                    for k in range(KD):
                        last = pe.transpose(pt[:, k * P:(k + 1) * P], xn[:, k * P:(k + 1) * P], ident[:])
                    last.then_inc(E["x_turned"], 1)

                def product(i, c):
                    need(pe, moved[c], i)
                    for k in range(KD):
                        if c == 0 and k % 4 == 0:
                            pe.wait_ge(E["nT_ok"], 2 * i + k // 4 + 1)
                        if isinstance(i, int) and i == 0 and c == 0:
                            pe.wait_ge(E["w_ok"], k + 1)
                        kk = slice(k * P, (k + 1) * P)
                        last = matmul3(pe, po[:, c, 0:cols[c].stop - cols[c].start], nT[:, 0, kk], nT[:, 1, kk],
                                       w[:, 0, k, cols[c]], w[:, 1, k, cols[c]], k == 0, k == KD - 1)
                        if c == C - 1 and k == KD // 2 - 1:
                            last.then_inc(E["halfway"], 1)
                    last.then_inc(E["proj"], 1)

                pe.wait_ge(E["consts_in"], 64)
                order(pe, lambda i: each((lambda i: product(i, 0), i), (lambda i: product(i, 1), i), (turn, i + 1),
                                         (lambda i: product(i, 2), i), (lambda i: product(i, 3), i)))


def attend_prompt(nc, t):
    VA = AD + 1
    with Stage(nc, "att") as s:
        ident = s.sb("ident", [P, P])
        identb = s.sb("identb", [P, P], BF16)
        mask = s.sb("mask", [P, 2 * 2 * P], BF16)
        raw = s.sb("raw", [P, 2, 2, AW])
        qT = s.sb("qT", [P, 4, P])
        kT = s.sb("kT", [P, 4, 4, P])
        va = s.sb("va", [P, 4, AH, VA])
        prob = s.sb("prob", [P, 2, AH, 2 * P])
        pT = s.sb("pT", [P, 4, 4, P])
        res = s.sb("res", [P, 2, AH * VA + AH])
        score = s.ps("score", [P, AH, 2 * P])
        turn = s.ps("turn", [P, 2, 512])
        outp = s.ps("outp", [P, 2, 512])
        raw_in = s.sem("raw_in0", "raw_in1")
        stored = s.sem("stored0", "stored1")
        v_in = s.sem("v_in0", "v_in1", "v_in2", "v_in3")
        (consts_in, ones_ok, qk_turned, qk_moved, score_ok, max_ok, exp_ok, p_turned,
         p_moved, pv_ok, o_moved) = s.sem(
            "consts_in", "ones_ok", "qk_turned", "qk_moved", "score_ok", "max_ok",
            "exp_ok", "p_turned", "p_moved", "pv_ok", "o_moved")
        flat = {n: t[n].rearrange("n p c -> (n p) c")[0:SEQ] for n in "qkv"}

        def place(h):
            return h // 4 * 4 + h % 2 * 2 + h % 4 // 2

        def rows(ap, d, i, u):
            if d == 1:
                return ap.rearrange("(n g j) c -> n g j c", g=4, j=P)[i, u]
            if d == 4:
                return ap.rearrange("(n j r) c -> r n j c", r=4, j=P)[i, u]
            return ap.rearrange("(j s g) c -> s g j c", s=4, g=4)[i, u]

        def groups(eng, group):
            group(0, 1, 0, (False, True, True, True))
            with eng.Fori(1, 4) as i:
                group(i, 1, i, (True,) * 4)
            with eng.Fori(0, 4) as i:
                group(i + 4, 4, i, (False, True, True, True))
            with eng.Fori(0, 4) as i:
                group(i + 8, 16, i, (False,) * 4)

        def both(ahead, behind):
            def group(g, d, i, prev):
                for u in range(5):
                    if u < 4:
                        ahead(g * 4 + u, g, u, d, i, prev[u])
                    if u > 0 and behind:
                        behind(g * 4 + u - 1, g, u - 1, d, i, prev[u - 1])
            return group

        def uses(g, u):
            return g * 2 + u // 2

        with nc.Block() as block:
            @block.sync
            def _(sp):
                sp.dma_start(ident[:], t["ident"]).then_inc(consts_in, 16)
                sp.dma_start(identb[:], t["identb"]).then_inc(consts_in, 16)
                sp.dma_start(mask[:], t["att_mask"]).then_inc(consts_in, 16)

                def load(b, g, u, d, i, prev):
                    need(sp, qk_turned, 2 * b - 2)
                    for n, name in enumerate("qk"):
                        sp.dma_start(raw[:, u % 2, n, :], rows(flat[name], d, i, u)).then_inc(raw_in[u % 2], 16)
                    need(sp, pv_ok, 2 * b - 4)
                    sp.dma_start(va[:, u, :, 0:AD], rows(flat["v"], d, i, u).rearrange("p (h d) -> p h d", h=AH)).then_inc(v_in[u], 16)

                groups(sp, both(load, None))

            @block.gpsimd
            def _(pool):
                pool.memset(va[:, :, :, AD:VA], 1.0).then_inc(ones_ok, 1)

            @block.scalar
            def _(act):
                def ahead(b, g, u, d, i, prev):
                    for n, dst in ((0, qT[:]), (1, kT[:, :, u, :])):
                        act.wait_ge(qk_turned, 2 * b + n + 1)
                        act.activation(dst, turn[:, n, :].rearrange("p (c n) -> p c n", c=4),
                                       ACT.Copy).then_inc(qk_moved, 1)
                    lo = 0 if prev else P
                    for h in range(AH):
                        if h % 4 == 0:
                            act.wait_ge(max_ok, 2 * b + h // 4 + 1)
                        e = act.activation(prob[:, u % 2, h, lo:], score[:, place(h), lo:], ACT.Exp,
                                           bias=res[:, u % 2, AH * VA + h:AH * VA + h + 1])
                        if h % 4 == 3:
                            e.then_inc(exp_ok, 1)

                def behind(b, g, u, d, i, prev):
                    for h in range(2):
                        act.wait_ge(pv_ok, 2 * b + h + 1)
                        act.activation(res[:, u % 2, h * 4 * VA:(h + 1) * 4 * VA], outp[:, h, 0:4 * VA],
                                       ACT.Copy).then_inc(o_moved, 1)
                    act.wait_ge(o_moved, 2 * b + 2)
                    dst = t["att"][DILS.index(d)].rearrange("n p c -> (n p) c")[0:SEQ]
                    act.dma_start(rows(dst, d, i, u), res[:, u % 2, :]).then_inc(stored[u % 2], 16)

                groups(act, both(ahead, behind))
                for k in range(2):
                    act.wait_ge(stored[k], len(DILS) * PT // 2 * 16)

            @block.vector
            def _(dve):
                def ahead(b, g, u, d, i, prev):
                    lo = 0 if prev else P
                    for h in range(2):
                        dve.wait_ge(score_ok, 2 * b + h + 1)
                        if h == 0:
                            need(dve, stored[u % 2], uses(g, u) * 16)
                        m = res[:, u % 2, AH * VA + 4 * h:AH * VA + 4 * h + 4].rearrange("p (c a) -> p a c", a=2)
                        dve.tensor_reduce(m, score[:, 4 * h:4 * h + 4, lo:].rearrange("p (a c) k -> p a c k", a=2),
                                          AXX, ALU.max, negate=True).then_inc(max_ok, 1)

                def behind(b, g, u, d, i, prev):
                    n = 4 if prev else 2
                    for j in range(4):
                        dve.wait_ge(p_turned, 4 * b + j + 1)
                        dve.tensor_copy(pT[:, j, 0:n, :], turn[:, j % 2, 0:n * P].rearrange("p (c n) -> p c n", c=n)).then_inc(p_moved, 1)

                groups(dve, both(ahead, behind))

            @block.tensor
            def _(pe):
                pe.wait_ge(consts_in, 48)
                pe.wait_ge(ones_ok, 1)

                def ahead(b, g, u, d, i, prev):
                    pe.wait_ge(raw_in[u % 2], uses(g, u) * 32 + 32)
                    need(pe, p_moved, 4 * (b - 1) if u else 4 * b)
                    for n in range(2):
                        for c in range(4):
                            last = pe.transpose(turn[:, n, c * P:(c + 1) * P], raw[:, u % 2, n, c * P:(c + 1) * P], ident[:])
                        last.then_inc(qk_turned, 1)
                    need(pe, exp_ok, 2 * b)
                    for h in range(2):
                        for n in range(2):
                            pe.matmul(score[:, 4 * h + 2 * n:4 * h + 2 * n + 2, :], identb[:], mask[:], start=True, stop=True)
                    pe.wait_ge(qk_moved, 2 * b + 2)
                    for h in range(AH):
                        r = slice(AD * (h % 2), AD * (h % 2) + AD)
                        parts = [(P, u)]
                        if prev:
                            parts = [(0, u - 1, 2)] if u else [(0, 3), (P, 0)]
                        for part in parts:
                            w = 2 if len(part) == 3 else 1
                            last = pe.matmul(score[:, place(h), part[0]:part[0] + w * P], qT[r, h // 2, :],
                                             kT[r, h // 2, part[1]:part[1] + w, :], start=False,
                                             stop=True, skip_group_check=True)
                        if h % 4 == 3:
                            last.then_inc(score_ok, 1)

                def behind(b, g, u, d, i, prev):
                    halves = 2 if prev else 1

                    def turn_p(j):
                        if j % 2 == 0:
                            pe.wait_ge(exp_ok, 2 * b + j // 2 + 1)
                        if j >= 2:
                            pe.wait_ge(p_moved, 4 * b + j - 1)
                        for h in range(2):
                            for k in range(halves):
                                c = (2 - halves + k) * P
                                last = pe.transpose(turn[:, j % 2, (h * halves + k) * P:(h * halves + k + 1) * P],
                                                    prob[:, u % 2, 2 * j + h, c:c + P], ident[:])
                        last.then_inc(p_turned, 1)

                    def product(j):
                        pe.wait_ge(p_moved, 4 * b + j + 1)
                        if j == 0:
                            pe.wait_ge(v_in[u], g * 16 + 16)
                            need(pe, o_moved, 2 * b)
                        for h in range(2):
                            for k in range(halves):
                                slot = (u - halves + 1 + k) % 4
                                last = pe.matmul(outp[:, j // 2, (2 * (j % 2) + h) * VA:(2 * (j % 2) + h + 1) * VA],
                                                 pT[:, j, h * halves + k, :], va[:, slot, 2 * j + h, :],
                                                 start=(j % 2 == 0 and h == 0 and k == 0), stop=(k == halves - 1),
                                                 skip_group_check=True)
                        if j % 2 == 1:
                            last.then_inc(pv_ok, 1)

                    turn_p(0)
                    turn_p(1)
                    product(0)
                    turn_p(2)
                    product(1)
                    turn_p(3)
                    product(2)
                    product(3)

                groups(pe, both(ahead, behind))


G_LNB, G_CUM, G_GAM, G_BETA, G_BGAM, G_TAIL, G_LAST0, G_LAST1, G_KINDS = range(9)


def gates(nc, s, t, cst, tiles, first, chunks, sample):
    G = s.sb("G", [P, tiles, G_KINDS, BH])
    with Stage(nc, s.name + "g") as r:
        ab = r.sb("ab", [P, tiles, 2, BH])
        par = r.sb("par", [P, 2, BH])
        xx = r.sb("xx", [P, tiles, 2, BH])
        ax = r.sb("ax", [P, tiles, 2, BH])
        m = r.sb("m", [P, 2 + chunks, P])
        g = r.sb("g", [P, tiles, BH])
        na = r.sb("na", [P, BH])
        acc = r.ps("acc", [P, 4, 512])
        loaded, dv, sc, mm = r.sem("loaded", "dv", "sc", "mm")
        n = tiles * BH
        with nc.Block() as block:
            @block.sync
            def _(sp):
                sp.dma_start(ab[:].rearrange("p n a h -> p n (a h)"),
                             t["ab"][first:first + tiles].rearrange("n p c -> p n c")).then_inc(loaded, 16)
                sp.dma_start(par[:], t["gate_par"]).then_inc(loaded, 16)
                sp.dma_start(m[:], t[cst + "_sums"]).then_inc(loaded, 16)

            @block.vector
            def _(dve):
                own = Chain(dve, dv, 0, 0)
                dve.wait_ge(loaded, 48)
                own.mark(dve.tensor_tensor(xx[:, :, 0, :], ab[:, :, 0, :],
                                           par[:, 1, :].unsqueeze(1).to_broadcast([P, tiles, BH]), ALU.add))
                own.then(dve.tensor_scalar(xx[:, :, 1, :], ab[:, :, 1, :], -1.0, None, ALU.mult))
                own.then(dve.tensor_scalar(ax[:], xx[:], -1.0, None, ALU.mult))
                own.then(dve.tensor_tensor(ax[:], ax[:], xx[:], ALU.min))
                dve.wait_ge(sc, 1)
                own.then(dve.tensor_scalar(ax[:], ax[:], 1.0, None, ALU.add))
                dve.wait_ge(sc, 2)
                own.then(dve.tensor_scalar(xx[:], xx[:], 0.0, None, ALU.max))
                own.then(dve.tensor_tensor(xx[:], xx[:], ax[:], ALU.add))
                dve.wait_ge(sc, 3)
                own.then(dve.tensor_tensor(g[:], xx[:, :, 0, :], na[:].unsqueeze(1).to_broadcast([P, tiles, BH]), ALU.mult))
                own.then(dve.tensor_scalar(g[:], g[:], -1.0, None, ALU.mult))
                own.then(dve.tensor_scalar(G[:, :, G_LNB, :], xx[:, :, 1, :], -1.0, None, ALU.mult))
                dve.wait_ge(mm, 1)
                v = lambda k: acc[:, k, 0:n].rearrange("p (n h) -> p n h", h=BH)
                own.then(dve.tensor_copy(G[:, :, G_CUM, :], v(0)))
                own.then(dve.tensor_tensor(G[:, :, G_TAIL, :], v(1), G[:, :, G_CUM, :], ALU.subtract))
                own.then(dve.tensor_tensor(G[:, :, G_BGAM, :], G[:, :, G_LNB, :], G[:, :, G_CUM, :], ALU.add))
                for c in range(chunks):
                    own.then(dve.tensor_copy(G[:, :, G_LAST0 + c, :], v(2 + c)))

            @block.scalar
            def _(act):
                act.wait_ge(dv, 4)
                act.activation(ax[:], ax[:], ACT.Exp).then_inc(sc, 1)
                act.wait_ge(dv, 5)
                act.activation(ax[:], ax[:], ACT.Ln).then_inc(sc, 1)
                act.activation(na[:], par[:, 0, :], ACT.Exp).then_inc(sc, 1)
                act.wait_ge(dv, 13 + chunks)
                act.activation(G[:, :, G_GAM, :], G[:, :, G_CUM, :], ACT.Exp).then_inc(sc, 1)
                act.activation(G[:, :, G_BETA, :], G[:, :, G_LNB, :], ACT.Exp).then_inc(sc, 1)
                act.activation(G[:, :, G_BGAM, :], G[:, :, G_BGAM, :], ACT.Exp).then_inc(sc, 1)
                for k in [G_TAIL] + [G_LAST0 + c for c in range(chunks)]:
                    act.activation(G[:, :, k, :], G[:, :, k, :], ACT.Exp).then_inc(sc, 1)

            @block.tensor
            def _(pe):
                pe.wait_ge(loaded, 48)
                pe.wait_ge(dv, 9)
                for k in range(2 + chunks):
                    last = pe.matmul(acc[:, k, 0:n], m[:, k, :], g[:].rearrange("p n h -> p (n h)"), start=True, stop=True)
                last.then_inc(mm, 1)
    return G


def delta_net(nc, t, sample=False):
    cst = "gs" if sample else "gp"
    tiles = 1 if sample else PT
    first = PT if sample else 0
    levels = 3 if sample else 6
    C = P // 2
    R = slice(0, C) if sample else slice(0, P)
    n_consts = 9 if sample else 7
    with Stage(nc, cst) as s:
        G = gates(nc, s, t, cst, tiles, first, 0 if sample else 2, sample)
        ident = s.sb("ident", [P, P])
        identb = s.sb("identb", [P, P], BF16)
        ones = s.sb("ones", [P, 2, P])
        maskb = s.sb("maskb", [P, 2, BH * P], BF16)
        lvl = s.sb("lvl", [P, levels, P])
        wc = s.sb("wc", [P, CONV, CCH])
        gout = s.sb("gout", [P, BD])
        U = s.sb("U", [P, CONV, CCH])
        cv = s.sb("cv", [P, CCH])
        uu = s.sb("uu", [P, 3, BH, BD])
        z = s.sb("z", [P, BH, BD])
        sq = s.sb("sq", [P, 2 * BH, BD])
        nrm = s.sb("nrm", [P, 4, 2, BH])
        cur = s.sb("cur", [P, G_KINDS, BH])
        fac = s.sb("fac", [P, 4, BH])
        kh = s.sb("kh", [P, BH, BD])
        qh = s.sb("qh", [P, BH, BD])
        qg = s.sb("qg", [P, BH, BD])
        kb = s.sb("kb", [P, BH, BD])
        kt = s.sb("kt", [P, BH, BD])
        vb = s.sb("vb", [P, BH, BD])
        dg = s.sb("dg", [P, BH, P])
        kqT = s.sb("kqT", [P, BH, 2, P])
        qgT = s.sb("qgT", [P, BH, P])
        dec = s.sb("dec", [P, 2, BH, P])
        A = s.sb("A", [P, BH, P])
        KQ = s.sb("KQ", [P, BH, P])
        As = s.sb("As", [P, levels, BH, P])
        MN = s.sb("MN", [P, BH, 2, P])
        Y = s.sb("Y", [P, BH, P])
        WT = s.sb("WT", [P, BH, P])
        uv = s.sb("uv", [P, BH, BD])
        u = s.sb("u", [P, BH, BD])
        ob = s.sb("ob", [P, BH, BD])
        fo = s.sb("fo", [P, 4, BH])
        sqo = s.sb("sqo", [P, BH, BD])
        late = s.sb("late", [P, 2, BH])
        if sample:
            S = s.sb("S", [P, DEC_B, BH, BD])
            cm = s.sb("cm", [P, DEC_B, C])
            rm = s.sb("rm", [P, 2, DEC_B])
            WTm = s.sb("WTm", [P, BH, DEC_B, C])
            qTm = s.sb("qTm", [P, BH, DEC_B, C])
            um = s.sb("um", [P, 2, DEC_B, BD])
            gl = s.sb("gl", [P, BH, DEC_B])
            last = s.sb("last", [P, BH, DEC_B])
        else:
            S = s.sb("S", [P, BH, BD])
            Sl = s.sb("Sl", [P, BH, BD])
        pk = s.ps("pk", [P, 4, 512])
        pd = s.ps("pd", [P, 2, BH // 2, 2, P])
        pw = s.ps("pw", [P, 512])
        po = s.ps("po", [P, 512])
        E = dict(zip(*(lambda n: (n, s.sem(*n)))(
            "consts_in conv_ok u_in z_in u_silu z_silu taps_ok qk_sq qk_sum qk_inv late_ok n2_ok n_ok cur_ok fac_ok kh_ok qh_ok qg_ok dg_ok kb_ok "
            "kt_ok vb_ok zg_ok turned_k turned_q turned_qg kT_ok qT_ok qgT_ok sums_ok dec_ok kkq_ok A_ok KQ_ok "
            "As_ok A0T_ok MN_ok Y_mm Y_ok step_mm half_ok WT_mm WT_ok uv_mm uv_ok ws_mm u_ok ds_mm Sl_ok "
            "S_ok o_mm o_sq o_n2 o_root ob_ok tile_done stored own_front own_dve own_pool "
            "gl_ok WTm_ok qTm_ok um_ok last_mm last_ok S_in S_out pad_ok".split())))
        halves = ((0, 2), (2, 4))
        h3 = lambda ap: ap.rearrange("p (h n) -> p h n", h=BH)

        def order(body):
            if tiles == 1:
                return lambda eng: body(0, False)

            def run(eng):
                body(0, True)
                with eng.Fori(1, tiles - 1) as i:
                    body(i, True)
                body(tiles - 1, False)
            return run

        with nc.Block() as block:
            @block.sync
            def _(sp):
                for dst, name in ((ident, "ident"), (identb, "identb"), (ones, "ones"), (maskb, cst + "_mask"),
                                  (lvl, cst + "_lvl"), (gout, "g_gdn")):
                    sp.dma_start(dst[:], t[name]).then_inc(E["consts_in"], 16)
                sp.dma_start(wc[:], t["conv_w"].partition_broadcast(P)).then_inc(E["consts_in"], 16)
                if sample:
                    sp.dma_start(cm[:], t["gs_cols"]).then_inc(E["consts_in"], 16)
                    sp.dma_start(rm[:], t["gs_rows"]).then_inc(E["consts_in"], 16)
                    for b in range(DEC_B):
                        sp.dma_start(S[:, b], t["delta0"][b].rearrange("h k v -> k h v")).then_inc(E["S_in"], 16)

                def rows(i):
                    sp.wait_ge(E["conv_ok"], i + 1)
                    for k in range(CONV):
                        if sample:
                            for b in range(DEC_B):
                                sp.dma_start(U[b * DEC_T:(b + 1) * DEC_T, k, :], t["us"][b, k:k + DEC_T, :]).then_inc(E["u_in"], 16)
                        else:
                            sp.dma_start(U[:, k, :], t["u"][k:k + SEQ].rearrange("(n p) c -> n p c", p=P)[i]).then_inc(E["u_in"], 16)

                def z_load(i):
                    sp.dma_start(z[:].rearrange("p h d -> p (h d)"), t["z"][i + first]).then_inc(E["z_in"], 16)

                def body(i, more, rows_too):
                    if rows_too:
                        rows(i + 2)
                    sp.wait_ge(E["tile_done"], i + 1)
                    sp.dma_start(t["ob"][i + first], ob[:].rearrange("p h d -> p (h d)")).then_inc(E["stored"], 16)
                    if more:
                        z_load(i + 1)

                rows(0)
                z_load(0)
                if sample:
                    body(0, False, False)
                else:
                    rows(1)
                    with sp.Fori(0, tiles - 2) as i:
                        body(i, True, True)
                    body(tiles - 2, True, False)
                    body(tiles - 1, False, False)
                sp.wait_ge(E["stored"], tiles * 16)

            u_loads = 16 * CONV * (DEC_B if sample else 1)

            @block.gpsimd
            def _(pool):
                pool.wait_ge(E["consts_in"], n_consts * 16)
                if sample:
                    pool.memset(U[:], 0.0).then_inc(E["conv_ok"], 1)
                else:
                    pool.sem_inc(E["conv_ok"], 1)

                def taps(i):
                    pool.wait_ge(E["u_in"], i * u_loads + u_loads)
                    for k in range(CONV):
                        pool.tensor_tensor(U[:, k, :], U[:, k, :], wc[:, k, :], ALU.mult).then_inc(E["taps_ok"], 1)

                def convolution(i):
                    own = Chain(pool, E["own_pool"], 2, i)
                    pool.wait_ge(E["taps_ok"], i * CONV + CONV)
                    own.mark(pool.tensor_tensor(U[:, 0, :], U[:, 0, :], U[:, 1, :], ALU.add))
                    own.then(pool.tensor_tensor(U[:, 2, :], U[:, 2, :], U[:, 3, :], ALU.add))
                    own.done()
                    need(pool, E["u_silu"], i)
                    pool.tensor_tensor(cv[:], U[:, 0, :], U[:, 2, :], ALU.add).then_inc(E["conv_ok"], 1)

                def body(i, more):
                    pool.wait_ge(E["fac_ok"], i + 1)
                    need(pool, E["ds_mm"], 2 * i)
                    pool.tensor_tensor(vb[:], uu[:, 2], bc(cur[:, G_BETA, :], [P, BH, BD]), ALU.mult).then_inc(E["vb_ok"], 1)
                    pool.tensor_tensor(kb[:], uu[:, 1], bc(fac[:, 1, :], [P, BH, BD]), ALU.mult).then_inc(E["kb_ok"], 1)
                    pool.tensor_tensor(kt[:], uu[:, 1], bc(fac[:, 2, :], [P, BH, BD]), ALU.mult).then_inc(E["kt_ok"], 1)
                    if more:
                        taps(i + 1)
                    if more:
                        convolution(i + 1)
                    pool.wait_ge(E["z_silu"], i + 1)
                    pool.tensor_tensor(z[:], z[:], gout[:].unsqueeze(1).to_broadcast([P, BH, BD]), ALU.mult).then_inc(E["zg_ok"], 1)

                taps(0)
                convolution(0)
                order(body)(pool)

            @block.scalar
            def _(act):

                def silu(i):
                    act.wait_ge(E["conv_ok"], i + 2)
                    need(act, E["kt_ok"], i)
                    need(act, E["qg_ok"], i)
                    act.activation(uu[:].rearrange("p a h d -> p (a h d)"), cv[:], ACT.Silu).then_inc(E["u_silu"], 1)
                    act.wait_ge(E["u_silu"], i + 1)
                    act.activation(sq[:], uu[:, 0:2].rearrange("p a h d -> p (a h) d"), ACT.Square).then_inc(E["qk_sq"], 1)

                def roots(i):
                    act.wait_ge(E["n2_ok"], i + 1)
                    act.activation(nrm[:, 2], nrm[:, 1], ACT.Sqrt).then_inc(E["n_ok"], 1)

                def body(i, more):
                    for ev, out, dst, k in (("turned_k", "kT_ok", kqT[:, :, 0, :], 0), ("turned_q", "qT_ok", kqT[:, :, 1, :], 1),
                                            ("turned_qg", "qgT_ok", qgT[:], 2)):
                        act.wait_ge(E[ev], i + 1)
                        act.activation(dst, h3(pk[:, k, :]), ACT.Copy).then_inc(E[out], 1)
                    act.wait_ge(E["sums_ok"], i + 1)
                    for k in range(2):
                        src = (pw, po)[k]
                        for h in range(BH):
                            act.activation(dec[:, k, h, :], src[:, h * P:(h + 1) * P], ACT.Exp,
                                           bias=(fac[:, 3, h:h + 1], nrm[:, 3, 0, h:h + 1])[k]).then_inc(E["dec_ok"], 1)
                    act.wait_ge(E["z_in"], i * 16 + 16)
                    act.activation(z[:], z[:], ACT.Silu).then_inc(E["z_silu"], 1)
                    for q in range(1, levels):
                        for a, (lo, hi) in enumerate(halves):
                            act.wait_ge(E["Y_mm"], i * 2 * (levels - 1) + 2 * (q - 1) + a + 1)
                            act.activation(Y[:, lo:hi, :], pk[:, 1 + a, 0:2 * P].rearrange("p (h n) -> p h n", h=2),
                                           ACT.Copy).then_inc(E["Y_ok"], 1)
                    act.wait_ge(E["uv_mm"], i + 1)
                    act.activation(uv[:], pd[:, 1].rearrange("p a b n -> p (a b) n"), ACT.Copy).then_inc(E["uv_ok"], 1)
                    act.activation(WT[:], pd[:, 0].rearrange("p a b n -> p (a b) n"), ACT.Copy).then_inc(E["WT_ok"], 1)
                    if more:
                        silu(i + 1)
                        roots(i + 1)
                    if sample:
                        act.wait_ge(E["last_mm"], 1)
                        act.activation(last[:], pk[:, 3, 0:BH * DEC_B].rearrange("p (h b) -> p h b", b=DEC_B), ACT.Exp).then_inc(E["last_ok"], 1)
                    act.wait_ge(E["o_mm"], i + 1)
                    act.activation(sqo[R], h3(po[R, :]), ACT.Square).then_inc(E["o_sq"], 1)
                    act.wait_ge(E["o_n2"], i + 1)
                    act.activation(fo[R, 2], fo[R, 1], ACT.Sqrt).then_inc(E["o_root"], 1)

                silu(0)
                roots(0)
                order(body)(act)
                if sample:
                    act.wait_ge(E["S_ok"], 2 * BH)
                    for b in range(DEC_B):
                        act.dma_start(t["delta_s"][b].rearrange("h k v -> k h v"), S[:, b]).then_inc(E["S_out"], 16)
                    act.wait_ge(E["S_out"], 16 * DEC_B)
                else:
                    act.wait_ge(E["S_ok"], 2 * tiles + 1)
                    act.dma_start(t["delta_p"].rearrange("h k v -> k h v"), S[:]).then_inc(E["S_out"], 16)
                    act.wait_ge(E["S_out"], 16)

            @block.vector
            def _(dve):
                if sample:
                    dve.memset(ob[:], 0.0).then_inc(E["pad_ok"], 1)
                    dve.wait_ge(E["pad_ok"], 1)
                else:
                    dve.memset(S[:], 0.0).then_inc(E["S_ok"], 1)
                dve.wait_ge(E["consts_in"], n_consts * 16)

                def front(i):
                    own = Chain(dve, E["own_front"], 1, i)
                    need(dve, E["kt_ok"], i)
                    kinds = G_LAST0 if sample else G_KINDS
                    own.then(dve.tensor_copy(cur[:, 0:kinds, :], G[:, 0 if sample else i, 0:kinds, :]))
                    own.done()
                    dve.tensor_tensor(dg[:], ident[:].unsqueeze(1).to_broadcast([P, BH, P]), bc(cur[:, G_CUM, :], [P, BH, P]),
                                      ALU.mult).then_inc(E["dg_ok"], 1)
                    dve.tensor_scalar(nrm[:, 3, 0, :], cur[:, G_CUM, :], -1.0, None, ALU.mult).then_inc(E["cur_ok"], 1)
                    dve.tensor_tensor(fac[:, 3, :], cur[:, G_CUM, :], cur[:, G_LNB, :], ALU.add).then_inc(E["cur_ok"], 1)

                def norms(i):
                    dve.wait_ge(E["qk_sq"], i + 1)
                    dve.tensor_reduce(nrm[:, 0].rearrange("p a h -> p (a h)"), sq[:], AXX, ALU.add).then_inc(E["qk_sum"], 1)
                    dve.wait_ge(E["qk_sum"], i + 1)
                    dve.tensor_scalar(nrm[:, 1, 0], nrm[:, 0, 0], float(BD), BD * EPS, ALU.mult, ALU.add).then_inc(E["cur_ok"], 1)
                    dve.tensor_scalar(nrm[:, 1, 1], nrm[:, 0, 1], EPS, None, ALU.add).then_inc(E["n2_ok"], 1)

                def scaled(i):
                    dve.wait_ge(E["n_ok"], i + 1)
                    dve.reciprocal(nrm[:, 0], nrm[:, 2]).then_inc(E["qk_inv"], 1)
                    dve.wait_ge(E["qk_inv"], i + 1)
                    dve.tensor_tensor(kh[:], uu[:, 1], bc(nrm[:, 0, 1], [P, BH, BD]), ALU.mult).then_inc(E["kh_ok"], 1)
                    dve.tensor_tensor(fac[:, 0, :], nrm[:, 0, 0], cur[:, G_GAM, :], ALU.mult).then_inc(E["cur_ok"], 1)
                    dve.tensor_tensor(fac[:, 1:3, :], cur[:, G_BGAM:G_TAIL + 1, :],
                                      nrm[:, 0, 1].unsqueeze(1).to_broadcast([P, 2, BH]), ALU.mult).then_inc(E["fac_ok"], 1)
                    dve.tensor_tensor(qh[:], uu[:, 0], bc(nrm[:, 0, 0], [P, BH, BD]), ALU.mult).then_inc(E["qh_ok"], 1)
                    dve.wait_ge(E["cur_ok"], i * 4 + 4)
                    dve.tensor_tensor(qg[:], uu[:, 0], bc(fac[:, 0, :], [P, BH, BD]), ALU.mult).then_inc(E["qg_ok"], 1)

                def body(i, more):
                    own = Chain(dve, E["own_dve"], 2, i)
                    dve.wait_ge(E["kkq_ok"], i + 1)
                    dve.wait_ge(E["dec_ok"], i * 2 * BH + BH)
                    kkq = pd[:].rearrange("p a b k n -> p (a b) k n")
                    dve.tensor_tensor(A[:], kkq[:, :, 0, :], dec[:, 0], ALU.mult).then_inc(E["A_ok"], 1)
                    dve.wait_ge(E["dec_ok"], i * 2 * BH + 2 * BH)
                    dve.tensor_tensor(KQ[:], kkq[:, :, 1, :], dec[:, 1], ALU.mult).then_inc(E["KQ_ok"], 1)
                    dve.wait_ge(E["A_ok"], i + 1)

                    def quarter(q):
                        dve.tensor_tensor(As[:, q], A[:], lvl[:, q].unsqueeze(1).to_broadcast([P, BH, P]), ALU.mult).then_inc(E["As_ok"], 1)

                    quarter(0)
                    dve.wait_ge(E["As_ok"], i * levels + 1)
                    ib = ident[:].unsqueeze(1).to_broadcast([P, BH, P])
                    dve.tensor_tensor(MN[:, :, 1, :], ib, As[:, 0], ALU.subtract).then_inc(E["MN_ok"], 1)
                    quarter(1)
                    dve.wait_ge(E["A0T_ok"], i + 1)
                    dve.tensor_tensor(MN[:, :, 0, :], ib, h3(pk[:, 0, :]), ALU.subtract).then_inc(E["MN_ok"], 1)
                    for q in range(1, levels):
                        if q + 1 < levels:
                            quarter(q + 1)
                        for a, (lo, hi) in enumerate(halves):
                            if q == 1 and a == 0:
                                dve.wait_ge(E["MN_ok"], i * 2 + 2)
                            dve.wait_ge(E["step_mm"], i * 2 * (levels - 1) + 2 * (q - 1) + a + 1)
                            dve.tensor_tensor(MN[:, lo:hi], MN[:, lo:hi], pd[:, a], ALU.subtract).then_inc(E["half_ok"], 1)
                    if more:
                        front(i + 1)
                    if not sample:
                        dve.tensor_copy(late[:], G[:, i, G_LAST0:G_LAST0 + 2, :]).then_inc(E["late_ok"], 1)
                        dve.wait_ge(E["late_ok"], i + 1)
                        dve.wait_ge(E["uv_ok"], i + 1)
                        for c in range(2):
                            if more and c == 1:
                                norms(i + 1)
                            r = slice(C * c, C * c + C)
                            dve.wait_ge(E["S_ok"], i * 2 + c + 1)
                            dve.tensor_tensor(Sl[:], S[:], bc(late[:, c, :], [P, BH, BD]), ALU.mult).then_inc(E["Sl_ok"], 1)
                            dve.wait_ge(E["ws_mm"], i * 2 + c + 1)
                            dve.tensor_tensor(u[r], uv[r], h3(pw[r, :]), ALU.subtract).then_inc(E["u_ok"], 1)
                            dve.wait_ge(E["ds_mm"], i * 2 + c + 1)
                            dve.wait_ge(E["Sl_ok"], i * 2 + c + 1)
                            dve.tensor_tensor(S[:], Sl[:], h3(pk[:, 3, :]), ALU.add).then_inc(E["S_ok"], 1)
                    else:
                        spread = lambda ap: ap[:, :, 0:C].unsqueeze(2).to_broadcast([P, BH, DEC_B, C])
                        cmb = cm[:].unsqueeze(1).to_broadcast([P, BH, DEC_B, C])
                        dve.tensor_tensor(gl[:], bc(cur[:, G_CUM, :], [P, BH, DEC_B]),
                                          rm[:, 1].unsqueeze(1).to_broadcast([P, BH, DEC_B]), ALU.mult).then_inc(E["gl_ok"], 1)
                        dve.wait_ge(E["WT_ok"], 1)
                        dve.tensor_tensor(WTm[:], spread(WT), cmb, ALU.mult).then_inc(E["WTm_ok"], 1)
                        dve.tensor_tensor(qTm[:], spread(qgT), cmb, ALU.mult).then_inc(E["qTm_ok"], 1)
                        dve.wait_ge(E["uv_ok"], 1)
                        dve.wait_ge(E["ws_mm"], 1)
                        dve.tensor_tensor(u[R], uv[R], h3(pw[R, :]), ALU.subtract).then_inc(E["u_ok"], 1)
                        dve.wait_ge(E["o_mm"], 1)
                        dve.wait_ge(E["last_ok"], 1)
                        for b in range(DEC_B):
                            dve.tensor_tensor(S[:, b], S[:, b], bc(last[:, :, b], [P, BH, BD]), ALU.mult).then_inc(E["Sl_ok"], 1)
                        for h in range(BH):
                            if h >= 2:
                                dve.wait_ge(E["ds_mm"], h - 1)
                            dve.tensor_tensor(um[R, h % 2], u[R, h].unsqueeze(1).to_broadcast([C, DEC_B, BD]),
                                              bc(rm[R, 0], [C, DEC_B, BD]), ALU.mult).then_inc(E["um_ok"], 1)
                            dve.wait_ge(E["ds_mm"], h + 1)
                            if h == 0:
                                dve.wait_ge(E["Sl_ok"], DEC_B)
                            for a in range(2):
                                dve.tensor_tensor(S[:, 4 * a:4 * a + 4, h, :], S[:, 4 * a:4 * a + 4, h, :],
                                                  h3(pk[:, 1 + a, :]), ALU.add).then_inc(E["S_ok"], 1)
                    if more:
                        scaled(i + 1)
                    dve.wait_ge(E["o_sq"], i + 1)
                    own.then(dve.tensor_reduce(fo[R, 0], sqo[R], AXX, ALU.add))
                    dve.tensor_scalar(fo[R, 1], fo[R, 0], 1.0 / BD, EPS, ALU.mult, ALU.add).then_inc(E["o_n2"], 1)
                    dve.wait_ge(E["o_root"], i + 1)
                    dve.wait_ge(E["zg_ok"], i + 1)
                    own.then(dve.reciprocal(fo[R, 3], fo[R, 2]))
                    need(dve, E["stored"], i * 16)
                    dve.tensor_tensor(ob[R], h3(po[R, :]), bc(fo[R, 3], [R.stop, BH, BD]), ALU.mult).then_inc(E["ob_ok"], 1)
                    dve.wait_ge(E["ob_ok"], i + 1)
                    dve.tensor_tensor(ob[R], ob[R], z[R], ALU.mult).then_inc(E["tile_done"], 1)
                    own.done()

                front(0)
                norms(0)
                scaled(0)
                order(body)(dve)

            @block.tensor
            def _(pe):
                pe.wait_ge(E["consts_in"], n_consts * 16)

                def body(i, more):
                    for ev, out, src, k in (("kh_ok", "turned_k", kh, 0), ("qh_ok", "turned_q", qh, 1), ("qg_ok", "turned_qg", qg, 2)):
                        pe.wait_ge(E[ev], i + 1)
                        for h in range(BH):
                            last = pe.transpose(pk[:, k, h * P:(h + 1) * P], src[:, h, :], ident[:])
                        last.then_inc(E[out], 1)
                    pe.wait_ge(E["dg_ok"], i + 1)
                    need(pe, E["ob_ok"], i)
                    for k, dst in ((0, pw), (1, po)):
                        pe.matmul(dst[:, :], ones[:, k, :], dg[:].rearrange("p h n -> p (h n)"), start=True, stop=False)
                        last = pe.matmul(dst[:, :], identb[:], maskb[:, k, :], start=False, stop=True)
                    last.then_inc(E["sums_ok"], 1)
                    pe.wait_ge(E["kT_ok"], i + 1)
                    pe.wait_ge(E["qT_ok"], i + 1)
                    for h in range(BH):
                        last = pe.matmul(pd[:, h // 2, h % 2], kqT[:, h, 0, :], kqT[:, h], start=True, stop=True)
                    last.then_inc(E["kkq_ok"], 1)
                    pe.wait_ge(E["As_ok"], i * levels + 1)
                    for h in range(BH):
                        last = pe.transpose(pk[:, 0, h * P:(h + 1) * P], As[:, 0, h, :], ident[:])
                    last.then_inc(E["A0T_ok"], 1)
                    pe.wait_ge(E["KQ_ok"], i + 1)
                    pe.wait_ge(E["qgT_ok"], i + 1)
                    for q in range(1, levels):
                        pe.wait_ge(E["As_ok"], i * levels + q + 1)
                        for a, (lo, hi) in enumerate(halves):
                            if q == 1:
                                pe.wait_ge(E["MN_ok"], i * 2 + 2)
                            else:
                                pe.wait_ge(E["half_ok"], i * 2 * (levels - 1) + 2 * (q - 2) + a + 1)
                            for h in range(lo, hi):
                                last = pe.matmul(pk[:, 1 + a, (h - lo) * P:(h - lo + 1) * P], As[:, q, h, :], MN[:, h, 0, :], start=True, stop=True)
                            last.then_inc(E["Y_mm"], 1)
                        for a, (lo, hi) in enumerate(halves):
                            pe.wait_ge(E["Y_ok"], i * 2 * (levels - 1) + 2 * (q - 1) + a + 1)
                            for h in range(lo, hi):
                                pe.matmul(pd[:, a, h - lo, 0, :], MN[:, h, 1, :], Y[:, h, :], start=True, stop=True)
                                last = pe.matmul(pd[:, a, h - lo, 1, :], Y[:, h, :], MN[:, h, 1, :], start=True, stop=True)
                            last.then_inc(E["step_mm"], 1)
                    pe.wait_ge(E["half_ok"], i * 2 * (levels - 1) + 2 * (levels - 1))
                    pe.wait_ge(E["vb_ok"], i + 1)
                    for h in range(BH):
                        last = pe.matmul(pd[:, 1, h // 2, h % 2], MN[:, h, 0, :], vb[:, h, :], start=True, stop=True)
                    pe.wait_ge(E["kb_ok"], i + 1)
                    for h in range(BH):
                        last = pe.matmul(pd[:, 0, h // 2, h % 2], kb[:, h, :], MN[:, h, 0, :], start=True, stop=True)
                    last.then_inc(E["uv_mm"], 1)
                    pe.wait_ge(E["WT_ok"], i + 1)
                    pe.wait_ge(E["kt_ok"], i + 1)
                    if not sample:
                        for c in range(2):
                            r = slice(C * c, C * c + C)
                            pe.wait_ge(E["S_ok"], i * 2 + c + 1)
                            for h in range(BH):
                                last = pe.matmul(pw[r, h * BD:(h + 1) * BD], WT[:, h, r], S[:, h, :], start=True, stop=True)
                            last.then_inc(E["ws_mm"], 1)
                            for h in range(BH):
                                pe.matmul(po[r, h * BD:(h + 1) * BD], qgT[:, h, r], S[:, h, :], start=(h == 0), stop=False, skip_group_check=True)
                            pe.wait_ge(E["u_ok"], i * 2 + c + 1)
                            for h in range(BH):
                                last = pe.matmul(pk[:, 3, h * BD:(h + 1) * BD], kt[r, h, :], u[r, h, :], start=True, stop=True)
                            last.then_inc(E["ds_mm"], 1)
                        for h in range(BH):
                            last = pe.matmul(po[:, h * BD:(h + 1) * BD], KQ[:, h, :], u[:, h, :], start=False, stop=True, skip_group_check=True)
                        last.then_inc(E["o_mm"], 1)
                    else:
                        pe.wait_ge(E["S_in"], 16 * DEC_B)
                        pe.wait_ge(E["WTm_ok"], 1)
                        for h in range(BH):
                            for b in range(DEC_B):
                                last = pe.matmul(pw[R, h * BD:(h + 1) * BD], WTm[:, h, b, :], S[:, b, h, :],
                                                 start=(b == 0), stop=(b == DEC_B - 1))
                        last.then_inc(E["ws_mm"], 1)
                        pe.wait_ge(E["qTm_ok"], 1)
                        for h in range(BH):
                            for b in range(DEC_B):
                                pe.matmul(po[R, h * BD:(h + 1) * BD], qTm[:, h, b, :], S[:, b, h, :],
                                          start=(h == 0 and b == 0), stop=False, skip_group_check=True)
                        pe.wait_ge(E["u_ok"], 1)
                        for h in range(BH):
                            last = pe.matmul(po[R, h * BD:(h + 1) * BD], KQ[R, h, R], u[R, h, :], start=False, stop=True, skip_group_check=True)
                        last.then_inc(E["o_mm"], 1)
                        pe.wait_ge(E["gl_ok"], 1)
                        pe.matmul(pk[:, 3, 0:BH * DEC_B], ones[:, 1, :], gl[:].rearrange("p h b -> p (h b)"),
                                  start=True, stop=True).then_inc(E["last_mm"], 1)
                        for h in range(BH):
                            pe.wait_ge(E["um_ok"], h + 1)
                            if h:
                                pe.wait_ge(E["S_ok"], 2 * h)
                            for a in range(2):
                                mm = pe.matmul(pk[:, 1 + a, :], kt[R, h, :], um[R, h % 2, 4 * a:4 * a + 4, :], start=True, stop=True)
                            mm.then_inc(E["ds_mm"], 1)

                order(body)(pe)


def attend_sample(nc, t, mem):
    H = XH if mem else AH
    R = H * DEC_T
    full = NMEM // P if mem else 6
    new = 0 if mem else DEC_T
    NK = full * P + new
    tiles = [(j, P) for j in range(full)] + ([(full, new)] if new else [])
    T = len(tiles)
    CH = AW // P
    splits = [(0, min(NK, 512))] + ([(512, NK)] if NK > 512 else [])
    qname, oname = ("qx", "ox") if mem else ("q", "oa")
    with Stage(nc, "sm" if mem else "sw") as s:
        ident = s.sb("ident", [P, P])
        q = s.sb("q", [P, AW])
        qT = s.sb("qT", [P, CH, NS])
        qz = s.sb("qz", [P, CH, R])
        hm = s.sb("hm", [P, CH, H])
        kk = s.sb("kk", [P, T, AW])
        vv = s.sb("vv", [P, T, AW])
        kT = s.sb("kT", [P, CH, NK])
        mult = s.sb("mult", [R, NK])
        sc = s.sb("sc", [R, NK])
        pr = s.sb("pr", [R, NK])
        st = s.sb("st", [R, 4])
        pT = s.sb("pT", [P, T, R])
        om = s.sb("om", [R, AW])
        own_cols = s.sb("own_cols", [R, AW])
        sel = s.sb("sel", [R, DEC_T])
        oT = s.sb("oT", [P, CH, NS])
        o = s.sb("o", [P, AW])
        tr = s.ps("tr", [P, 2, 512])
        ps = s.ps("ps", [P, 2, 512])
        pp = s.ps("pp", [P, 512])
        pv = s.ps("pv", [P, 512])
        px = s.ps("px", [P, 512])
        names = ("consts_in q_in pad_ok qT_mm qT_ok k_in v_in qz_ok kT_mm kT_ok score_ok sc_ok max_ok exp_ok pT_mm "
                 "seen pT_ok pv_ok rden_ok on_ok om_ok sel_mm oT_ok back_mm o_ok stored").split()
        E = dict(zip(names, s.sem(*names)))
        k_loads = (2 if mem else 4) * 16

        def loads(eng, b, dst, cache, newrows, sem):
            if mem:
                for j in range(full):
                    eng.dma_start(dst[:, j, :], cache[b, j * P:(j + 1) * P, :]).then_inc(sem, 16)
            else:
                far = cache[b, 0:W_BUF // 2].rearrange("(j n r) c -> j n r c", j=2, r=16)
                for j in range(2):
                    eng.dma_start(dst[:, j, :], far[j, :, 0:DEC_T, :]).then_inc(sem, 16)
                eng.dma_start(dst[:, 2:6, :], cache[b, W_BUF // 2:].rearrange("(j p) c -> p j c", p=P)).then_inc(sem, 16)
                eng.dma_start(dst[0:new, full, :], newrows[b]).then_inc(sem, 16)

        with nc.Block() as block:
            @block.sync
            def _(sp):
                ck, cv = (t["mem_k"], t["mem_v"]) if mem else (t["cache_k"], t["cache_v"])
                nk = t["k"][PT, 0:NS].rearrange("(b r) c -> b r c", b=DEC_B)
                nv = t["v"][PT, 0:NS].rearrange("(b r) c -> b r c", b=DEC_B)
                sp.dma_start(q[:], t[qname][PT]).then_inc(E["q_in"], 16)
                sp.dma_start(ident[:], t["ident"]).then_inc(E["consts_in"], 16)
                pre = "sm_" if mem else "sw_"
                for dst, name in ((hm, "hm"), (own_cols, "own"), (sel, "sel")):
                    sp.dma_start(dst[:], t[pre + name]).then_inc(E["consts_in"], 16)
                sp.dma_start(mult[:], t[pre + "mult"]).then_inc(E["consts_in"], 16)
                with sp.Fori(0, DEC_B) as b:
                    sp.wait_ge(E["kT_mm"], b * T + 1)
                    loads(sp, b, kk, ck, nk, E["k_in"])
                    sp.wait_ge(E["pv_ok"], b + 1)
                    loads(sp, b, vv, cv, nv, E["v_in"])
                sp.wait_ge(E["o_ok"], 1)
                sp.dma_start(t[oname][PT], o[:]).then_inc(E["stored"], 16)
                sp.wait_ge(E["stored"], 16)

            @block.scalar
            def _(act):
                act.wait_ge(E["qT_mm"], 1)
                act.activation(qT[:], px[:, 0:CH * NS].rearrange("p (c n) -> p c n", c=CH), ACT.Copy).then_inc(E["qT_ok"], 1)
                with act.Fori(0, DEC_B) as b:
                    for j, n in tiles:
                        act.wait_ge(E["kT_mm"], b * T + j + 2)
                        if j == 0:
                            act.wait_ge(E["score_ok"], b + 1)
                        act.activation(kT[:, :, j * P:j * P + n], tr[:, j % 2, 0:CH * n].rearrange("p (c n) -> p c n", c=CH),
                                       ACT.Copy).then_inc(E["kT_ok"], 1)
                    act.wait_ge(E["max_ok"], b + 1)
                    act.wait_ge(E["pT_mm"], b + 1)
                    act.activation(pr[:], sc[:], ACT.Exp, bias=st[:, 0:1], accum_out=st[:, 1:2]).then_inc(E["exp_ok"], 1)
                    act.wait_ge(E["pT_mm"], b + 2)
                    act.wait_ge(E["pv_ok"], b + 1)
                    act.activation(pT[:], pp[:, 0:T * R].rearrange("p (j r) -> p j r", j=T), ACT.Copy).then_inc(E["pT_ok"], 1) \
                        if not new else None
                    if new:
                        act.activation(pT[:, 0:full], pp[:, 0:full * R].rearrange("p (j r) -> p j r", j=full), ACT.Copy).then_inc(E["pT_ok"], 1)
                        act.activation(pT[0:new, full], pp[0:new, full * R:T * R], ACT.Copy).then_inc(E["pT_ok"], 1)
                    act.wait_ge(E["rden_ok"], b + 1)
                    act.wait_ge(E["pv_ok"], b + 2)
                    act.wait_ge(E["om_ok"], b + 1)
                    act.activation(om[:], pv[0:R, :], ACT.Copy, scale=st[:, 2:3]).then_inc(E["on_ok"], 1)

            @block.vector
            def _(dve):
                dve.sem_inc(E["om_ok"], 1)
                dve.memset(o[:], 0.0).then_inc(E["pad_ok"], 1)
                dve.wait_ge(E["consts_in"], 80)
                dve.wait_ge(E["qT_ok"], 1)
                with dve.Fori(0, DEC_B) as b:
                    dve.wait_ge(E["score_ok"], b + 1)
                    dve.tensor_tensor(qz[:].rearrange("p c (h n) -> p c h n", h=H),
                                      qT[:, :, bass.ds(b * DEC_T, DEC_T)].unsqueeze(2).to_broadcast([P, CH, H, DEC_T]),
                                      hm[:].unsqueeze(3).to_broadcast([P, CH, H, DEC_T]), ALU.mult).then_inc(E["qz_ok"], 1)
                    dve.wait_ge(E["score_ok"], b + 2)
                    for k, (lo, hi) in enumerate(splits):
                        dve.tensor_tensor(sc[:, lo:hi], ps[0:R, k, 0:hi - lo], mult[:, lo:hi], ALU.add).then_inc(E["sc_ok"], 1)
                    dve.wait_ge(E["sc_ok"], (b + 1) * len(splits))
                    dve.tensor_reduce(st[:, 0:1], sc[:], AXX, ALU.max, negate=True).then_inc(E["max_ok"], 1)
                    dve.wait_ge(E["exp_ok"], b + 1)
                    dve.reciprocal(st[:, 2:3], st[:, 1:2]).then_inc(E["rden_ok"], 1)
                    dve.wait_ge(E["on_ok"], b + 1)
                    dve.tensor_tensor(om[:], om[:], own_cols[:], ALU.mult).then_inc(E["om_ok"], 1)
                    dve.wait_ge(E["sel_mm"], b + 1)
                    dve.tensor_copy(oT[:, :, bass.ds(b * DEC_T, DEC_T)],
                                    px[:, 0:CH * DEC_T].rearrange("p (c n) -> p c n", c=CH)).then_inc(E["oT_ok"], 1)
                dve.wait_ge(E["back_mm"], 1)
                dve.wait_ge(E["pad_ok"], 1)
                dve.tensor_copy(o[0:NS, :], pv[0:NS, :]).then_inc(E["o_ok"], 1)

            @block.tensor
            def _(pe):
                pe.sem_inc(E["kT_mm"], 1)
                pe.sem_inc(E["pv_ok"], 1)
                pe.sem_inc(E["score_ok"], 1)
                pe.sem_inc(E["pT_mm"], 1)
                pe.wait_ge(E["consts_in"], 80)
                pe.wait_ge(E["q_in"], 16)
                for c in range(CH):
                    last = pe.transpose(px[:, c * NS:(c + 1) * NS], q[0:NS, c * P:(c + 1) * P], ident[0:NS, 0:NS])
                last.then_inc(E["qT_mm"], 1)
                with pe.Fori(0, DEC_B) as b:
                    pe.wait_ge(E["k_in"], b * k_loads + k_loads)
                    for j, n in tiles:
                        if j >= 2:
                            pe.wait_ge(E["kT_ok"], b * T + j - 1)
                            pe.sem_inc(E["seen"], 1)
                        for c in range(CH):
                            last = pe.transpose(tr[:, j % 2, c * n:(c + 1) * n], kk[0:n, j, c * P:(c + 1) * P], ident[0:n, 0:n])
                        last.then_inc(E["kT_mm"], 1)
                    pe.wait_ge(E["kT_ok"], b * T + T)
                    pe.wait_ge(E["qz_ok"], b + 1)
                    for k, (lo, hi) in enumerate(splits):
                        for c in range(CH):
                            last = pe.matmul(ps[0:R, k, 0:hi - lo], qz[:, c, :], kT[:, c, lo:hi], start=(c == 0), stop=(c == CH - 1))
                    last.then_inc(E["score_ok"], 1)
                    pe.wait_ge(E["exp_ok"], b + 1)
                    pe.sem_inc(E["seen"], 1)
                    for j, n in tiles:
                        last = pe.transpose(pp[0:n, j * R:(j + 1) * R], pr[:, j * P:j * P + n], ident[0:R, 0:R])
                    last.then_inc(E["pT_mm"], 1)
                    pe.wait_ge(E["v_in"], b * k_loads + k_loads)
                    pe.wait_ge(E["pT_ok"], b * (2 if new else 1) + (2 if new else 1))
                    pe.wait_ge(E["om_ok"], b + 1)
                    for j, n in tiles:
                        last = pe.matmul(pv[0:R, :], pT[0:n, j, :], vv[0:n, j, :], start=(j == 0), stop=(j == T - 1))
                    last.then_inc(E["pv_ok"], 1)
                    pe.wait_ge(E["om_ok"], b + 2)
                    for c in range(CH):
                        last = pe.matmul(px[:, c * DEC_T:(c + 1) * DEC_T], om[:, c * P:(c + 1) * P], sel[:], start=True, stop=True)
                    last.then_inc(E["sel_mm"], 1)
                pe.wait_ge(E["oT_ok"], DEC_B)
                for c in range(CH):
                    last = pe.transpose(pv[0:NS, c * P:(c + 1) * P], oT[:, c, :], ident[:])
                last.then_inc(E["back_mm"], 1)


def attend_window_sample(nc, t):
    attend_sample(nc, t, mem=False)


def attend_memory_sample(nc, t):
    attend_sample(nc, t, mem=True)


def memory_kv(nc, t):
    M = NMEM // P
    with Stage(nc, "mkv") as s:
        ident = s.sb("ident", [P, P])
        w = s.sb("w", [P, 2, KD, XW])
        gm = s.sb("gm", [P, KD])
        gk = s.sb("gk", [P, XD])
        x = s.sb("x", [P, M, D])
        xn = s.sb("xn", [P, D])
        nT = s.sb("nT", [P, KD, P])
        st = s.sb("st", [P, M, 4])
        sq = s.sb("sq", [P, XH, XD])
        kst = s.sb("kst", [P, 3, XH])
        kv = s.sb("kv", [P, M, 2, XH, XD])
        tr = s.ps("tr", [P, 2, 512])
        po = s.ps("po", [P, 2, 512])
        names = ("loaded w_in ss_ok mean_ok root_ok rstd_ok xn_ok xT_ok nT_ok kv_mm sq_ok sum_ok n2_ok kroot_ok krec_ok kn_ok k_ok v_ok stored").split()
        E = dict(zip(names, s.sem(*names)))
        v3 = lambda ap: ap.rearrange("p (h d) -> p h d", h=XH)
        with nc.Block() as block:
            @block.sync
            def _(sp):
                sp.dma_start(x[:], t["mem"].rearrange("n p d -> p n d")).then_inc(E["loaded"], 16)
                sp.dma_start(ident[:], t["ident"]).then_inc(E["loaded"], 16)
                sp.dma_start(gm[:], t["g_mem"]).then_inc(E["loaded"], 16)
                sp.dma_start(gk[:], t["g_xk"]).then_inc(E["loaded"], 16)
                for n, name in enumerate(("w_xk", "w_xv")):
                    sp.dma_start(w[:, n], t[name].rearrange("(k p) c -> p k c", p=P)).then_inc(E["w_in"], 16)
                for i in range(M):
                    sp.wait_ge(E["k_ok"], i + 1)
                    sp.dma_start(t["mem_kp"][i], kv[:, i, 0].rearrange("p h d -> p (h d)")).then_inc(E["stored"], 16)
                    sp.wait_ge(E["v_ok"], i + 1)
                    sp.dma_start(t["mem_vp"][i], kv[:, i, 1].rearrange("p h d -> p (h d)")).then_inc(E["stored"], 16)
                sp.wait_ge(E["stored"], 32 * M)

            @block.scalar
            def _(act):
                act.wait_ge(E["loaded"], 64)
                for i in range(M):
                    need(act, E["xT_ok"], i)
                    act.activation(xn[:], x[:, i], ACT.Square, accum_out=st[:, i, 0:1]).then_inc(E["ss_ok"], 1)
                    act.wait_ge(E["mean_ok"], i + 1)
                    act.activation(st[:, i, 2:3], st[:, i, 1:2], ACT.Sqrt).then_inc(E["root_ok"], 1)
                    act.wait_ge(E["rstd_ok"], i + 1)
                    act.activation(xn[:], x[:, i], ACT.Copy, scale=st[:, i, 3:4]).then_inc(E["xn_ok"], 1)
                    act.wait_ge(E["kv_mm"], 2 * i + 1)
                    need(act, E["kn_ok"], i)
                    act.activation(sq[:], v3(po[:, 0, :]), ACT.Square).then_inc(E["sq_ok"], 1)
                    act.wait_ge(E["n2_ok"], i + 1)
                    act.activation(kst[:, 2], kst[:, 1], ACT.Sqrt).then_inc(E["kroot_ok"], 1)
                    act.wait_ge(E["kv_mm"], 2 * i + 2)
                    act.activation(kv[:, i, 1], v3(po[:, 1, :]), ACT.Copy).then_inc(E["v_ok"], 1)

            @block.vector
            def _(dve):
                dve.wait_ge(E["loaded"], 64)
                for i in range(M):
                    dve.wait_ge(E["ss_ok"], i + 1)
                    dve.tensor_scalar(st[:, i, 1:2], st[:, i, 0:1], 1.0 / D, EPS, ALU.mult, ALU.add).then_inc(E["mean_ok"], 1)
                    dve.wait_ge(E["root_ok"], i + 1)
                    dve.reciprocal(st[:, i, 3:4], st[:, i, 2:3]).then_inc(E["rstd_ok"], 1)
                    dve.wait_ge(E["xT_ok"], i + 1)
                    need(dve, E["kv_mm"], 2 * i)
                    for h in range(2):
                        dve.tensor_tensor(nT[:, 4 * h:4 * h + 4, :], tr[:, h, :].rearrange("p (k n) -> p k n", k=4),
                                          bc(gm[:, 4 * h:4 * h + 4], [P, 4, P]), ALU.mult).then_inc(E["nT_ok"], 1)
                    dve.wait_ge(E["sq_ok"], i + 1)
                    dve.tensor_reduce(kst[:, 0], sq[:], AXX, ALU.add).then_inc(E["sum_ok"], 1)
                    dve.wait_ge(E["sum_ok"], i + 1)
                    dve.tensor_scalar(kst[:, 1], kst[:, 0], 1.0 / XD, EPS, ALU.mult, ALU.add).then_inc(E["n2_ok"], 1)
                    dve.wait_ge(E["kroot_ok"], i + 1)
                    dve.reciprocal(kst[:, 0], kst[:, 2]).then_inc(E["krec_ok"], 1)
                    dve.wait_ge(E["krec_ok"], i + 1)
                    dve.tensor_tensor(sq[:], v3(po[:, 0, :]), bc(kst[:, 0], [P, XH, XD]), ALU.mult).then_inc(E["kn_ok"], 1)
                    dve.wait_ge(E["kn_ok"], i + 1)
                    dve.tensor_tensor(kv[:, i, 0], sq[:], gk[:].unsqueeze(1).to_broadcast([P, XH, XD]), ALU.mult).then_inc(E["k_ok"], 1)

            @block.tensor
            def _(pe):
                pe.wait_ge(E["loaded"], 64)
                for i in range(M):
                    pe.wait_ge(E["xn_ok"], i + 1)
                    need(pe, E["nT_ok"], 2 * i)
                    for k in range(KD):
                        last = pe.transpose(tr[:, k // 4, (k % 4) * P:(k % 4 + 1) * P], xn[:, k * P:(k + 1) * P], ident[:])
                    last.then_inc(E["xT_ok"], 1)
                    pe.wait_ge(E["nT_ok"], 2 * i + 2)
                    pe.wait_ge(E["w_in"], 32)
                    need(pe, E["kn_ok"], i)
                    need(pe, E["v_ok"], i)
                    for n in range(2):
                        for k in range(KD):
                            last = pe.matmul(po[:, n, :], nT[:, k, :], w[:, n, k, :], start=(k == 0), stop=(k == KD - 1))
                        last.then_inc(E["kv_mm"], 1)


def project_out(nc, t):
    VA = AD + 1
    with Stage(nc, "pout") as s:
        ident = s.sb("ident", [P, P])
        w = s.sb("w", [P, 2, KD, D], F32R)
        wq = s.sb("wq", [P, 2, KD, XW], F32R)
        raw = s.sb("raw", [P, 2, 4096])
        gx = s.sb("gx", [P, KD])
        gq = s.sb("gq", [P, XD])
        att = s.sb("att", [P, len(DILS), AH * (AD + 2)])
        wa = s.sb("wa", [P, len(DILS), AH, VA])
        wt = s.sb("wt", [P, 4, AH])
        cat = s.sb("cat", [P, D])
        catT = s.sb("catT", [P, 2, KD * P], F32R)
        x = s.sb("x", [P, D])
        h1 = s.sb("h1", [P, D])
        hn = s.sb("hn", [P, D])
        hT = s.sb("hT", [P, 2, KD * P], F32R)
        st = s.sb("st", [P, 4])
        sq = s.sb("sq", [P, XH, XD])
        qst = s.sb("qst", [P, 3, XH])
        qx = s.sb("qx", [P, XH, XD])
        trc = s.ps("trc", [P, 2 * 512])
        po = s.ps("po", [P, 2, 512])
        trh = s.ps("trh", [P, 2 * 512])
        pq = s.ps("pq", [P, 512])
        names = ("consts_in w_in0 w_in1 w_hi w_ok att_in oa_in ob_in x_in dw_ok wt_ok cat_ok cat_turned catT_hi catT_ok out_mm h1_ok ss_ok mean_ok "
                 "root_ok rstd_ok hn_ok h_turned hT_hi hT_ok q_mm sq_ok n2_ok qroot_ok qx_ok h1_out qx_out own own2 own3").split()
        E = dict(zip(names, s.sem(*names)))
        ND = len(DILS)
        v3 = lambda ap: ap.rearrange("p (h d) -> p h d", h=XH)

        def order(eng, turn):
            for i in (0, 1):
                turn(i)
            with eng.Fori(2, PT - 1) as i:
                turn(i)
            for i in range(PT - 1, NT + 2):
                turn(i)

        with nc.Block() as block:
            @block.sync
            def _(sp):
                def rows(i):
                    sample = isinstance(i, int) and i == PT
                    need(sp, E["cat_ok"], i)
                    if not sample:
                        sp.dma_start(att[:], t["att"][:, i].rearrange("a p c -> p a c")).then_inc(E["att_in"], 16)
                    need(sp, E["cat_turned"], i)
                    sp.dma_start(cat[:, AW:], t["ob"][i]).then_inc(E["ob_in"], 16)
                    if sample:
                        sp.dma_start(cat[:, 0:AW], t["oa"][i]).then_inc(E["oa_in"], 16)

                def residual(i):
                    need(sp, E["h1_ok"], 2 * i)
                    sp.dma_start(x[:], t["x"][i]).then_inc(E["x_in"], 16)

                for dst, name in ((ident, "ident"), (gx, "g_xattn"), (gq, "g_xq")):
                    sp.dma_start(dst[:], t[name]).then_inc(E["consts_in"], 16)
                rows(0)
                wide = t["w_out"].rearrange("(n k p) c -> n p k c", n=2, p=P)
                for n in range(2):
                    sp.dma_start(raw[:, n].rearrange("p (k c) -> p k c", c=D), wide[n]).then_inc(E[f"w_in{n}"], 16)
                sp.wait_ge(E["w_ok"], 1)
                sp.dma_start(raw[:, 0].rearrange("p (k c) -> p k c", c=XW), t["w_xq"].rearrange("(k p) c -> p k c", p=P)).then_inc(E["w_in0"], 16)
                order(sp, lambda i: each((residual, i), (rows, i + 1)))

            @block.gpsimd
            def _(pool):
                def h1_store(i):
                    pool.wait_ge(E["h1_ok"], 2 * i + 2)
                    pool.dma_start(t["h1"][i], h1[:]).then_inc(E["h1_out"], 16)

                def q_store(i):
                    pool.wait_ge(E["qx_ok"], i + 1)
                    pool.dma_start(t["qx"][i], qx[:].rearrange("p h d -> p (h d)")).then_inc(E["qx_out"], 16)

                order(pool, lambda i: each((h1_store, i - 1), (q_store, i - 2)))
                pool.wait_ge(E["h1_out"], NT * 16)
                pool.wait_ge(E["qx_out"], NT * 16)

            @block.scalar
            def _(act):
                def norm(i):
                    act.wait_ge(E["h1_ok"], 2 * i + 2)
                    need(act, E["h_turned"], i)
                    act.activation(hn[:], h1[:], ACT.Square, accum_out=st[:, 0:1]).then_inc(E["ss_ok"], 1)
                    act.wait_ge(E["mean_ok"], i + 1)
                    act.activation(st[:, 2:3], st[:, 1:2], ACT.Sqrt).then_inc(E["root_ok"], 1)
                    act.wait_ge(E["rstd_ok"], i + 1)
                    act.activation(hn[:], h1[:], ACT.Copy, scale=st[:, 3:4]).then_inc(E["hn_ok"], 1)

                def weights(i):
                    if isinstance(i, int) and i == PT:
                        return
                    act.wait_ge(E["dw_ok"], i + 1)
                    act.activation(wt[:, 1:], wt[:, 1:], ACT.Exp).then_inc(E["wt_ok"], 1)

                def queries(i):
                    act.wait_ge(E["q_mm"], i + 1)
                    need(act, E["qx_ok"], i)
                    act.activation(sq[:], v3(pq[:, :]), ACT.Square).then_inc(E["sq_ok"], 1)
                    act.wait_ge(E["n2_ok"], i + 1)
                    act.activation(qst[:, 2], qst[:, 1], ACT.Sqrt).then_inc(E["qroot_ok"], 1)

                weights(0)
                order(act, lambda i: each((norm, i - 1), (weights, i + 1), (queries, i - 2)))

            @block.vector
            def _(dve):
                def combine_dilations(i):
                    if isinstance(i, int) and i == PT:
                        dve.wait_ge(E["oa_in"], 16)
                        dve.sem_inc(E["cat_ok"], 1)
                        return
                    own = Chain(dve, E["own"], 6, i)
                    nm = att[:, :, AH * VA:]
                    dve.wait_ge(E["att_in"], i * 16 + 16)
                    own.then(dve.tensor_tensor(wt[:, 0], nm[:, 0], nm[:, 1], ALU.min))
                    own.then(dve.tensor_tensor(wt[:, 0], wt[:, 0], nm[:, 2], ALU.min))
                    dve.tensor_tensor(wt[:, 1:], wt[:, 0].unsqueeze(1).to_broadcast([P, ND, AH]), nm, ALU.subtract).then_inc(E["dw_ok"], 1)
                    dve.wait_ge(E["wt_ok"], i + 1)
                    for a in range(ND):
                        dd = dve.tensor_tensor(wa[:, a], att[:, a, 0:AH * VA].rearrange("p (h d) -> p h d", h=AH),
                                               bc(wt[:, 1 + a], [P, AH, VA]), ALU.mult)
                    own.then(dd)
                    own.then(dve.tensor_tensor(wa[:, 0], wa[:, 0], wa[:, 1], ALU.add))
                    own.then(dve.tensor_tensor(wa[:, 0], wa[:, 0], wa[:, 2], ALU.add))
                    own.then(dve.reciprocal(wt[:, 0], wa[:, 0, :, AD]))
                    own.done()
                    need(dve, E["cat_turned"], i)
                    dve.tensor_tensor(cat[:, 0:AW].rearrange("p (h d) -> p h d", h=AH), wa[:, 0, :, 0:AD],
                                      bc(wt[:, 0], [P, AH, AD]), ALU.mult).then_inc(E["cat_ok"], 1)

                def residual(i):
                    dve.wait_ge(E["out_mm"], i + 1)
                    dve.wait_ge(E["x_in"], i * 16 + 16)
                    need(dve, E["hn_ok"], i)
                    need(dve, E["h1_out"], i * 16)
                    for h in range(2):
                        dve.tensor_tensor(h1[:, 512 * h:512 * h + 512], po[:, h, :], x[:, 512 * h:512 * h + 512], ALU.add).then_inc(E["h1_ok"], 1)

                def norm(i):
                    dve.wait_ge(E["ss_ok"], i + 1)
                    dve.tensor_scalar(st[:, 1:2], st[:, 0:1], 1.0 / D, EPS, ALU.mult, ALU.add).then_inc(E["mean_ok"], 1)
                    dve.wait_ge(E["root_ok"], i + 1)
                    dve.reciprocal(st[:, 3:4], st[:, 2:3]).then_inc(E["rstd_ok"], 1)

                def rows_turned(i):
                    dve.wait_ge(E["cat_turned"], i + 1)
                    need(dve, E["out_mm"], i)
                    split(dve, catT[:, 0], catT[:, 1], trc[:], E["catT_hi"], i + 1).then_inc(E["catT_ok"], 1)

                def h_turned(i):
                    dve.wait_ge(E["h_turned"], i + 1)
                    need(dve, E["q_mm"], i)
                    split(dve, hT[:, 0], hT[:, 1], trh[:], E["hT_hi"], i + 1).then_inc(E["hT_ok"], 1)

                def queries(i):
                    own = Chain(dve, E["own2"], 3, i)
                    dve.wait_ge(E["sq_ok"], i + 1)
                    own.then(dve.tensor_reduce(qst[:, 0], sq[:], AXX, ALU.add))
                    dve.tensor_scalar(qst[:, 1], qst[:, 0], 1.0, XD * EPS, ALU.mult, ALU.add).then_inc(E["n2_ok"], 1)
                    dve.wait_ge(E["qroot_ok"], i + 1)
                    own.then(dve.reciprocal(qst[:, 0], qst[:, 2]))
                    own.then(dve.tensor_tensor(sq[:], v3(pq[:, :]), bc(qst[:, 0], [P, XH, XD]), ALU.mult))
                    own.done()
                    need(dve, E["qx_out"], i * 16)
                    dve.tensor_tensor(qx[:], sq[:], gq[:].unsqueeze(1).to_broadcast([P, XH, XD]), ALU.mult).then_inc(E["qx_ok"], 1)

                dve.wait_ge(E["consts_in"], 48)
                combine_dilations(0)
                flat = lambda ap: ap.rearrange("p k c -> p (k c)")
                for n in range(2):
                    dve.wait_ge(E[f"w_in{n}"], 16)
                    split(dve, flat(w[:, 0, 4 * n:4 * n + 4]), flat(w[:, 1, 4 * n:4 * n + 4]), raw[:, n], E["w_hi"], n + 1).then_inc(E["w_ok"], 1)
                rq = raw[:, 0].rearrange("p (k c) -> p k c", c=XW)
                dve.wait_ge(E["w_in0"], 32)
                dve.tensor_tensor(rq, rq, bc(gx[:], [P, KD, XW]), ALU.mult).then_inc(E["own3"], 1)
                dve.wait_ge(E["own3"], 1)
                split(dve, wq[:, 0], wq[:, 1], rq, E["w_hi"], 3).then_inc(E["w_ok"], 1)
                order(dve, lambda i: each((residual, i - 1), (rows_turned, i), (norm, i - 1), (combine_dilations, i + 1),
                                          (queries, i - 2), (h_turned, i - 1)))

            @block.tensor
            def _(pe):
                def turn_rows(i):
                    pe.wait_ge(E["ob_in"], i * 16 + 16)
                    pe.wait_ge(E["cat_ok"], i + 1)
                    need(pe, E["catT_ok"], i)
                    for k in range(KD):
                        last = pe.transpose(trc[:, k * P:(k + 1) * P], cat[:, k * P:(k + 1) * P], ident[:])
                    last.then_inc(E["cat_turned"], 1)

                def out(i):
                    pe.wait_ge(E["catT_ok"], i + 1)
                    if isinstance(i, int) and i == 0:
                        pe.wait_ge(E["w_ok"], 2)
                    need(pe, E["h1_ok"], 2 * i)
                    for n in range(2):
                        for k in range(KD):
                            kk, cols = slice(k * P, (k + 1) * P), slice(512 * n, 512 * n + 512)
                            last = matmul3(pe, po[:, n, :], catT[:, 0, kk], catT[:, 1, kk], w[:, 0, k, cols], w[:, 1, k, cols],
                                           k == 0, k == KD - 1)
                    last.then_inc(E["out_mm"], 1)

                def turn_h(i):
                    pe.wait_ge(E["hn_ok"], i + 1)
                    need(pe, E["hT_ok"], i)
                    for k in range(KD):
                        last = pe.transpose(trh[:, k * P:(k + 1) * P], hn[:, k * P:(k + 1) * P], ident[:])
                    last.then_inc(E["h_turned"], 1)

                def queries(i):
                    if isinstance(i, int) and i == 0:
                        pe.wait_ge(E["w_ok"], 3)
                    pe.wait_ge(E["hT_ok"], i + 1)
                    need(pe, E["qx_ok"], i)
                    for k in range(KD):
                        kk = slice(k * P, (k + 1) * P)
                        last = matmul3(pe, pq[:, :], hT[:, 0, kk], hT[:, 1, kk], wq[:, 0, k, :], wq[:, 1, k, :], k == 0, k == KD - 1)
                    last.then_inc(E["q_mm"], 1)

                pe.wait_ge(E["consts_in"], 48)
                order(pe, lambda i: each((turn_rows, i), (queries, i - 2), (turn_h, i - 1), (out, i)))


def attend_memory(nc, t):
    NL = NG + NE
    with Stage(nc, "mx") as s:
        ident = s.sb("ident", [P, P])
        raw = s.sb("raw", [P, XH, D])
        wo = s.sb("wo", [P, 2, XH, D], F32R)
        wr = s.sb("wr", [P, KD, NL])
        br = s.sb("br", [P, NL])
        gf = s.sb("gf", [P, D])
        km = s.sb("km", [P, 2, XW])
        vm = s.sb("vm", [P, 2, XW])
        kT = s.sb("kT", [P, XH, NMEM])
        q = s.sb("q", [P, XW])
        qT = s.sb("qT", [P, XH, P])
        ft = s.sb("ft", [P, 3, XH])
        pr = s.sb("pr", [P, XH, NMEM])
        pT = s.sb("pT", [P, 2, 4, P])
        ox = s.sb("ox", [P, XW])
        oxT = s.sb("oxT", [P, 2, XH * P], F32R)
        h1 = s.sb("h1", [P, D])
        h2 = s.sb("h2", [P, D])
        h0 = s.sb("h0", [P, D])
        hn = s.sb("hn", [P, D])
        hT = s.sb("hT", [P, KD, P])
        st = s.sb("st", [P, 4])
        lg = s.sb("lg", [P, NL])
        A = s.ps("A", [P, 2, 512])
        S = s.ps("S", [P, XH, NMEM])
        V = s.ps("V", [P, 512])
        X = s.ps("X", [P, 2, 512])
        T = s.ps("T", [P, 512])
        names = ("consts_in w_in w_hi w_ok km_mm kT_ok q_in q_turned qT_ok score_ok max_ok exp_ok p_turned pT_ok pv_ok rden_ok ox_ok ox_in "
                 "ox_turned oxT_hi oxT_ok xo_mm h1_in h2_ok ss_ok mean_ok root_ok rstd_ok h0_ok hn_ok h_turned hT_ok lg_mm lg_ok h2_out hn_out lg_out").split()
        E = dict(zip(names, s.sem(*names)))
        v3 = lambda ap: ap.rearrange("p (h d) -> p h d", h=XH)

        def order(eng, turn):
            for i in range(3):
                turn(i)
            with eng.Fori(3, PT) as i:
                turn(i)
            for i in range(PT, NT + 3):
                turn(i)

        def prompt(step):
            return lambda i: None if isinstance(i, int) and i >= PT else step(i)

        with nc.Block() as block:
            @block.sync
            def _(sp):
                for dst, src in ((ident[:], t["ident"]), (km[:], t["mem_kp"].rearrange("n p c -> p n c")),
                                 (vm[:], t["mem_vp"].rearrange("n p c -> p n c")), (br[:], t["b_r"]), (gf[:], t["g_ffn"])):
                    sp.dma_start(dst, src).then_inc(E["consts_in"], 16)

                def q_load(i):
                    need(sp, E["q_turned"], i)
                    sp.dma_start(q[:], t["qx"][i]).then_inc(E["q_in"], 16)

                def h1_load(i):
                    need(sp, E["h2_ok"], 2 * i)
                    sp.dma_start(h1[:], t["h1"][i]).then_inc(E["h1_in"], 16)

                def sample_rows(i):
                    if isinstance(i, int) and i == PT:
                        sp.wait_ge(E["ox_turned"], PT)
                        sp.dma_start(ox[:], t["ox"][PT]).then_inc(E["ox_in"], 16)

                def h2_store(i):
                    sp.wait_ge(E["h2_ok"], 2 * i + 2)
                    sp.dma_start(t["h2"][i], h2[:]).then_inc(E["h2_out"], 16)

                def hn_store(i):
                    sp.wait_ge(E["hn_ok"], i + 1)
                    sp.dma_start(t["hn"][i], hn[:]).then_inc(E["hn_out"], 16)

                def lg_store(i):
                    sp.wait_ge(E["lg_ok"], i + 1)
                    sp.dma_start(t["lg"][i], lg[:]).then_inc(E["lg_out"], 16)

                q_load(0)
                sp.dma_start(raw[:], t["w_xo"].rearrange("(k p) c -> p k c", p=P)).then_inc(E["w_in"], 16)
                sp.dma_start(wr[:], t["w_r"].rearrange("(k p) c -> p k c", p=P)).then_inc(E["w_in"], 16)
                order(sp, lambda i: each((prompt(q_load), i + 1), (h1_load, i - 1), (h2_store, i - 2), (hn_store, i - 2),
                                         (sample_rows, i - 1), (lg_store, i - 3)))
                for e in ("h2_out", "hn_out", "lg_out"):
                    sp.wait_ge(E[e], NT * 16)

            @block.gpsimd
            def _(pool):
                def gain(i):
                    pool.wait_ge(E["h0_ok"], i + 1)
                    need(pool, E["h_turned"], 2 * i)
                    need(pool, E["hn_out"], i * 16)
                    pool.tensor_tensor(hn[:], h0[:], gf[:], ALU.mult).then_inc(E["hn_ok"], 1)

                pool.wait_ge(E["consts_in"], 80)
                order(pool, lambda i: each((gain, i - 2)))

            @block.scalar
            def _(act):
                for n in range(2):
                    act.wait_ge(E["km_mm"], n + 1)
                    act.activation(kT[:, :, n * P:(n + 1) * P], v3(A[:, n, :]), ACT.Copy).then_inc(E["kT_ok"], 1)

                def q_turned(i):
                    act.wait_ge(E["q_turned"], i + 1)
                    need(act, E["score_ok"], i)
                    act.activation(qT[:], v3(A[:, 0, :]), ACT.Copy).then_inc(E["qT_ok"], 1)

                def squares(i):
                    act.wait_ge(E["h2_ok"], 2 * i + 2)
                    need(act, E["hn_ok"], i)
                    act.activation(h0[:], h2[:], ACT.Square, accum_out=st[:, 0:1]).then_inc(E["ss_ok"], 1)

                def exponentials(i):
                    act.wait_ge(E["max_ok"], i + 1)
                    need(act, E["p_turned"], 2 * i)
                    for h in range(XH):
                        e = act.activation(pr[:, h, :], S[:, h, :], ACT.Exp, bias=ft[:, 0, h:h + 1], accum_out=ft[:, 1, h:h + 1])
                        e.then_inc(E["exp_ok"], 1)

                def h_turned(i):
                    need(act, E["lg_mm"], i)
                    for n in range(2):
                        act.wait_ge(E["h_turned"], 2 * i + n + 1)
                        act.activation(hT[:, 4 * n:4 * n + 4, :], v3((T[:, :], X[:, 1, :])[n]), ACT.Copy).then_inc(E["hT_ok"], 1)

                def norm(i):
                    act.wait_ge(E["mean_ok"], i + 1)
                    act.activation(st[:, 2:3], st[:, 1:2], ACT.Sqrt).then_inc(E["root_ok"], 1)
                    act.wait_ge(E["rstd_ok"], i + 1)
                    act.activation(h0[:], h2[:], ACT.Copy, scale=st[:, 3:4]).then_inc(E["h0_ok"], 1)

                order(act, lambda i: each((prompt(q_turned), i), (squares, i - 2), (prompt(exponentials), i), (h_turned, i - 3), (norm, i - 2)))

            @block.vector
            def _(dve):
                def residual(i):
                    dve.wait_ge(E["xo_mm"], i + 1)
                    dve.wait_ge(E["h1_in"], i * 16 + 16)
                    need(dve, E["h0_ok"], i)
                    need(dve, E["h2_out"], i * 16)
                    for n in range(2):
                        dve.tensor_tensor(h2[:, 512 * n:512 * n + 512], X[:, n, :], h1[:, 512 * n:512 * n + 512], ALU.add).then_inc(E["h2_ok"], 1)

                def row_sums(i):
                    dve.wait_ge(E["exp_ok"], i * XH + XH)
                    need(dve, E["ox_ok"], i)
                    dve.reciprocal(ft[:, 2], ft[:, 1]).then_inc(E["rden_ok"], 1)

                def maxima(i):
                    dve.wait_ge(E["score_ok"], i + 1)
                    dve.tensor_reduce(ft[:, 0], S[:], AXX, ALU.max, negate=True).then_inc(E["max_ok"], 1)

                def mean(i):
                    dve.wait_ge(E["ss_ok"], i + 1)
                    dve.tensor_scalar(st[:, 1:2], st[:, 0:1], 1.0 / D, EPS, ALU.mult, ALU.add).then_inc(E["mean_ok"], 1)

                def attention(i):
                    dve.wait_ge(E["rden_ok"], i + 1)
                    dve.wait_ge(E["pv_ok"], i + 1)
                    need(dve, E["ox_turned"], i)
                    dve.tensor_tensor(v3(ox[:]), v3(V[:, :]), bc(ft[:, 2], [P, XH, XD]), ALU.mult).then_inc(E["ox_ok"], 1)

                def p_turned(i):
                    need(dve, E["pv_ok"], i)
                    for n in range(2):
                        dve.wait_ge(E["p_turned"], 2 * i + n + 1)
                        dve.tensor_copy(pT[:, n], v3(A[:, n, :])).then_inc(E["pT_ok"], 1)

                def norm(i):
                    dve.wait_ge(E["root_ok"], i + 1)
                    dve.reciprocal(st[:, 3:4], st[:, 2:3]).then_inc(E["rstd_ok"], 1)

                def rows_turned(i):
                    dve.wait_ge(E["ox_turned"], i + 1)
                    need(dve, E["xo_mm"], i)
                    split(dve, oxT[:, 0], oxT[:, 1], T[:], E["oxT_hi"], i + 1).then_inc(E["oxT_ok"], 1)

                def logits(i):
                    dve.wait_ge(E["lg_mm"], i + 1)
                    need(dve, E["lg_out"], i * 16)
                    dve.tensor_tensor(lg[:], X[:, 0, 0:NL], br[:], ALU.add).then_inc(E["lg_ok"], 1)

                dve.wait_ge(E["consts_in"], 80)
                dve.wait_ge(E["w_in"], 32)
                split(dve, wo[:, 0], wo[:, 1], raw[:], E["w_hi"], 1).then_inc(E["w_ok"], 1)
                order(dve, lambda i: each((residual, i - 2), (prompt(row_sums), i - 1), (prompt(maxima), i), (mean, i - 2), (prompt(attention), i - 1),
                                          (norm, i - 2), (prompt(p_turned), i), (rows_turned, i - 1), (logits, i - 3)))

            @block.tensor
            def _(pe):
                def turn_q(i):
                    pe.wait_ge(E["q_in"], i * 16 + 16)
                    need(pe, E["pT_ok"], 2 * i)
                    for h in range(XH):
                        last = pe.transpose(A[:, 0, h * P:(h + 1) * P], q[:, h * P:(h + 1) * P], ident[:])
                    last.then_inc(E["q_turned"], 1)

                def out(i):
                    if isinstance(i, int) and i == 0:
                        pe.wait_ge(E["w_ok"], 1)
                    pe.wait_ge(E["oxT_ok"], i + 1)
                    need(pe, E["lg_ok"], i - 1)
                    for n in range(2):
                        for h in range(XH):
                            kk, cols = slice(h * P, (h + 1) * P), slice(512 * n, 512 * n + 512)
                            last = matmul3(pe, X[:, n, :], oxT[:, 0, kk], oxT[:, 1, kk], wo[:, 0, h, cols], wo[:, 1, h, cols], h == 0, h == XH - 1)
                    last.then_inc(E["xo_mm"], 1)

                def scores(i):
                    pe.wait_ge(E["qT_ok"], i + 1)
                    need(pe, E["exp_ok"], i * XH)
                    for h in range(XH):
                        last = pe.matmul(S[:, h, :], qT[:, h, :], kT[:, h, :], start=True, stop=True)
                    last.then_inc(E["score_ok"], 1)

                def turn_h(i):
                    pe.wait_ge(E["hn_ok"], i + 1)
                    if isinstance(i, int) and i >= PT - 1:
                        pe.wait_ge(E["h2_ok"], 2 * NT)
                    else:
                        pe.wait_ge(E["h2_ok"], 2 * i + 4)
                    for n in range(2):
                        for k in range(4):
                            last = pe.transpose((T[:, :], X[:, 1, :])[n][:, k * P:(k + 1) * P], hn[:, (4 * n + k) * P:(4 * n + k + 1) * P], ident[:])
                        last.then_inc(E["h_turned"], 1)

                def p_v(i):
                    need(pe, E["ox_ok"], i)
                    for n in range(2):
                        pe.wait_ge(E["pT_ok"], 2 * i + n + 1)
                        for m in range(4):
                            h, k = 2 * n + m // 2, m % 2
                            last = pe.matmul(V[:, h * P:(h + 1) * P], pT[:, n, m, :], vm[:, k, h * P:(h + 1) * P],
                                             start=(h == 0 and k == 0), stop=(k == 1), skip_group_check=True)
                    last.then_inc(E["pv_ok"], 1)

                def turn_p(i):
                    for n in range(2):
                        pe.wait_ge(E["exp_ok"], i * XH + 2 * n + 2)
                        for m in range(4):
                            h, k = 2 * n + m // 2, m % 2
                            last = pe.transpose(A[:, n, m * P:(m + 1) * P], pr[:, h, k * P:(k + 1) * P], ident[:])
                        last.then_inc(E["p_turned"], 1)

                def turn_rows(i):
                    if isinstance(i, int) and i == PT:
                        pe.wait_ge(E["ox_in"], 16)
                    else:
                        pe.wait_ge(E["ox_ok"], i + 1)
                    need(pe, E["oxT_ok"], i)
                    need(pe, E["hT_ok"], 2 * (i - 1))
                    for h in range(XH):
                        last = pe.transpose(T[:, h * P:(h + 1) * P], ox[:, h * P:(h + 1) * P], ident[:])
                    last.then_inc(E["ox_turned"], 1)

                def logits(i):
                    need(pe, E["lg_ok"], i)
                    pe.wait_ge(E["hT_ok"], 2 * i + 2)
                    for k in range(KD):
                        last = pe.matmul(X[:, 0, 0:NL], hT[:, k, :], wr[:, k, :], start=(k == 0), stop=(k == KD - 1))
                    last.then_inc(E["lg_mm"], 1)

                pe.wait_ge(E["consts_in"], 80)
                for n in range(2):
                    for h in range(XH):
                        last = pe.transpose(A[:, n, h * P:(h + 1) * P], km[:, n, h * P:(h + 1) * P], ident[:])
                    last.then_inc(E["km_mm"], 1)
                pe.wait_ge(E["kT_ok"], 2)
                order(pe, lambda i: each((prompt(turn_q), i), (out, i - 2), (prompt(scores), i), (turn_h, i - 3), (prompt(p_v), i - 1), (prompt(turn_p), i),
                                         (turn_rows, i - 1), (logits, i - 3)))


def route(nc, t):
    KB = ROWS // BLK
    with Stage(nc, "rt") as s:
        lg = s.sb("lg", [P, NT, NG + NE])
        io = s.sb("io", [P, NE])
        kb = s.sb("kb", [P, KB])
        ib = s.sb("ib", [P, NBX])
        tri = s.sb("tri", [P, 2, P])
        tok = s.sb("tok", [P, NT], I32)
        valid = s.sb("valid", [P, NT])
        zero = s.sb("zero", [P, NBX], I32)
        g4 = s.sb("g4", [P, 3, NT, NG])
        m = s.sb("m", [P, 8, NT])
        le = s.sb("le", [P, NT, NE])
        ca = s.sb("ca", [P, NT, NE])
        oh = s.sb("oh", [P, 2, NT, NE])
        C = s.sb("C", [P, NT, NE])
        tot = s.sb("tot", [P, NT + 1, NE])
        cmpk = s.sb("cmpk", [P, NE, KB])
        pe_ = s.sb("ends", [P, 2, 16 + NE])
        nb = s.sb("nb", [P, NE])
        starts = s.sb("starts", [P, NE])
        some = s.sb("some", [P, NE])
        cmpb = s.sb("cmpb", [P, NBX, NE])
        be = s.sb("be", [P, NBX])
        runs = s.sb("runs", [P, NBX + 1])
        plan = s.sb("plan", [P, 3, NBX + 1], I32)
        dst = s.sb("dst", [P, 2, NT])
        dsti = s.sb("dsti", [P, 2, NT], I32)
        wts = s.sb("wts", [P, 2, NT])
        pr = s.ps("rank", [P, 2, 512])
        pt = s.ps("total", [P, 2, 512])
        names = "loaded zero_ok zeroed own exp_ok sums_ok placed scattered saved".split()
        E = dict(zip(names, s.sem(*names)))
        CH = 16
        parts = [(0, CH), (CH, NT)]
        with nc.Block() as block:
            @block.sync
            def _(sp):
                sp.dma_start(lg[:], t["lg"].rearrange("n p c -> p n c")).then_inc(E["loaded"], 16)
                for dstt, name in ((io, "r_iota"), (kb, "r_blocks"), (ib, "r_places"), (tri, "r_tri"), (tok, "r_tok"), (valid, "r_valid")):
                    sp.dma_start(dstt[:], t[name]).then_inc(E["loaded"], 16)
                sp.wait_ge(E["zero_ok"], 1)
                sp.dma_start(t["i_rows"].rearrange("(p n) o -> p (n o)", p=P), zero[:]).then_inc(E["zeroed"], 16)
                sp.wait_ge(E["placed"], 1)
                for dd, src in ((t["i_dst"], dsti[:]), (t["wts"], wts[:]), (t["i_plan"], plan[0:1])):
                    sp.dma_start(dd, src).then_inc(E["saved"], 16)
                sp.wait_ge(E["saved"], 48)

            @block.gpsimd
            def _(pool):
                pool.memset(zero[:], 0).then_inc(E["zero_ok"], 1)
                pool.wait_ge(E["zeroed"], 16)
                pool.wait_ge(E["placed"], 1)
                for i in range(NT):
                    n = P if i < PT else NS
                    for a in range(2):
                        pool.indirect_dma_start(t["i_rows"], bass.IndirectOffsetOnAxis(ap=dsti[0:n, a, i:i + 1].bitcast(U32), axis=0),
                                                tok[0:n, i:i + 1], None).then_inc(E["scattered"], 16)
                pool.wait_ge(E["scattered"], 16 * 2 * NT)

            @block.scalar
            def _(act):
                act.wait_ge(E["own"], 4)
                act.activation(g4[:, 1], g4[:, 0], ACT.Exp).then_inc(E["exp_ok"], 1)
                act.wait_ge(E["own"], 22)
                act.activation(m[:, 6], m[:, 5], ACT.Exp).then_inc(E["exp_ok"], 1)

            @block.tensor
            def _(pe):
                pe.wait_ge(E["loaded"], 7 * 16)
                pe.wait_ge(E["own"], 21)
                for k, (lo, hi) in enumerate(parts):
                    rhs = C[:, lo:hi, :].rearrange("p n e -> p (n e)")
                    pe.matmul(pr[:, k, 0:(hi - lo) * NE], tri[:, 0, :], rhs, start=True, stop=True)
                    last = pe.matmul(pt[:, k, 0:(hi - lo) * NE], tri[:, 1, :], rhs, start=True, stop=True)
                last.then_inc(E["sums_ok"], 1)

            @block.vector
            def _(dve):
                own = Chain(dve, E["own"], 0, 0)
                V = dve.tensor_tensor
                TS = dve.tensor_scalar
                bn = lambda ap, n: bc(ap, [P, NT, n])
                row = lambda ap, n: ap.unsqueeze(1).to_broadcast([P, NT, n])
                dve.wait_ge(E["loaded"], 7 * 16)
                own.then(dve.tensor_reduce(m[:, 0], lg[:, :, 0:NG], AXX, ALU.max))
                own.then(V(g4[:, 0], lg[:, :, 0:NG], bn(m[:, 0], NG), ALU.subtract))
                own.then(TS(g4[:, 2], g4[:, 0], 0.0, 1000.0, ALU.is_lt, ALU.mult))
                own.then(V(g4[:, 2], g4[:, 2], row(io[:, 0:NG], NG), ALU.add))
                own.then(dve.tensor_reduce(m[:, 1], g4[:, 2], AXX, ALU.min))
                own.then(V(g4[:, 2], row(io[:, 0:NG], NG), bn(m[:, 1], NG), ALU.not_equal))
                own.then(TS(g4[:, 2], g4[:, 2], NEG, None, ALU.mult))
                own.then(V(le[:].rearrange("p n (g e) -> p n g e", g=NG), lg[:, :, NG:].rearrange("p n (g e) -> p n g e", g=NG),
                           g4[:, 2].unsqueeze(3).to_broadcast([P, NT, NG, GE]), ALU.add))
                for a in range(2):
                    own.then(dve.tensor_reduce(m[:, 2 + a], le[:], AXX, ALU.max))
                    own.then(V(ca[:], le[:], bn(m[:, 2 + a], NE), ALU.is_lt))
                    own.then(dve.scalar_tensor_tensor(out=ca[:], in0=ca[:], scalar=1000.0, in1=row(io[:], NE), op0=ALU.mult, op1=ALU.add))
                    own.then(dve.tensor_reduce(m[:, 4], ca[:], AXX, ALU.min))
                    own.then(V(oh[:, a], row(io[:], NE), bn(m[:, 4], NE), ALU.is_equal))
                    if a == 0:
                        own.then(dve.scalar_tensor_tensor(out=le[:], in0=oh[:, 0], scalar=3 * NEG, in1=le[:], op0=ALU.mult, op1=ALU.add))
                own.then(V(C[:], oh[:, 0], oh[:, 1], ALU.add))
                own.then(V(C[:], C[:], bn(valid[:], NE), ALU.mult))
                own.then(V(m[:, 5], m[:, 3], m[:, 2], ALU.subtract))
                dve.wait_ge(E["exp_ok"], 2)
                own.then(dve.tensor_reduce(m[:, 0], g4[:, 1], AXX, ALU.add))
                own.then(TS(m[:, 7], m[:, 6], 1.0, None, ALU.add))
                own.then(V(m[:, 0], m[:, 0], m[:, 7], ALU.mult))
                own.then(dve.reciprocal(wts[:, 0], m[:, 0]))
                own.then(V(wts[:, 1], wts[:, 0], m[:, 6], ALU.mult))
                dve.wait_ge(E["sums_ok"], 1)
                own.then(dve.memset(tot[:, 0], 0.0))
                for i in range(NT):
                    k, j = divmod(i, CH)
                    own.then(V(tot[:, i + 1], tot[:, i], pt[:, k, j * NE:(j + 1) * NE], ALU.add))
                own.then(V(cmpk[:], bc(tot[:, NT], [P, NE, KB]), kb[:].unsqueeze(1).to_broadcast([P, NE, KB]), ALU.is_gt))
                own.then(dve.tensor_reduce(nb[:], cmpk[:], AXX, ALU.add))
                own.then(dve.memset(pe_[:], 0.0))
                own.then(dve.tensor_copy(pe_[:, 0, 16:], nb[:]))
                for k in range(5):
                    a, b, d = k % 2, 1 - k % 2, 1 << k
                    own.then(V(pe_[:, b, 16:], pe_[:, a, 16:], pe_[:, a, 16 - d:16 + NE - d], ALU.add))
                ends = pe_[:, 1, 16:]
                wide = lambda ap: ap.unsqueeze(1).to_broadcast([P, NBX, NE])
                own.then(V(cmpb[:], wide(ends), bc(ib[:], [P, NBX, NE]), ALU.is_le))
                own.then(dve.tensor_reduce(be[:], cmpb[:], AXX, ALU.add))
                own.then(TS(plan[:, 0, 0:NBX], be[:], float(NE - 1), None, ALU.min))
                own.then(V(starts[:], ends, nb[:], ALU.subtract))
                own.then(TS(some[:], nb[:], 0.0, None, ALU.is_gt))
                own.then(V(cmpb[:], wide(starts[:]), bc(ib[:], [P, NBX, NE]), ALU.is_le))
                own.then(V(cmpb[:], cmpb[:], wide(some[:]), ALU.mult))
                own.then(dve.memset(runs[:], 0.0))
                own.then(dve.tensor_reduce(runs[:, 1:], cmpb[:], AXX, ALU.add))
                own.then(dve.tensor_copy(plan[:, 1, 0:NBX], runs[:, 1:]))
                own.then(V(plan[:, 2, 0:NBX], runs[:, 1:], runs[:, 0:NBX], ALU.subtract))
                own.then(dve.tensor_copy(plan[:, :, NBX:], ends[:, NE - 1:NE].unsqueeze(1).to_broadcast([P, 3, 1])))
                own.then(TS(nb[:], starts[:], float(BLK), None, ALU.mult))
                for k, (lo, hi) in enumerate(parts):
                    own.then(V(C[:, lo:hi], pr[:, k, 0:(hi - lo) * NE].rearrange("p (n e) -> p n e", e=NE), tot[:, lo:hi], ALU.add))
                own.then(V(C[:], C[:], row(nb[:], NE), ALU.add))
                for a in range(2):
                    own.then(V(oh[:, a], oh[:, a], C[:], ALU.mult))
                    own.then(dve.tensor_reduce(dst[:, a], oh[:, a], AXX, ALU.add))
                dve.tensor_copy(dsti[:], dst[:]).then_inc(E["placed"], 1)


def experts(nc, t):
    KF = FF // P
    with Stage(nc, "ex") as s:
        ident = s.sb("ident", [P, P])
        plan = s.sb("plan", [1, 3, NBX + 1], I32)
        idx = s.sb("idx", [P, 2, 1], I32)
        xb = s.sb("xb", [P, 2, D])
        xT = s.sb("xT", [P, 2, 2, KD, P], F32R)
        raw = {"g": s.sb("gate_raw", [P, KD, FF]), "u": s.sb("up_raw", [P, KD, FF]), "d": s.sb("down_raw", [P, KF, D])}
        half = {"g": s.sb("gate", [P, 2, KD, FF], F32R), "u": s.sb("up", [P, 2, KD, FF], F32R), "d": s.sb("down", [P, 2, KF, D], F32R)}
        sg = s.sb("sg", [P, FF])
        hh = s.sb("hh", [P, FF])
        hT = s.sb("hT", [P, 2, KF, P], F32R)
        y = s.sb("y", [P, 2, D])
        zero = s.sb("zero", [P, D])
        tr = s.ps("tr", [P, 2, 512])
        gu = s.ps("gu", [P, 2, 512])
        th = s.ps("th", [P, 512])
        py = s.ps("py", [P, 2, 512])
        names = ("consts_in seen idx_in0 idx_in1 x_in0 x_in1 g_in u_in d_in g_hi u_hi d_hi g_split u_split d_split d_split2 x_turned x_hi x_ok "
                 "gate_mm up_mm sg_ok hh_ok h_turned h_hi h_ok y_mm y_ok y_out0 y_out1 zero_ok zero_out").split()
        E = dict(zip(names, s.sem(*names)))
        flat = lambda ap: ap.rearrange("p k n -> p (k n)")

        def read(eng, row, b, top):
            return eng.value_load(plan[0:1, row, bass.ds(b, 1)], min_val=0, max_val=top)

        def began(eng, b):
            return read(eng, 1, b, NE)

        def blocks(eng, body, beyond=None):
            used = read(eng, 0, NBX, NBLK)
            with eng.Fori(0, NBLK // 2) as i:
                with eng.If(2 * i < used):
                    for u in range(2):
                        body(i, u, 2 * i + u)
                if beyond:
                    with eng.If(2 * i >= used):
                        for u in range(2):
                            beyond(2 * i + u)
            return (used + 1) // 2

        def start(eng):
            eng.wait_ge(E["consts_in"], 32)

        def lower_d(eng, n):
            k = slice(n * KF // 2, (n + 1) * KF // 2)
            return eng.tensor_tensor(half["d"][:, 1, k], raw["d"][:, k], half["d"][:, 0, k].bitcast(F32), ALU.subtract)

        with nc.Block() as block:
            @block.sync
            def _(sp):
                sp.dma_start(ident[:], t["ident"]).then_inc(E["consts_in"], 16)
                sp.dma_start(plan[:], t["i_plan"]).then_inc(E["consts_in"], 16)
                start(sp)

                def load(i, u, b):
                    sp.sem_inc(E["zero_out"], 16)
                    with sp.If(read(sp, 2, b, 1)):
                        e = read(sp, 0, b, NE - 1)
                        r = began(sp, b)
                        for piece, name in (("g", "w_gate"), ("u", "w_up")):
                            sp.wait_ge(E[piece + "_split"], r)
                            sp.dma_start(raw[piece][:], t[name][e].rearrange("(k p) c -> p k c", p=P)).then_inc(E[piece + "_in"], 16)

                def nothing(b):
                    sp.dma_start(t["yb"][b], zero[:]).then_inc(E["zero_out"], 16)

                sp.wait_ge(E["zero_ok"], 1)
                blocks(sp, load, nothing)
                sp.wait_ge(E["zero_out"], 16 * NBLK)

            @block.gpsimd
            def _(pool):
                pool.memset(zero[:], 0.0).then_inc(E["zero_ok"], 1)
                rows = t["i_rows"].rearrange("(n p) o -> n p o", p=P)
                start(pool)

                def load_rows(u, b):
                    pool.dma_start(idx[:, u, :], rows[b]).then_inc(E[f"idx_in{u}"], 16)

                def gather(u, b, nth):
                    pool.wait_ge(E[f"idx_in{u}"], 16 * nth)
                    if not isinstance(nth, int):
                        pool.sem_inc(E["seen"], 1)
                    pool.indirect_dma_start(xb[:, u, :], None, t["hn"].rearrange("n p d -> (n p) d"),
                                            bass.IndirectOffsetOnAxis(ap=idx[:, u, :].bitcast(U32), axis=0)).then_inc(E[f"x_in{u}"], 16)

                def load_down(e):
                    pool.dma_start(raw["d"][:], t["w_down"][e].rearrange("(k p) c -> p k c", p=P)).then_inc(E["d_in"], 16)

                for u in range(2):
                    load_rows(u, u)
                for u in range(2):
                    gather(u, u, 1)
                for u in range(2):
                    pool.wait_ge(E[f"x_in{u}"], 16)
                    load_rows(u, 2 + u)

                load_down(read(pool, 0, 0, NE - 1))

                def work(i, u, b):
                    pool.wait_ge(E["x_turned"], b + 1)
                    gather(u, b + 2, i + 2)
                    with pool.If(read(pool, 2, b, 1)):
                        r = began(pool, b)
                        pool.wait_ge(E["d_hi"], r)
                        lower_d(pool, 0).then_inc(E["d_split"], 1)
                    with pool.If(read(pool, 2, b + 1, 1)):
                        e = read(pool, 0, b + 1, NE - 1)
                        r = began(pool, b + 1)
                        pool.wait_ge(E["d_split"], r)
                        pool.sem_inc(E["seen"], 1)
                        pool.wait_ge(E["d_split2"], r)
                        pool.sem_inc(E["seen"], 1)
                        load_down(e)
                    pool.wait_ge(E[f"x_in{u}"], 16 * i + 32)
                    pool.sem_inc(E["seen"], 1)
                    load_rows(u, b + 4)

                pairs = blocks(pool, work)
                for u in range(2):
                    pool.wait_ge(E[f"idx_in{u}"], 16 * pairs + 32)

            @block.scalar
            def _(act):
                start(act)

                def upper(p, r):
                    act.wait_ge(E[p + "_in"], 16 * r)
                    act.activation(half[p][:, 0], raw[p][:], ACT.Copy).then_inc(E[p + "_hi"], 1)

                upper("u", 1)

                def work(i, u, b):
                    act.wait_ge(E["gate_mm"], b + 1)
                    act.wait_ge(E["hh_ok"], b + 1)
                    act.activation(sg[:], gu[:, 0, :], ACT.Silu).then_inc(E["sg_ok"], 1)
                    with act.If(read(act, 2, b, 1)):
                        r = began(act, b)
                        act.wait_ge(E["y_mm"], b + 1)
                        act.sem_inc(E["seen"], 1)
                        upper("d", r)
                    with act.If(read(act, 2, b + 1, 1)):
                        r = began(act, b + 1)
                        act.wait_ge(E["up_mm"], b + 1)
                        act.sem_inc(E["seen"], 1)
                        upper("u", r)
                    act.wait_ge(E["y_mm"], b + 2)
                    act.wait_ge(E[f"y_out{u}"], i * 16 + 16)
                    for n in range(2):
                        act.activation(y[:, u, 512 * n:512 * n + 512], py[:, n, :], ACT.Copy).then_inc(E["y_ok"], 1)
                    act.wait_ge(E["y_ok"], 2 * b + 4)
                    act.dma_start(t["yb"][b], y[:, u, :]).then_inc(E[f"y_out{u}"], 16)

                pairs = blocks(act, work)
                for u in range(2):
                    act.wait_ge(E[f"y_out{u}"], 16 * pairs + 16)
                    act.sem_inc(E["seen"], 1)

            @block.vector
            def _(dve):
                for n in ("g_split", "u_split", "d_split", "d_split2", "hh_ok", "h_turned", "y_mm"):
                    dve.sem_inc(E[n], 1)
                dve.sem_inc(E["y_ok"], 2)
                dve.sem_inc(E["y_out0"], 16)
                dve.sem_inc(E["y_out1"], 16)
                start(dve)

                def halves(p, r):
                    dve.wait_ge(E[p + "_in"], 16 * r)
                    split(dve, half[p][:, 0], half[p][:, 1], raw[p][:], E[p + "_hi"], r).then_inc(E[p + "_split"], 1)

                def lower(p, r):
                    dve.wait_ge(E[p + "_hi"], r)
                    dve.tensor_tensor(half[p][:, 1], raw[p][:], half[p][:, 0].bitcast(F32), ALU.subtract).then_inc(E[p + "_split"], 1)

                def rows(u, b):
                    dve.wait_ge(E["x_turned"], b + 1)
                    split(dve, flat(xT[:, u, 0]), flat(xT[:, u, 1]), tr[:].rearrange("p k n -> p (k n)"), E["x_hi"], b + 1).then_inc(E["x_ok"], 1)

                halves("g", 1)
                rows(0, 0)
                rows(1, 1)
                lower("u", 1)

                def work(i, u, b):
                    with dve.If(read(dve, 2, b + 1, 1)):
                        dve.wait_ge(E["gate_mm"], b + 1)
                        halves("g", began(dve, b + 1))
                    dve.wait_ge(E["sg_ok"], b + 1)
                    dve.wait_ge(E["up_mm"], b + 1)
                    dve.wait_ge(E["h_turned"], b + 1)
                    dve.tensor_tensor(hh[:], sg[:], gu[:, 1, :], ALU.mult).then_inc(E["hh_ok"], 1)
                    with dve.If(read(dve, 2, b, 1)):
                        dve.wait_ge(E["d_hi"], began(dve, b))
                        lower_d(dve, 1).then_inc(E["d_split2"], 1)
                    rows(u, b + 2)
                    dve.wait_ge(E["h_turned"], b + 2)
                    dve.wait_ge(E["y_mm"], b + 1)
                    split(dve, flat(hT[:, 0]), flat(hT[:, 1]), th[:], E["h_hi"], b + 1).then_inc(E["h_ok"], 1)
                    with dve.If(read(dve, 2, b + 1, 1)):
                        lower("u", began(dve, b + 1))

                blocks(dve, work)

            @block.tensor
            def _(pe):
                start(pe)

                def turn(u, b, nth):
                    pe.wait_ge(E[f"x_in{u}"], 16 * nth)
                    need(pe, E["x_ok"], b)
                    for k in range(KD):
                        last = pe.transpose(tr[:, k // 4, (k % 4) * P:(k % 4 + 1) * P], xb[:, u, k * P:(k + 1) * P], ident[:])
                    last.then_inc(E["x_turned"], 1)

                def project(p, u, n, b, sem):
                    pe.wait_ge(E[p + "_split"], began(pe, b) + 1)
                    for k in range(KD):
                        last = matmul3(pe, gu[:, n, :], xT[:, u, 0, k, :], xT[:, u, 1, k, :], half[p][:, 0, k, :], half[p][:, 1, k, :],
                                       k == 0, k == KD - 1)
                    last.then_inc(sem, 1)

                turn(0, 0, 1)
                turn(1, 1, 1)
                project("g", 0, 0, 0, E["gate_mm"])

                def work(i, u, b):
                    project("u", u, 1, b, E["up_mm"])
                    turn(u, b + 2, i + 2)
                    pe.wait_ge(E["hh_ok"], b + 2)
                    for k in range(KF):
                        last = pe.transpose(th[:, k * P:(k + 1) * P], hh[:, k * P:(k + 1) * P], ident[:])
                    last.then_inc(E["h_turned"], 1)
                    project("g", 1 - u, 0, b + 1, E["gate_mm"])
                    r = began(pe, b)
                    pe.wait_ge(E["h_ok"], b + 1)
                    pe.wait_ge(E["d_split"], r + 1)
                    pe.wait_ge(E["d_split2"], r + 1)
                    pe.wait_ge(E["y_ok"], 2 * b + 2)
                    for n in range(2):
                        for k in range(KF):
                            cols = slice(512 * n, 512 * n + 512)
                            last = matmul3(pe, py[:, n, :], hT[:, 0, k, :], hT[:, 1, k, :], half["d"][:, 0, k, cols], half["d"][:, 1, k, cols],
                                           k == 0, k == KF - 1)
                    last.then_inc(E["y_mm"], 1)

                blocks(pe, work)


def combine(nc, t):
    with Stage(nc, "cb") as s:
        di = s.sb("di", [P, 2, NT], I32)
        w = s.sb("w", [P, 2, NT])
        h = s.sb("h", [P, 2, D])
        a1 = s.sb("a1", [P, 2, D])
        a2 = s.sb("a2", [P, 2, D])
        s1 = s.sb("s1", [P, 2, D])
        s2 = s.sb("s2", [P, 2, D])
        consts_in, first_ok, both_ok = s.sem("consts_in", "first_ok", "both_ok")
        h_in, a_in, b_in, out_ok = (s.sem(n + "0", n + "1") for n in ("h_in", "a_in", "b_in", "out_ok"))
        rows_of = lambda i: P if i < PT else NS
        yb = t["yb"].rearrange("n p d -> (n p) d")
        with nc.Block() as block:
            def store(sp, i):
                n = rows_of(i)
                sp.wait_ge(both_ok, i + 1)
                sp.dma_start(t["y"][i, 0:n], s2[0:n, i % 2, :]).then_inc(out_ok[i % 2], 16)

            @block.sync
            def _(sp):
                sp.dma_start(di[:], t["i_dst"]).then_inc(consts_in, 16)
                sp.dma_start(w[:], t["wts"]).then_inc(consts_in, 16)
                for i in range(NT):
                    n, u = rows_of(i), i % 2
                    need(sp, first_ok, i - 1)
                    sp.dma_start(h[0:n, u, :], t["h2"][i, 0:n]).then_inc(h_in[u], 16)
                    if i:
                        store(sp, i - 1)
                store(sp, NT - 1)
                for u in range(2):
                    sp.wait_ge(out_ok[u], 16 * ((NT + 1 - u) // 2))

            @block.gpsimd
            def _(pool):
                pool.wait_ge(consts_in, 32)
                for i in range(NT):
                    n, u = rows_of(i), i % 2
                    need(pool, both_ok, i - 1)
                    for a, dst, sem in ((0, a1, a_in), (1, a2, b_in)):
                        pool.indirect_dma_start(dst[0:n, u, :], None, yb,
                                                bass.IndirectOffsetOnAxis(ap=di[0:n, a, i:i + 1].bitcast(U32), axis=0)).then_inc(sem[u], 16)

            @block.vector
            def _(dve):
                dve.wait_ge(consts_in, 32)
                for i in range(NT):
                    n, u = rows_of(i), i % 2
                    dve.wait_ge(h_in[u], 16 * (i // 2) + 16)
                    dve.wait_ge(a_in[u], 16 * (i // 2) + 16)
                    dve.scalar_tensor_tensor(out=s1[0:n, u, :], in0=a1[0:n, u, :], scalar=w[0:n, 0, i:i + 1], in1=h[0:n, u, :],
                                             op0=ALU.mult, op1=ALU.add).then_inc(first_ok, 1)
                    dve.wait_ge(first_ok, i + 1)
                    dve.wait_ge(b_in[u], 16 * (i // 2) + 16)
                    need(dve, out_ok[u], 16 * (i // 2))
                    dve.scalar_tensor_tensor(out=s2[0:n, u, :], in0=a2[0:n, u, :], scalar=w[0:n, 1, i:i + 1], in1=s1[0:n, u, :],
                                             op0=ALU.mult, op1=ALU.add).then_inc(both_ok, 1)


def build(nc, t, stages=None):
    for f in (stages or STAGES):
        f(nc, t)


def delta_net_sample(nc, t):
    delta_net(nc, t, sample=True)


STAGES = [project_in, project_in_rest, attend_prompt, delta_net, delta_net_sample, attend_window_sample, memory_kv, project_out, attend_memory_sample, attend_memory, route, experts, combine]


def delta_consts(name, chunk, rows, levels):
    i, j = np.arange(P)[:, None], np.arange(P)[None, :]
    same = i // chunk == j // chunk
    sums = [same & (i <= j), same] + [(i // chunk == c) & (j >= 0) for c in range(2 if chunk == P // 2 else 0)]
    lvl = [((i >> q + 1) == (j >> q + 1)) & ((i >> q & 1) == 1) & ((j >> q & 1) == 0) for q in range(levels)]
    low = np.where(same & (j <= i), 0, NEG)
    return {
        name + "_sums": np.ascontiguousarray(np.stack(sums, 1).astype(np.float32)),
        name + "_lvl": np.ascontiguousarray(np.stack(lvl, 1).astype(np.float32)),
        name + "_mask": np.ascontiguousarray(np.stack([np.tile(low, (1, BH)), np.tile(low.T, (1, BH))], 1).astype(bf16)),
    }


def window_counts():
    far = [r for r in range(W_BUF // 2) if r % 16 < DEC_T]
    pos = np.array(far + list(range(W_BUF // 2, W_BUF + DEC_T)))
    back = W_BUF + np.arange(DEC_T)[:, None] - pos[None]
    return sum(((back >= 0) & (back % d == 0) & (back <= BLK * d)).astype(int) for d in DILS)


def sample_consts(name, heads, counts):
    f32 = np.float32
    feat = np.arange(AW)
    row = np.arange(heads * DEC_T)
    own = feat[None] // (AW // heads) == row[:, None] // DEC_T
    logs = np.where(counts > 0, np.log(np.maximum(counts, 1)), NEG)
    return {
        name + "hm": np.ascontiguousarray((feat[:, None] // (AW // heads) == np.arange(heads)[None]).astype(f32)
                                          .reshape(AW // P, P, heads).transpose(1, 0, 2)),
        name + "own": own.astype(f32),
        name + "sel": (row[:, None] % DEC_T == np.arange(DEC_T)[None]).astype(f32),
        name + "mult": np.tile(logs, (heads, 1)).astype(f32),
    }


def layout(a):
    f = lambda n: np.ascontiguousarray(np.asarray(a[n]))
    cols = lambda n: np.ascontiguousarray(f(n).reshape(KD, P).T)
    rep = lambda v: np.ascontiguousarray(np.broadcast_to(v, (P,) + v.shape))
    i, j = np.arange(P)[:, None], np.arange(P)[None, :]
    x = np.zeros((ROWS, D), np.float32)
    x[:SEQ] = f("x_prompt").reshape(SEQ, D)
    x[SEQ:SEQ + NS] = f("x_sample").reshape(NS, D)
    return {
        "x": x.reshape(NT, P, D),
        "ident": np.eye(P, dtype=np.float32),
        "identb": np.eye(P).astype(bf16),
        "att_mask": np.tile(np.concatenate([np.where(j >= i, 0, NEG), np.where(j <= i, 0, NEG)], 1), (1, 2)).astype(bf16),
        **delta_consts("gp", P // 2, P, 6), **delta_consts("gs", DEC_T, NS, 3),
        "ones": rep(np.ones((2, P), np.float32) * np.array([[-1.0], [1.0]], np.float32)),
        "gate_par": rep(np.stack([f("a_log").reshape(BH), f("dt_bias").reshape(BH)])),
        "conv_w": f("conv_w").reshape(CONV, CCH),
        **sample_consts("sw_", AH, window_counts()), **sample_consts("sm_", XH, np.ones((DEC_T, NMEM))),
        "mem_k": f("cache_mem_k").reshape(DEC_B, NMEM, XW),
        "mem_v": f("cache_mem_v").reshape(DEC_B, NMEM, XW),
        "mem": f("mem_prompt").reshape(NMEM // P, P, D),
        "g_mem": cols("g_mem"), "g_xattn": cols("g_xattn"),
        "g_xk": rep(f("g_xk").reshape(XD)), "g_xq": rep(f("g_xq").reshape(XD)),
        "w_xk": f("w_xk").reshape(D, XW), "w_xv": f("w_xv").reshape(D, XW),
        "w_xq": f("w_xq").reshape(D, XW), "w_out": f("w_out").reshape(D, D),
        "w_xo": f("w_xo").reshape(XW, D), "g_ffn": rep(f("g_ffn").reshape(D)),
        "w_r": np.ascontiguousarray(np.concatenate([f("w_rg")[0], f("w_re")[0]], 1)),
        "b_r": rep(np.concatenate([f("b_rg")[0], f("b_re")[0]])),
        "w_gate": f("w_gate")[0], "w_up": f("w_up")[0], "w_down": f("w_down")[0],
        "r_iota": rep(np.arange(NE, dtype=np.float32)),
        "r_blocks": rep(np.arange(ROWS // BLK, dtype=np.float32) * BLK),
        "r_places": rep(np.arange(NBX, dtype=np.float32)),
        "r_tri": np.ascontiguousarray(np.stack([i < j, i < P + j], 1).astype(np.float32)),
        "r_tok": (i + P * np.arange(NT)[None]).astype(np.int32),
        "r_valid": (i + P * np.arange(NT)[None] < SEQ + NS).astype(np.float32),
        "conv0": f("state_conv").reshape(DEC_B, CONV - 1, CCH),
        "delta0": f("state_delta").reshape(DEC_B, BH, BD, BD),
        "cache_k": f("cache_win_k").reshape(DEC_B, W_BUF, AW),
        "cache_v": f("cache_win_v").reshape(DEC_B, W_BUF, AW),
        "gs_cols": rep((np.arange(NS)[None] // DEC_T == np.arange(DEC_B)[:, None]).astype(np.float32)),
        "gs_rows": np.ascontiguousarray(np.stack([i // DEC_T == np.arange(DEC_B)[None], i == DEC_T * np.arange(DEC_B)[None] + DEC_T - 1], 1).astype(np.float32)),
        "g_gdn": rep(f("g_gdn").reshape(BD)),
        "g_mix": cols("g_mix"),
        "g_qa": rep(f("g_qa").reshape(AD)),
        "g_ka": rep(f("g_ka").reshape(AD)),
        "w_in": f("w_in").reshape(D, IN_COLS),
    }


SCRATCH = {
    "i_rows": (NBX * BLK, 1), "i_dst": (P, 2, NT), "wts": (P, 2, NT), "i_plan": (1, 3, NBX + 1), "yb": (NBLK, P, D),
    "lg": (NT, P, NG + NE),
    "oa": (NT, P, AW), "ox": (NT, P, XW), "qx": (NT, P, XW), "h1": (NT, P, D), "h2": (NT, P, D), "hn": (NT, P, D),
    "att": (len(DILS), NT, P, AH * (AD + 2)),
    "q": (NT, P, AW), "u": (CONV - 1 + ROWS, CCH), "ob": (NT, P, BW), "us": (DEC_B, CONV - 1 + DEC_T, CCH), "z": (NT, P, BW), "ab": (NT, P, 2 * BH),
}
OUTPUTS = {
    "k": (NT, P, AW), "v": (NT, P, AW), "delta_p": (BH, BD, BD), "delta_s": (DEC_B, BH, BD, BD),
    "y": (NT, P, D), "mem_kp": (NMEM // P, P, XW), "mem_vp": (NMEM // P, P, XW),
    "win_k": (DEC_B, W_BUF, AW), "win_v": (DEC_B, W_BUF, AW), "conv_p": (CONV - 1, CCH), "conv_s": (DEC_B, CONV - 1, CCH),
}


def declare(nc, arrays, debug=False):
    t = {}
    for n, v in arrays.items():
        t[n] = nc.dram_tensor(f"in_{n}", v.shape, mybir.dt.from_np(v.dtype), kind="ExternalInput").ap()
    for n, sh in OUTPUTS.items():
        t[n] = nc.dram_tensor(f"out_{n}", sh, F32, kind="ExternalOutput").ap()
    for n, sh in SCRATCH.items():
        dt = I32 if n.startswith("i_") else F32
        if debug:
            t[n] = nc.dram_tensor(f"out_{n}", sh, dt, kind="ExternalOutput").ap()
        else:
            t[n] = nc.dram_tensor(f"tmp_{n}", sh, dt, kind="Internal").ap()
    return t


def kernel(**inputs):
    import concourse.bacc as bacc
    from concourse.bass_utils import run_bass_kernel_spmd

    arrays = layout(inputs)
    nc = bacc.Bacc("TRN2", target_bir_lowering=False, num_devices=1)
    t = declare(nc, arrays)
    build(nc, t)
    r = run_bass_kernel_spmd(nc, [{f"in_{n}": a for n, a in arrays.items()}], core_ids=[0]).results[0]
    out = {n: r[f"out_{n}"] for n in OUTPUTS}
    flat = {n: out[n].reshape((ROWS, -1)) for n in ("k", "v", "y")}
    return (flat["y"][:SEQ].reshape(1, SEQ, D), flat["y"][SEQ:SEQ + NS].reshape(DEC_B, DEC_T, D),
            flat["k"][:SEQ].reshape(1, 1, SEQ, AH, AD), flat["v"][:SEQ].reshape(1, 1, SEQ, AH, AD),
            out["conv_p"].reshape(1, 1, CONV - 1, CCH), out["delta_p"].reshape(1, 1, BH, BD, BD),
            out["mem_kp"].reshape(1, 1, NMEM, XH, XD), out["mem_vp"].reshape(1, 1, NMEM, XH, XD),
            out["win_k"].reshape(1, DEC_B, W_BUF, AH, AD), out["win_v"].reshape(1, DEC_B, W_BUF, AH, AD),
            out["conv_s"].reshape(1, DEC_B, CONV - 1, CCH), out["delta_s"].reshape(1, DEC_B, BH, BD, BD))
```
